# Optimizing a Trainium2 kernel written in Bass

```python
import math
import jax
import jax.numpy as jnp
from jax import lax
import numpy as np

D_MODEL = 1024
BATCH = 1
SEQ = 256
DEPTH = 2
DEC_BATCH = 8
DEC_SEQ = 1
PAST_LEN = 2048
PAGE_SIZE = 128

N_AB = (DEPTH + 1) // 2
N_C = DEPTH // 2
MIX_WIDTH = D_MODEL
RWKV_WIDTH = MIX_WIDTH // 2
RWKV_HEAD_DIM = 64
RWKV_HEADS = RWKV_WIDTH // RWKV_HEAD_DIM
DECAY_LORA = 64
AAA_LORA = 64
GATE_LORA = 128
RWKV_SPLITS = (RWKV_WIDTH, 2 * RWKV_WIDTH, 3 * RWKV_WIDTH, 3 * RWKV_WIDTH + DECAY_LORA, 3 * RWKV_WIDTH + DECAY_LORA + AAA_LORA)
RWKV_PROJ = 3 * RWKV_WIDTH + DECAY_LORA + AAA_LORA + GATE_LORA
HGRN_WIDTH = MIX_WIDTH - RWKV_WIDTH
HGRN_EXPAND = 128
HGRN_HEADS = HGRN_WIDTH // HGRN_EXPAND
HGRN_PROJ = 4 * HGRN_WIDTH
AB_PROJ = RWKV_PROJ + HGRN_PROJ
SSM_INNER = 2 * D_MODEL
SSM_HEAD_DIM = 64
SSM_HEADS = SSM_INNER // SSM_HEAD_DIM
SSM_STATE = 128
SSM_GROUPS = 4
SSM_HPG = SSM_HEADS // SSM_GROUPS
CONV_WIDTH = 4
CONV_DIM = SSM_INNER + 2 * SSM_GROUPS * SSM_STATE
SSM_PROJ = SSM_INNER + CONV_DIM + SSM_HEADS
CHUNK = 64
PEER_HEADS = 8
PEER_KEYS = 128
PEER_EXPERTS = PEER_KEYS * PEER_KEYS
PEER_KEY_DIM = 256
PEER_HALF = PEER_KEY_DIM // 2
PEER_TOPK = 16
PEER_BLOCK = 128
RMS_EPS = 1e-6
GN_EPS = 64e-5
L2_EPS = 1e-12
F32 = jnp.float32

kernel_name = 'rwkv7_hgrn2_mamba2_peer_step'

def rms_norm(x, w, eps=RMS_EPS):
    xf = x.astype(F32)
    y = xf * lax.rsqrt(jnp.mean(xf * xf, axis=-1, keepdims=True) + eps)
    return (y * w.astype(F32)).astype(x.dtype)

def to_chunks(a, c):
    b, l = a.shape[:2]
    return jnp.swapaxes(a.reshape((b, l // c, c) + a.shape[2:]), 0, 1)

def from_chunks(a):
    n, b, c = a.shape[:3]
    return jnp.swapaxes(a, 0, 1).reshape((b, n * c) + a.shape[3:])

def causal_mask(c):
    return jnp.tril(jnp.ones((c, c), dtype=bool))

def masked_decay(diff, mask):
    return jnp.where(mask, jnp.exp(jnp.where(mask, diff, 0.0)), 0.0)

def rwkv7_mixer(p, shift_prev, s0, mu, w0, w_up, a0, a_up, g_up, k_k, k_a, r_k, gn_w, gn_b):
    b, l, _ = p.shape
    p = p.astype(F32)
    prev = jnp.concatenate([shift_prev.astype(F32)[:, None], p[:, :-1]], axis=1)
    m = p + mu * (prev - p)
    r, k, v, wd, ad, gd = jnp.split(m, RWKV_SPLITS, axis=-1)
    w_raw = w0 + jnp.tanh(wd) @ w_up
    decay = jnp.exp(-jnp.exp(-jax.nn.softplus(-w_raw) - 0.5))
    a = jax.nn.sigmoid(a0 + ad @ a_up)
    g = jax.nn.sigmoid(gd) @ g_up
    heads = lambda t: t.reshape(b, l, RWKV_HEADS, RWKV_HEAD_DIM)
    kk = heads(k * k_k)
    kk = kk / jnp.maximum(jnp.sqrt(jnp.sum(kk * kk, axis=-1, keepdims=True)), L2_EPS)
    k = heads(k * (1.0 + (a - 1.0) * k_a))
    r, v, a, decay = heads(r), heads(v), heads(a), heads(decay)

    def step(s, inp):
        r_t, w_t, k_t, v_t, kk_t, a_t = inp
        sa = jnp.einsum('bhvk,bhk->bhv', s, -kk_t)
        s = (s * w_t[:, :, None, :] + sa[..., None] * (kk_t * a_t)[:, :, None, :]
             + v_t[..., None] * k_t[:, :, None, :])
        return s, jnp.einsum('bhvk,bhk->bhv', s, r_t)

    xs = tuple(jnp.swapaxes(t, 0, 1) for t in (r, decay, k, v, kk, a))
    s_fin, o = lax.scan(step, s0.astype(F32), xs)
    o = jnp.swapaxes(o, 0, 1)
    mean = jnp.mean(o, axis=-1, keepdims=True)
    var = jnp.mean(jnp.square(o - mean), axis=-1, keepdims=True)
    o = ((o - mean) * lax.rsqrt(var + GN_EPS)).reshape(b, l, RWKV_WIDTH) * gn_w + gn_b
    bonus = jnp.sum(r * k * r_k, axis=-1, keepdims=True) * v
    out = (o + bonus.reshape(b, l, RWKV_WIDTH)) * g
    return out, p[:, -1], s_fin

def chunked_gla(q, k, v, g, s0):
    c = math.gcd(q.shape[1], CHUNK)
    mask = causal_mask(c)[None, :, :, None, None]

    def step(s, inp):
        qc, kc, vc, gc = inp
        gcum = jnp.cumsum(gc, axis=1)
        rel = masked_decay(gcum[:, :, None] - gcum[:, None, :], mask)
        att = jnp.einsum('bthk,btshk->btsh', qc, rel * kc[:, None])
        o = (jnp.einsum('btsh,bshv->bthv', att, vc)
             + jnp.einsum('bthk,bhkv->bthv', qc * jnp.exp(gcum), s))
        g_end = gcum[:, -1]
        s = s * jnp.exp(g_end)[..., None] + jnp.einsum(
            'bshk,bshv->bhkv', kc * jnp.exp(g_end[:, None] - gcum), vc)
        return s, o

    s_fin, o = lax.scan(step, s0, tuple(to_chunks(t, c) for t in (q, k, v, g)))
    return from_chunks(o), s_fin

def hgrn2_mixer(p, s0, lb, norm_w):
    b, l, _ = p.shape
    p = p.astype(F32)
    q, f, i, og = jnp.split(p, 4, axis=-1)
    fg = lb + (1.0 - lb) * jax.nn.sigmoid(f)
    log_f = jnp.log(fg)
    k = 1.0 - fg
    heads = lambda t: t.reshape(b, l, HGRN_HEADS, HGRN_EXPAND)
    o, s_fin = chunked_gla(heads(jax.nn.silu(q)), heads(k), heads(i), heads(log_f), s0.astype(F32))
    o = o * lax.rsqrt(jnp.mean(o * o, axis=-1, keepdims=True) + RMS_EPS) * norm_w
    out = o.reshape(b, l, HGRN_WIDTH) * jax.nn.silu(og)
    return out, s_fin

def chunked_ssd(x, bm, cm, log_a, s0):
    c = math.gcd(x.shape[1], CHUNK)
    mask = causal_mask(c)[None, :, :, None, None]

    def step(s, inp):
        xc, bc, cc, ac = inp
        acum = jnp.cumsum(ac, axis=1)
        lmat = masked_decay(acum[:, :, None] - acum[:, None, :], mask)
        cb = jnp.einsum('btgn,bsgn->btsg', cc, bc)
        y = jnp.einsum('btsgr,bsgrp->btgrp', cb[..., None] * lmat, xc)
        y = y + jnp.einsum('btgn,bgrpn->btgrp', cc, s) * jnp.exp(acum)[..., None]
        a_end = acum[:, -1]
        s = s * jnp.exp(a_end)[..., None, None] + jnp.einsum(
            'bsgn,bsgrp->bgrpn', bc, xc * jnp.exp(a_end[:, None] - acum)[..., None])
        return s, y

    s_fin, y = lax.scan(step, s0, tuple(to_chunks(t, c) for t in (x, bm, cm, log_a)))
    return from_chunks(y), s_fin

def mamba2_mixer(p, conv_buf, s0, conv_w, conv_b, dt_bias, a_log, d_skip, norm_w):
    b, l, _ = p.shape
    p = p.astype(F32)
    z, xbc, dt = jnp.split(p, [SSM_INNER, SSM_INNER + CONV_DIM], axis=-1)
    xpad = jnp.concatenate([conv_buf.astype(F32), xbc], axis=1)
    conv = conv_b + xpad[:, 0:l] * conv_w[0]
    for j in range(1, CONV_WIDTH):
        conv = conv + xpad[:, j:j + l] * conv_w[j]
    xbc = jax.nn.silu(conv)
    new_buf = xpad[:, -(CONV_WIDTH - 1):]
    xs, bm, cm = jnp.split(xbc, [SSM_INNER, SSM_INNER + SSM_GROUPS * SSM_STATE], axis=-1)
    xs = xs.reshape(b, l, SSM_GROUPS, SSM_HPG, SSM_HEAD_DIM)
    bm = bm.reshape(b, l, SSM_GROUPS, SSM_STATE)
    cm = cm.reshape(b, l, SSM_GROUPS, SSM_STATE)
    dt = jax.nn.softplus(dt + dt_bias).reshape(b, l, SSM_GROUPS, SSM_HPG)
    log_a = dt * (-jnp.exp(a_log.astype(F32))).reshape(SSM_GROUPS, SSM_HPG)
    s0 = s0.astype(F32).reshape(b, SSM_GROUPS, SSM_HPG, SSM_HEAD_DIM, SSM_STATE)
    y, s_fin = chunked_ssd(xs * dt[..., None], bm, cm, log_a, s0)
    y = y + xs * d_skip.reshape(SSM_GROUPS, SSM_HPG, 1)
    y = y.reshape(b, l, SSM_INNER) * jax.nn.silu(z)
    yg = y.reshape(b, l, SSM_GROUPS, SSM_INNER // SSM_GROUPS)
    yg = yg * lax.rsqrt(jnp.mean(yg * yg, axis=-1, keepdims=True) + RMS_EPS)
    out = yg.reshape(b, l, SSM_INNER) * norm_w
    return out, new_buf, s_fin.reshape(b, SSM_HEADS, SSM_HEAD_DIM, SSM_STATE)

def peer_ffn(x, w_q, sub_keys, u, v):
    b, l, d = x.shape
    t = b * l
    blk = min(PEER_BLOCK, t)
    pad = (-t) % blk
    xt = jnp.pad(x.reshape(t, d), ((0, pad), (0, 0)))

    def block(xb):
        q = (xb @ w_q).reshape(blk, PEER_HEADS, 2, PEER_HALF)
        s = jnp.einsum('thcd,chkd->thck', q, sub_keys).astype(F32)
        sv, si = lax.top_k(s, PEER_TOPK)
        cand = (sv[:, :, 0, :, None] + sv[:, :, 1, None, :]).reshape(blk, PEER_HEADS, PEER_TOPK * PEER_TOPK)
        top_s, ci = lax.top_k(cand, PEER_TOPK)
        i1 = jnp.take_along_axis(si[:, :, 0], ci // PEER_TOPK, axis=-1)
        i2 = jnp.take_along_axis(si[:, :, 1], ci % PEER_TOPK, axis=-1)
        e = i1 * PEER_KEYS + i2
        gate = jax.nn.softmax(top_s, axis=-1)
        act = jax.nn.gelu(jnp.einsum('thed,td->the', u[e], xb).astype(F32), approximate=False)
        return jnp.einsum('the,thed->td', (gate * act).astype(xb.dtype), v[e])

    y = lax.map(block, xt.reshape(-1, blk, d))
    return y.reshape(-1, d)[:t].reshape(b, l, d).astype(x.dtype)

def run_trunk(x, st_shift, st_rwkv, st_hgrn, st_ssm, st_conv, w):
    lb = jax.nn.softmax(w['hgrn_lower_bounds'].astype(F32), axis=0)
    lb = jnp.cumsum(lb, axis=0) - lb[0]
    n_shift, n_rwkv, n_hgrn, n_ssm, n_conv = [], [], [], [], []
    for i in range(DEPTH):
        j = i // 2
        h = rms_norm(x, w['norm_mix'][i])
        if i % 2 == 0:
            proj = h @ w['ab_w_in'][j]
            o_a, sh, sa = rwkv7_mixer(proj[..., :RWKV_PROJ], st_shift[j], st_rwkv[j],
                                      w['rwkv_mu'][j], w['rwkv_w0'][j], w['rwkv_w_up'][j], w['rwkv_a0'][j],
                                      w['rwkv_a_up'][j], w['rwkv_g_up'][j], w['rwkv_k_k'][j], w['rwkv_k_a'][j],
                                      w['rwkv_r_k'][j], w['rwkv_gn_w'][j], w['rwkv_gn_b'][j])
            o_b, sb = hgrn2_mixer(proj[..., RWKV_PROJ:], st_hgrn[j], lb[j], w['hgrn_norm_w'][j])
            mix = jnp.concatenate([o_a, o_b], axis=-1).astype(x.dtype) @ w['ab_w_out'][j]
            n_shift.append(sh); n_rwkv.append(sa); n_hgrn.append(sb)
        else:
            proj = h @ w['ssm_w_in'][j]
            o_c, cb, sc = mamba2_mixer(proj, st_conv[j], st_ssm[j], w['ssm_conv_w'][j], w['ssm_conv_b'][j],
                                       w['ssm_dt_bias'][j], w['ssm_a_log'][j], w['ssm_d'][j], w['ssm_norm_w'][j])
            mix = o_c.astype(x.dtype) @ w['ssm_w_out'][j]
            n_conv.append(cb); n_ssm.append(sc)
        x = x + mix
        x = x + peer_ffn(rms_norm(x, w['norm_ffn'][i]), w['peer_w_q'][i], w['peer_sub_keys'][i],
                         w['peer_u'][i], w['peer_v'][i])
    y = rms_norm(x, w['norm_final'])
    dt = x.dtype
    return (y, jnp.stack(n_shift).astype(dt), jnp.stack(n_rwkv).astype(dt), jnp.stack(n_hgrn).astype(dt),
            jnp.stack(n_ssm).astype(dt), jnp.stack(n_conv).astype(dt))

def setup_inputs(seed: int = 0) -> dict:
    key = jax.random.key(seed)
    ks = jax.random.split(key, 40)
    nrm = lambda k, shape, s: s * jax.random.normal(k, shape, F32)
    ones_n = lambda k, shape: 1.0 + 0.02 * jax.random.normal(k, shape, F32)
    dt0 = jnp.exp(jax.random.uniform(ks[29], (N_C, SSM_HEADS), F32, math.log(1e-3), math.log(1e-1)))
    return {
        'x_prompt': nrm(ks[0], (BATCH, SEQ, D_MODEL), 1.0),
        'x_sample': nrm(ks[1], (DEC_BATCH, DEC_SEQ, D_MODEL), 1.0),
        'state_rwkv_shift': nrm(ks[2], (N_AB, DEC_BATCH, RWKV_PROJ), 1.0),
        'state_rwkv': nrm(ks[3], (N_AB, DEC_BATCH, RWKV_HEADS, RWKV_HEAD_DIM, RWKV_HEAD_DIM), 0.5),
        'state_hgrn': nrm(ks[4], (N_AB, DEC_BATCH, HGRN_HEADS, HGRN_EXPAND, HGRN_EXPAND), 0.5),
        'state_ssm': nrm(ks[5], (N_C, DEC_BATCH, SSM_HEADS, SSM_HEAD_DIM, SSM_STATE), 0.5),
        'state_conv': nrm(ks[6], (N_C, DEC_BATCH, CONV_WIDTH - 1, CONV_DIM), 1.0),
        'norm_mix': ones_n(ks[7], (DEPTH, D_MODEL)),
        'norm_ffn': ones_n(ks[8], (DEPTH, D_MODEL)),
        'norm_final': ones_n(ks[9], (D_MODEL,)),
        'ab_w_in': nrm(ks[10], (N_AB, D_MODEL, AB_PROJ), D_MODEL ** -0.5),
        'ab_w_out': nrm(ks[11], (N_AB, MIX_WIDTH, D_MODEL), MIX_WIDTH ** -0.5),
        'rwkv_mu': jax.random.uniform(ks[12], (N_AB, RWKV_PROJ), F32),
        'rwkv_w0': -0.5 + nrm(ks[13], (N_AB, RWKV_WIDTH), 0.5),
        'rwkv_w_up': nrm(ks[14], (N_AB, DECAY_LORA, RWKV_WIDTH), 0.5 * DECAY_LORA ** -0.5),
        'rwkv_a0': nrm(ks[15], (N_AB, RWKV_WIDTH), 0.5),
        'rwkv_a_up': nrm(ks[16], (N_AB, AAA_LORA, RWKV_WIDTH), 0.5 * AAA_LORA ** -0.5),
        'rwkv_g_up': nrm(ks[17], (N_AB, GATE_LORA, RWKV_WIDTH), GATE_LORA ** -0.5),
        'rwkv_k_k': 0.85 + nrm(ks[18], (N_AB, RWKV_WIDTH), 0.1),
        'rwkv_k_a': 1.0 + nrm(ks[19], (N_AB, RWKV_WIDTH), 0.1),
        'rwkv_r_k': nrm(ks[20], (N_AB, RWKV_HEADS, RWKV_HEAD_DIM), 0.1),
        'rwkv_gn_w': ones_n(ks[21], (N_AB, RWKV_WIDTH)),
        'rwkv_gn_b': nrm(ks[22], (N_AB, RWKV_WIDTH), 0.02),
        'hgrn_lower_bounds': nrm(ks[23], (N_AB, HGRN_WIDTH), 0.5),
        'hgrn_norm_w': ones_n(ks[24], (N_AB, HGRN_EXPAND)),
        'ssm_w_in': nrm(ks[25], (N_C, D_MODEL, SSM_PROJ), D_MODEL ** -0.5),
        'ssm_conv_w': nrm(ks[26], (N_C, CONV_WIDTH, CONV_DIM), CONV_WIDTH ** -0.5),
        'ssm_conv_b': nrm(ks[27], (N_C, CONV_DIM), 0.02),
        'ssm_dt_bias': dt0 + jnp.log(-jnp.expm1(-dt0)),
        'ssm_a_log': jnp.log(jax.random.uniform(ks[30], (N_C, SSM_HEADS), F32, 1.0, 16.0)),
        'ssm_d': 1.0 + nrm(ks[31], (N_C, SSM_HEADS), 0.1),
        'ssm_norm_w': ones_n(ks[32], (N_C, SSM_INNER)),
        'ssm_w_out': nrm(ks[33], (N_C, SSM_INNER, D_MODEL), SSM_INNER ** -0.5),
        'peer_w_q': nrm(ks[34], (DEPTH, D_MODEL, PEER_HEADS * PEER_KEY_DIM), D_MODEL ** -0.5),
        'peer_sub_keys': nrm(ks[35], (DEPTH, 2, PEER_HEADS, PEER_KEYS, PEER_HALF), PEER_HALF ** -0.5),
        'peer_u': nrm(ks[36], (DEPTH, PEER_EXPERTS, D_MODEL), D_MODEL ** -0.5),
        'peer_v': nrm(ks[37], (DEPTH, PEER_EXPERTS, D_MODEL), 0.5 * PEER_HEADS ** -0.5),
    }

def reference(x_prompt, x_sample, state_rwkv_shift, state_rwkv, state_hgrn, state_ssm, state_conv,
              norm_mix, norm_ffn, norm_final, ab_w_in, ab_w_out, rwkv_mu, rwkv_w0, rwkv_w_up, rwkv_a0,
              rwkv_a_up, rwkv_g_up, rwkv_k_k, rwkv_k_a, rwkv_r_k, rwkv_gn_w, rwkv_gn_b, hgrn_lower_bounds,
              hgrn_norm_w, ssm_w_in, ssm_conv_w, ssm_conv_b, ssm_dt_bias, ssm_a_log, ssm_d, ssm_norm_w,
              ssm_w_out, peer_w_q, peer_sub_keys, peer_u, peer_v):
    w = dict(norm_mix=norm_mix, norm_ffn=norm_ffn, norm_final=norm_final, ab_w_in=ab_w_in, ab_w_out=ab_w_out,
             rwkv_mu=rwkv_mu, rwkv_w0=rwkv_w0, rwkv_w_up=rwkv_w_up, rwkv_a0=rwkv_a0, rwkv_a_up=rwkv_a_up,
             rwkv_g_up=rwkv_g_up, rwkv_k_k=rwkv_k_k, rwkv_k_a=rwkv_k_a, rwkv_r_k=rwkv_r_k, rwkv_gn_w=rwkv_gn_w,
             rwkv_gn_b=rwkv_gn_b, hgrn_lower_bounds=hgrn_lower_bounds, hgrn_norm_w=hgrn_norm_w,
             ssm_w_in=ssm_w_in, ssm_conv_w=ssm_conv_w, ssm_conv_b=ssm_conv_b, ssm_dt_bias=ssm_dt_bias,
             ssm_a_log=ssm_a_log, ssm_d=ssm_d, ssm_norm_w=ssm_norm_w, ssm_w_out=ssm_w_out,
             peer_w_q=peer_w_q, peer_sub_keys=peer_sub_keys, peer_u=peer_u, peer_v=peer_v)
    bp = x_prompt.shape[0]
    y_prompt, p_shift, p_rwkv, p_hgrn, p_ssm, p_conv = run_trunk(
        x_prompt,
        jnp.zeros((N_AB, bp, RWKV_PROJ), F32),
        jnp.zeros((N_AB, bp, RWKV_HEADS, RWKV_HEAD_DIM, RWKV_HEAD_DIM), F32),
        jnp.zeros((N_AB, bp, HGRN_HEADS, HGRN_EXPAND, HGRN_EXPAND), F32),
        jnp.zeros((N_C, bp, SSM_HEADS, SSM_HEAD_DIM, SSM_STATE), F32),
        jnp.zeros((N_C, bp, CONV_WIDTH - 1, CONV_DIM), F32),
        w)
    y_sample, s_shift, s_rwkv, s_hgrn, s_ssm, s_conv = run_trunk(
        x_sample, state_rwkv_shift, state_rwkv, state_hgrn, state_ssm, state_conv, w)
    return (y_prompt, y_sample, p_shift, p_rwkv, p_hgrn, p_ssm, p_conv, s_shift, s_rwkv, s_hgrn, s_ssm, s_conv)


_drawn_inputs = setup_inputs


def setup_inputs(seed=0):
    import zlib

    import numpy as np

    out = dict(_drawn_inputs(seed))
    spreads = {}
    factors = {'norm_ffn': 9.086,
     'norm_final': 7.93,
     'rwkv_gn_w': 4.302,
     'rwkv_gn_b': 3.627,
     'hgrn_norm_w': 3.604,
     'ssm_norm_w': 10.797}
    for name, (base, spread) in spreads.items():
        noise = np.random.default_rng([zlib.crc32(name.encode()), seed]).standard_normal(out[name].shape)
        drawn = base * np.exp(spread * noise) if base else spread * noise
        out[name] = jnp.asarray(drawn.astype(out[name].dtype))
    for name, factor in factors.items():
        out[name] = (out[name] * factor).astype(out[name].dtype)
    return out
```

```python
from contextlib import ExitStack

import concourse.bass as bass
from concourse import mybir

F32 = mybir.dt.float32
U32 = mybir.dt.uint32
ACT = mybir.ActivationFunctionType
ALU = mybir.AluOpType
AX_X = mybir.AxisListType.X

P = 128
D_MODEL = 1024
SEQ = 256
DEC = 8
T = SEQ + DEC
KC = D_MODEL // P
RMS_EPS = 1e-6


class Count:

    def __init__(self, nc, name):
        self.sem = nc.alloc_semaphore(name)
        self.at = 0

    def inc(self, ins, by=1):
        ins.then_inc(self.sem, by)
        self.at += by
        return self.at


class Link:

    def __init__(self, eng, count):
        self.eng, self.count = eng, count

    def __call__(self, ins):
        self.eng.wait_ge(self.count.sem, self.count.inc(ins))


class Core:

    def __init__(self, nc, ctx):
        self.nc, self.ctx = nc, ctx
        self.names = 0
        self.dve_done = Count(nc, "dve_done")
        self.act_done = Count(nc, "act_done")
        self.pool_done = Count(nc, "pool_done")
        self.pe_done = Count(nc, "pe_done")
        self.loaded = Count(nc, "loaded")
        self.stored = Count(nc, "stored")
        self.tile_loaded = [Count(nc, f"tile_loaded{i}") for i in range(8)]
        self.tile_multiplied = Count(nc, "tile_multiplied")
        self.tile_evicted = Count(nc, "tile_evicted")

    def sb(self, ctx, name, shape, dt=F32):
        self.names += 1
        return ctx.enter_context(self.nc.sbuf_tensor(f"{name}_{self.names}", shape, dt))[:]

    def banks(self, ctx, name, n):
        self.names += 1
        return [ctx.enter_context(self.nc.psum_tensor(f"{name}_{self.names}_{i}", [P, 512], F32)) for i in range(n)]

    def load(self, eng, dst, src):
        self.loaded.inc(eng.dma_start(dst, src), 16)

    def wait_loads(self, eng):
        eng.wait_ge(self.loaded.sem, self.loaded.at)


def constants(core, ctx):
    nc = core.nc
    core.ident = core.sb(ctx, "ident", [P, P])
    core.ones = core.sb(ctx, "ones", [P, P])
    core.block_ones = core.sb(ctx, "block_ones", [P, P])
    core.index_row = core.sb(ctx, "index_row", [P, P])
    with nc.Block() as block:
        @block.gpsimd
        def _(pool):
            link = Link(pool, core.pool_done)
            link(pool.iota(core.index_row, [[1, P]], base=0, channel_multiplier=0,
                           allow_small_or_imprecise_dtypes=True))
            link(pool.memset(core.ident, 0.0))
            link(pool.affine_select(core.ident, core.ident, [[-1, P]], ALU.not_equal, 1.0, 0, 1))
            link(pool.memset(core.ones, 1.0))
            link(pool.memset(core.block_ones, 0.0))
            link(pool.memset(core.block_ones[0:64, 0:64], 1.0))
            link(pool.memset(core.block_ones[64:128, 64:128], 1.0))


def rms_norm(core, x, weight, out):
    nc = core.nc
    with ExitStack() as ctx:
        squares = core.sb(ctx, "squares", [P, KC, T])
        rstd = core.sb(ctx, "rstd", [P, T])
        (total,) = core.banks(ctx, "square_sum", 1)
        squared, summed, mean_ready, root_ready = (
            core.act_done.at, core.pe_done.at, core.dve_done.at, core.act_done.at + 1)
        with nc.Block() as block:
            @block.scalar
            def _(act):
                core.act_done.inc(act.activation(squares[:], x, ACT.Square))
                act.wait_ge(core.dve_done.sem, mean_ready + 1)
                core.act_done.inc(act.activation(rstd[:], rstd[:], ACT.Sqrt))

            @block.tensor
            def _(pe):
                pe.wait_ge(core.act_done.sem, squared + 1)
                for k in range(KC):
                    last = pe.matmul(total[:, 0:T], core.ones, squares[:, k, :], start=k == 0, stop=k == KC - 1)
                core.pe_done.inc(last)

            @block.vector
            def _(dve):
                link = Link(dve, core.dve_done)
                dve.wait_ge(core.pe_done.sem, summed + 1)
                core.dve_done.inc(dve.tensor_scalar(rstd[:], total[:, 0:T], 1.0 / D_MODEL, RMS_EPS, ALU.mult, ALU.add))
                dve.wait_ge(core.act_done.sem, root_ready + 1)
                link(dve.reciprocal(rstd[:], rstd[:]))
                for k in range(KC):
                    dve.scalar_tensor_tensor(out[:, k, :], x[:, k, :], weight[:, k:k + 1], rstd[:],
                                             ALU.mult, ALU.mult)


def tile_loop(eng, n, unroll, one):
    for u in range(min(n, unroll)):
        one(0, u)
    if n // unroll > 1:
        with eng.Fori(1, n // unroll) as i:
            for u in range(unroll):
                one(i, u)
    if n > unroll:
        for u in range(n % unroll):
            one(n // unroll, u)


def project(core, weights, n, kc, rhs, dst, unroll=4, width=T, residual=False):
    nc = core.nc
    with ExitStack() as ctx:
        ring = core.sb(ctx, "weight_ring", [P, unroll, kc * P])
        banks = core.banks(ctx, "projected", unroll)
        loaded0 = [c.at for c in core.tile_loaded]
        done0, out0 = core.tile_multiplied.at, core.tile_evicted.at
        with nc.Block() as block:
            @block.sync
            def _(sp):
                def load(i, u):
                    if not (isinstance(i, int) and i == 0):
                        sp.wait_ge(core.tile_multiplied.sem, (i - 1) * unroll + (u + 1 + done0))
                    sp.dma_start(ring[:, u, :], weights[bass.ds(i * unroll + u, 1)].rearrange("a p f -> p (a f)")
                                 ).then_inc(core.tile_loaded[u].sem, 16)
                tile_loop(sp, n, unroll, load)

            @block.tensor
            def _(pe):
                def multiply(i, u):
                    pe.wait_ge(core.tile_loaded[u].sem, i * 16 + (16 + loaded0[u]))
                    if not (isinstance(i, int) and i == 0):
                        pe.wait_ge(core.tile_evicted.sem, (i - 1) * unroll + (u + 1 + out0))
                    for k in range(kc):
                        last = pe.matmul(banks[u][:, 0:width], ring[:, u, k * P:(k + 1) * P], rhs[:, k, :],
                                         start=k == 0, stop=k == kc - 1)
                    last.then_inc(core.tile_multiplied.sem, 1)
                tile_loop(pe, n, unroll, multiply)

            def evict(eng, i, u):
                eng.wait_ge(core.tile_multiplied.sem, i * unroll + (u + 1 + done0))
                to = dst[:, bass.ds(i * unroll + u, 1), :]
                got = banks[u][:, 0:width].rearrange("p (a f) -> p a f", a=1)
                if residual:
                    ins = eng.tensor_tensor(to, got, to, ALU.add)
                else:
                    ins = eng.copy(to, got)
                ins.then_inc(core.tile_evicted.sem, 1)

            if residual:
                @block.vector
                def _(dve):
                    tile_loop(dve, n, unroll, lambda i, u: evict(dve, i, u))
            else:
                @block.scalar
                def _(act):
                    tile_loop(act, n, unroll, lambda i, u: evict(act, i, u))
        for u in range(unroll):
            core.tile_loaded[u].at += 16 * (n // unroll + (u < n % unroll))
        core.tile_multiplied.at += n
        core.tile_evicted.at += n


PEER_HEADS = 8
KEYS = 128
TOPK = 16
SETS = 2 * PEER_HEADS
TOKEN_TILES = [(0, P), (P, P), (2 * P, DEC)]
LOWEST = -3.0e38


def peer_scores(core, h, w_q, sub_keys, scores):
    nc = core.nc
    with ExitStack() as ctx:
        queries = core.sb(ctx, "queries", [P, SETS, T])
        keys = core.sb(ctx, "keys", [P, SETS, KEYS])
        with nc.Block() as block:
            @block.sync
            def _(sp):
                core.load(sp, keys[:], sub_keys)

            @block.gpsimd
            def _(pool):
                core.pool_done.inc(pool.memset(scores[:, 2, :, :], 0.0))
        project(core, w_q, SETS, KC, h, queries)
        banks = core.banks(ctx, "score", 4)
        per_tile = SETS // 4
        done0, out0 = core.pe_done.at, core.act_done.at
        with nc.Block() as block:
            @block.tensor
            def _(pe):
                core.wait_loads(pe)
                for tile, (t0, rows) in enumerate(TOKEN_TILES):
                    for q in range(per_tile):
                        n = tile * per_tile + q
                        if n >= 4:
                            pe.wait_ge(core.act_done.sem, out0 + n - 3)
                        for s in range(4):
                            last = pe.matmul(banks[n % 4][0:rows, s * KEYS:(s + 1) * KEYS],
                                             queries[:, 4 * q + s, t0:t0 + rows], keys[:, 4 * q + s, :],
                                             start=True, stop=True)
                        core.pe_done.inc(last)

            @block.scalar
            def _(act):
                for tile, (t0, rows) in enumerate(TOKEN_TILES):
                    for q in range(per_tile):
                        n = tile * per_tile + q
                        act.wait_ge(core.pe_done.sem, done0 + n + 1)
                        core.act_done.inc(act.copy(scores[0:rows, tile, 4 * q:4 * q + 4, :],
                                                   banks[n % 4][0:rows, :].rearrange("p (s k) -> p s k", s=4)))


def top16(dve, link, values, sets, top, index):
    for s in range(sets):
        last = dve.max(top[:, s, 0:8], values(s))
    link(last)
    for s in range(sets):
        dve.max_index(index[:, s, 0:8], top[:, s, 0:8], values(s))
    for s in range(sets):
        last = dve.match_replace(values(s), top[:, s, 0:8], values(s), LOWEST)
    link(last)
    for s in range(sets):
        last = dve.max(top[:, s, 8:16], values(s))
    link(last)
    for s in range(sets):
        last = dve.max_index(index[:, s, 8:16], top[:, s, 8:16], values(s))
    link(last)


def peer_select(core, scores, first_t, second_t, gate_t):
    nc = core.nc
    links = 20
    with ExitStack() as ctx:
        top = core.sb(ctx, "top", [P, SETS, TOPK])
        index = core.sb(ctx, "index", [P, SETS, TOPK], U32)
        index_f = core.sb(ctx, "index_f", [P, SETS, TOPK])
        pairs = core.sb(ctx, "pairs", [P, PEER_HEADS, TOPK, TOPK])
        best = core.sb(ctx, "best", [P, PEER_HEADS, TOPK])
        place = core.sb(ctx, "place", [P, PEER_HEADS, TOPK], U32)
        rank = core.sb(ctx, "rank", [P, 2, PEER_HEADS, TOPK], U32)
        rank_f = core.sb(ctx, "rank_f", [P, 2, PEER_HEADS, TOPK])
        hit = core.sb(ctx, "hit", [P, PEER_HEADS, TOPK, TOPK])
        chosen = core.sb(ctx, "chosen", [P, 3, 3, PEER_HEADS, TOPK])
        total = core.sb(ctx, "total", [P, PEER_HEADS])
        bases = core.dve_done.at
        exp_done = core.act_done.at
        with nc.Block() as block:
            @block.vector
            def _(dve):
                for tile in range(3):
                    link = Link(dve, core.dve_done)
                    top16(dve, link, lambda s: scores[:, tile, s, :], SETS, top, index)
                    dve.tensor_copy(index_f[:], index[:])
                    by_head = top[:].rearrange("p (h c) k -> p h c k", c=2)
                    link(dve.tensor_tensor(
                        pairs[:], by_head[:, :, 0, :].unsqueeze(3).broadcast_to((P, PEER_HEADS, TOPK, TOPK)),
                        by_head[:, :, 1, :].unsqueeze(2).broadcast_to((P, PEER_HEADS, TOPK, TOPK)), ALU.add))
                    top16(dve, link, lambda s: pairs[:, s, :, :].rearrange("p i j -> p (i j)"), PEER_HEADS, best, place)
                    dve.tensor_single_scalar(rank[:, 0], place[:], 4, ALU.logical_shift_right)
                    dve.tensor_single_scalar(rank[:, 1], place[:], 15, ALU.bitwise_and)
                    link(dve.tensor_tensor(chosen[:, tile, 2], best[:],
                                           best[:, :, 0:1].broadcast_to((P, PEER_HEADS, TOPK)), ALU.subtract))
                    link(dve.tensor_copy(rank_f[:], rank[:]))
                    for c in range(2):
                        steps = core.index_row[:, 0:TOPK].unsqueeze(1).unsqueeze(1).broadcast_to(
                            (P, PEER_HEADS, TOPK, TOPK))
                        link(dve.tensor_tensor(hit[:], rank_f[:, c].unsqueeze(3).broadcast_to(
                            (P, PEER_HEADS, TOPK, TOPK)), steps, ALU.is_equal))
                        ids = index_f[:].rearrange("p (h c) k -> p h c k", c=2)[:, :, c, :]
                        link(dve.tensor_tensor(hit[:], hit[:], ids.unsqueeze(2).broadcast_to(
                            (P, PEER_HEADS, TOPK, TOPK)), ALU.mult))
                        link(dve.tensor_reduce(chosen[:, tile, c], hit[:], AX_X, ALU.add))
                    dve.wait_ge(core.act_done.sem, exp_done + tile + 1)
                    link(dve.tensor_reduce(total[:], chosen[:, tile, 2], AX_X, ALU.add))
                    link(dve.reciprocal(total[:], total[:]))
                    link(dve.tensor_tensor(chosen[:, tile, 2], chosen[:, tile, 2],
                                           total[:].unsqueeze(2).broadcast_to((P, PEER_HEADS, TOPK)), ALU.mult))
            per_tile = (core.dve_done.at - bases) // 3

            @block.scalar
            def _(act):
                for tile in range(3):
                    act.wait_ge(core.dve_done.sem, bases + tile * per_tile + 10)
                    core.act_done.inc(act.activation(chosen[:, tile, 2], chosen[:, tile, 2], ACT.Exp))

        banks = core.banks(ctx, "turned", 3)
        turned = core.pe_done.at
        with nc.Block() as block:
            @block.tensor
            def _(pe):
                for kind in range(3):
                    for tile, (t0, rows) in enumerate(TOKEN_TILES):
                        last = pe.transpose(banks[kind][:, t0:t0 + rows],
                                            chosen[0:rows, tile, kind].rearrange("p h k -> p (h k)"),
                                            core.ident[0:rows, 0:rows])
                    core.pe_done.inc(last)

            @block.vector
            def _(dve):
                for kind, dst in enumerate((first_t, second_t, gate_t)):
                    dve.wait_ge(core.pe_done.sem, turned + kind + 1)
                    dve.tensor_copy(dst[:], banks[kind][:, 0:T])


def peer_gates(core, first_t, second_t, gate_t, gates):
    nc = core.nc
    quad = 4
    with ExitStack() as ctx:
        one_hot = core.sb(ctx, "one_hot", [P, 2, quad, KEYS])
        weighted = core.sb(ctx, "weighted", [P, 2, quad, KEYS])
        banks = core.banks(ctx, "gate", 2)
        n = T // quad
        weighted0, mult0, out0 = core.dve_done.at, core.pe_done.at, core.act_done.at
        first_round = lambda i: isinstance(i, int) and i == 0
        with nc.Block() as block:
            def build(eng, i, u, t, first):
                token = i * (2 * quad) + (u * quad + t)
                if first:
                    return eng.tensor_scalar(one_hot[:, u, t, :], core.index_row, first_t[:, bass.ds(token, 1)],
                                             None, ALU.is_equal)
                return eng.tensor_scalar(weighted[:, u, t, :], core.index_row, second_t[:, bass.ds(token, 1)],
                                         gate_t[:, bass.ds(token, 1)], ALU.is_equal, ALU.mult)

            @block.vector
            def _(dve):
                def quarter(i, u):
                    if not first_round(i):
                        dve.wait_ge(core.pe_done.sem, i * 2 + (u - 1 + mult0))
                    for t in range(quad):
                        build(dve, i, u, t, True)
                        last = build(dve, i, u, t, False)
                    last.then_inc(core.dve_done.sem, 1)
                tile_loop(dve, n, 2, quarter)

            @block.tensor
            def _(pe):
                def quarter(i, u):
                    pe.wait_ge(core.dve_done.sem, i * 2 + (u + 1 + weighted0))
                    if not first_round(i):
                        pe.wait_ge(core.act_done.sem, i * 2 + (u - 1 + out0))
                    for t in range(quad):
                        last = pe.matmul(banks[u][:, t * KEYS:(t + 1) * KEYS], one_hot[:, u, t, :],
                                         weighted[:, u, t, :], start=True, stop=True)
                    last.then_inc(core.pe_done.sem, 1)
                tile_loop(pe, n, 2, quarter)

            @block.scalar
            def _(act):
                def quarter(i, u):
                    act.wait_ge(core.pe_done.sem, i * 2 + (u + 1 + mult0))
                    act.copy(gates[:, :, bass.ds(i * (2 * quad) + u * quad, quad)].rearrange("p k t -> p t k"),
                             banks[u][:, :].rearrange("p (t k) -> p t k", t=quad)).then_inc(core.act_done.sem, 1)
                tile_loop(act, n, 2, quarter)
        for c in (core.dve_done, core.pe_done, core.act_done):
            c.at += n


def peer_experts(core, x, h, up_w, down_w, gates, rings):
    nc = core.nc
    pair = 2
    groups = KEYS // pair
    up_ring, down_ring, up_loaded, down_loaded = rings
    with ExitStack() as ctx:
        gelu = core.sb(ctx, "gelu", [P, 4, T])
        active = core.sb(ctx, "active", [P, 4, T])
        up_banks = core.banks(ctx, "up", 4)
        sum_banks = core.banks(ctx, "down", 4)
        up0, gelu0, active0 = core.pe_done.at, core.act_done.at, core.dve_done.at
        down0, added0 = core.tile_multiplied.at, core.tile_evicted.at
        upl0, downl0 = [c.at for c in up_loaded], [c.at for c in down_loaded]
        at_start = lambda i: isinstance(i, int) and i == 0

        def rounds(eng, body):
            body(0)
            with eng.Fori(1, KEYS // 4) as i:
                body(i)

        with nc.Block() as block:
            @block.sync
            def _(sp):
                def body(i):
                    for s in range(4):
                        if not at_start(i):
                            sp.wait_ge(core.pe_done.sem, i * 4 + (s - 3 + up0))
                        sp.dma_start(up_ring[:, s, :], up_w[bass.ds(i * 4 + s, 1)].rearrange("a p f -> p (a f)")
                                     ).then_inc(up_loaded[s].sem, 16)
                        if s % 2 == 1:
                            for r in (s - 1, s):
                                if not at_start(i):
                                    sp.wait_ge(core.tile_multiplied.sem, i * (2 * KC) + (-2 * KC + (s // 2 + 1) * KC + down0))
                                sp.dma_start(down_ring[:, r, :], down_w[bass.ds(i * 4 + r, 1)].rearrange(
                                    "a p f -> p (a f)")).then_inc(down_loaded[r].sem, 16)
                rounds(sp, body)

            @block.tensor
            def _(pe):
                def up(i, s):
                    pe.wait_ge(up_loaded[s].sem, i * 16 + (16 + upl0[s]))
                    if not at_start(i):
                        pe.wait_ge(core.act_done.sem, i * 4 + (s - 3 + gelu0))
                    for k in range(KC):
                        last = pe.matmul(up_banks[s][:, 0:T], up_ring[:, s, k * P:(k + 1) * P], h[:, k, :],
                                         start=k == 0, stop=k == KC - 1)
                    last.then_inc(core.pe_done.sem, 1)

                def down(i, g, begun=False):
                    for s in (2 * g, 2 * g + 1):
                        pe.wait_ge(down_loaded[s].sem, i * 16 + (16 + downl0[s]))
                    pe.wait_ge(core.dve_done.sem, i * 4 + (2 * g + 2 + active0))
                    for d in range(KC):
                        if not (begun and d < 4):
                            pe.wait_ge(core.tile_evicted.sem, i * (2 * KC) + (g * KC + d - 3 + added0))
                        for s in (2 * g, 2 * g + 1):
                            last = pe.matmul(sum_banks[d % 4][:, 0:T], down_ring[:, s, d * P:(d + 1) * P],
                                             active[:, s, :], start=s == 2 * g, stop=s == 2 * g + 1)
                        last.then_inc(core.tile_multiplied.sem, 1)

                up(0, 0)
                up(0, 1)
                up(0, 2)
                up(0, 3)
                down(0, 0, begun=True)
                with pe.Fori(1, KEYS // 4) as i:
                    up(i, 0)
                    up(i, 1)
                    down(i - 1, 1)
                    up(i, 2)
                    up(i, 3)
                    down(i, 0)
                down(KEYS // 4 - 1, 1)

            @block.scalar
            def _(act):
                def body(i):
                    for s in range(4):
                        act.wait_ge(core.pe_done.sem, i * 4 + (s + 1 + up0))
                        if not at_start(i):
                            act.wait_ge(core.dve_done.sem, i * 4 + (s - 3 + active0))
                        act.activation(gelu[:, s, :], up_banks[s][:, 0:T], ACT.Gelu).then_inc(core.act_done.sem, 1)
                rounds(act, body)

            @block.vector
            def _(dve):
                def gate(i, s):
                    dve.wait_ge(core.act_done.sem, i * 4 + (s + 1 + gelu0))
                    if not at_start(i):
                        dve.wait_ge(core.tile_multiplied.sem, i * (2 * KC) + (-2 * KC + (s // 2 + 1) * KC + down0))
                    dve.tensor_tensor(active[:, s, :], gelu[:, s, :], gates[:, bass.ds(i * 4 + s, 1), :].rearrange(
                        "p a t -> p (a t)"), ALU.mult).then_inc(core.dve_done.sem, 1)

                def add(i, g):
                    for d in range(KC):
                        dve.wait_ge(core.tile_multiplied.sem, i * (2 * KC) + (g * KC + d + 1 + down0))
                        dve.tensor_tensor(x[:, d, :], sum_banks[d % 4][:, 0:T], x[:, d, :], ALU.add
                                          ).then_inc(core.tile_evicted.sem, 1)

                for s in range(4):
                    gate(0, s)
                add(0, 0)
                with dve.Fori(1, KEYS // 4) as i:
                    gate(i, 0)
                    gate(i, 1)
                    add(i - 1, 1)
                    gate(i, 2)
                    gate(i, 3)
                    add(i, 0)
                add(KEYS // 4 - 1, 1)
        for c, n in ((core.pe_done, KEYS), (core.act_done, KEYS), (core.dve_done, KEYS),
                     (core.tile_multiplied, groups * KC), (core.tile_evicted, groups * KC)):
            c.at += n
        for c in up_loaded + down_loaded:
            c.at += 16 * (KEYS // 4)


def peer(core, x, norm_w, w_q, sub_keys, up_w, down_w):
    with ExitStack() as ctx:
        h = core.sb(ctx, "ffn_in", [P, KC, T])
        rms_norm(core, x, norm_w, h)
        first_t = core.sb(ctx, "first_t", [P, T])
        second_t = core.sb(ctx, "second_t", [P, T])
        gate_t = core.sb(ctx, "gate_t", [P, T])
        with ExitStack() as select:
            scores = core.sb(select, "scores", [P, 3, SETS, KEYS])
            peer_scores(core, h, w_q, sub_keys, scores)
            peer_select(core, scores, first_t, second_t, gate_t)
        gates = core.sb(ctx, "gates", [P, KEYS, T])
        peer_gates(core, first_t, second_t, gate_t, gates)
        up_ring = core.sb(ctx, "up_ring", [P, 4, D_MODEL])
        down_ring = core.sb(ctx, "down_ring", [P, 4, D_MODEL])
        peer_experts(core, x, h, up_w, down_w, gates,
                     (up_ring, down_ring, core.tile_loaded[0:4], core.tile_loaded[4:8]))


HALVES = SEQ // P
CHUNK = 64
CHUNKS = SEQ // CHUNK
RWKV_TILES = 4
SHIFT_TILES = 14
AB_TILES = 30
GN_EPS = 64e-5
L2_EPS = 1e-12
DECAY_SCALE = -0.6065306597126334

AB_PARAM = {}
_at = 0
for _name, _n in (("norm", 8), ("mu", 14), ("w0", 4), ("a0", 4), ("k_k", 4), ("k_a", 4), ("r_k", 4), ("gn_w", 4),
                  ("gn_b", 4), ("bound", 4), ("hgrn_norm", 1)):
    AB_PARAM[_name] = slice(_at, _at + _n)
    _at += _n
AB_PARAMS = _at

MASK_QUAD = 0
MASK_LOWER = 4
MASK_LEVEL = 5
MASK_FIRST = 12
MASK_CAUSAL = 13
MASK_EYE64 = 14
MASK_SCAN64 = 15
MASK_SCAN128 = 17
MASKS = 19


def masks():
    import numpy as np
    s, t = np.arange(P)[:, None], np.arange(P)[None, :]
    m = np.zeros((P, MASKS, P), np.float32)
    same = s // CHUNK == t // CHUNK
    m[:, 0], m[:, 1], m[:, 2], m[:, 3] = same & (s < t), same & (s <= t), same & (s < t), same & (s <= t)
    m[:, MASK_LOWER] = same & (t < s)
    for level in range(7):
        w = 1 << level
        m[:, MASK_LEVEL + level] = (s // (2 * w) == t // (2 * w)) & (s % (2 * w) < w) & (t % (2 * w) >= w)
    m[:, MASK_FIRST] = m[:, MASK_LEVEL].T
    m[:, MASK_CAUSAL] = s <= t
    m[:, MASK_EYE64] = (s % 64 == t) & (t < 64)
    m[:, MASK_SCAN64:MASK_SCAN64 + 2] = (np.arange(SEQ) % 64 != 0).reshape(2, P)
    m[:, MASK_SCAN128:MASK_SCAN128 + 2] = (np.arange(SEQ) % 128 != 0).reshape(2, P)
    return m


def sum_features(core, weights, src, banks, n, start=0, width=T):
    with core.nc.Block() as block:
        @block.tensor
        def _(pe):
            for i in range(n):
                pe.matmul(banks[start + i][:, 0:width], weights, src[:, i, :], start=True, stop=True)


def inverse_root(core, banks, n, out, scale, eps):
    nc = core.nc
    with nc.Block() as block:
        @block.vector
        def _(dve):
            for i in range(n):
                dve.tensor_scalar(out[:, i, :], banks[i][:, 0:T], scale, eps, ALU.mult, ALU.add)
    with nc.Block() as block:
        @block.scalar
        def _(act):
            act.activation(out, out, ACT.Sqrt)
    with nc.Block() as block:
        @block.vector
        def _(dve):
            dve.reciprocal(out, out)


def rwkv_inputs(core, ctx, p, par, mask, shift_in, lora_up, gate_up, w):
    nc = core.nc
    tile4 = [P, RWKV_TILES, T]
    for name in ("logw", "rate", "gate", "kk", "key", "b", "bonus"):
        w[name] = core.sb(ctx, name, tile4)
    w["m"] = m = p[:, 0:SHIFT_TILES, :]
    with ExitStack() as local:
        diff = core.sb(local, "diff", [P, SHIFT_TILES, T])
        lora = core.sb(local, "lora", [P, 512])
        gup = core.sb(local, "gup", [P, 512])
        shift = core.sb(local, "shift", [P, SHIFT_TILES, DEC])
        hidden = core.sb(local, "hidden", [P, 2, T])
        work = core.sb(local, "work", tile4)
        with nc.Block() as block:
            @block.sync
            def _(sp):
                core.load(sp, lora, lora_up)
                core.load(sp, gup, gate_up)
                core.load(sp, shift, shift_in)
                core.wait_loads(sp)
        with nc.Block() as block:
            @block.vector
            def _(dve):
                link = Link(dve, core.dve_done)
                old = p[:, 0:SHIFT_TILES, :]
                dve.tensor_tensor(diff[:, :, 1:SEQ], old[:, :, 0:SEQ - 1], old[:, :, 1:SEQ], ALU.subtract)
                dve.tensor_scalar(diff[:, :, 0:1], old[:, :, 0:1], -1.0, None, ALU.mult)
                link(dve.tensor_tensor(diff[:, :, SEQ:T], shift, old[:, :, SEQ:T], ALU.subtract))
                for i in range(SHIFT_TILES):
                    dve.scalar_tensor_tensor(m[:, i, :], diff[:, i, :], par("mu", i), old[:, i, :],
                                             ALU.mult, ALU.add)
        with nc.Block() as block:
            @block.scalar
            def _(act):
                act.activation(hidden[0:64, 0, :], m[0:64, 12, :], ACT.Tanh)
                act.copy(hidden[64:128, 0, :], m[64:128, 12, :])
                act.activation(hidden[:, 1, :], m[:, 13, :], ACT.Sigmoid)
        with ExitStack() as ps:
            banks = core.banks(ps, "lora", 8)
            with nc.Block() as block:
                @block.tensor
                def _(pe):
                    for i in range(RWKV_TILES):
                        pe.matmul(banks[i][:, 0:T], lora[0:64, i * P:(i + 1) * P], hidden[0:64, 0, :],
                                  start=True, stop=True)
                        pe.matmul(banks[4 + i][:, 0:T], lora[64:128, i * P:(i + 1) * P], hidden[64:128, 0, :],
                                  start=True, stop=True)
            with nc.Block() as block:
                @block.scalar
                def _(act):
                    for i in range(RWKV_TILES):
                        act.activation(w["logw"][:, i, :], banks[i][:, 0:T], ACT.Sigmoid, bias=par("w0", i))
                        act.activation(w["rate"][:, i, :], banks[4 + i][:, 0:T], ACT.Sigmoid, bias=par("a0", i))

                @block.vector
                def _(dve):
                    link = Link(dve, core.dve_done)
                    for i in range(RWKV_TILES):
                        last = dve.tensor_scalar(w["kk"][:, i, :], m[:, 4 + i, :], par("k_k", i), None, ALU.mult)
                    link(last)
                    dve.tensor_tensor(work, w["kk"], w["kk"], ALU.mult)
            with nc.Block() as block:
                @block.tensor
                def _(pe):
                    for i in range(RWKV_TILES):
                        pe.matmul(banks[i][:, 0:T], gup[:, i * P:(i + 1) * P], hidden[:, 1, :], start=True, stop=True)
                        pe.matmul(banks[4 + i][:, 0:T], core.block_ones, work[:, i, :], start=True, stop=True)

                @block.vector
                def _(dve):
                    link = Link(dve, core.dve_done)
                    dve.tensor_scalar(w["logw"], w["logw"], DECAY_SCALE, None, ALU.mult)
                    for i in range(RWKV_TILES):
                        last = dve.tensor_scalar(w["key"][:, i, :], w["rate"][:, i, :], -1.0, par("k_a", i),
                                                 ALU.add, ALU.mult)
                    link(last)
                    dve.scalar_tensor_tensor(w["key"], w["key"], 1.0, m[:, 4:8, :], ALU.add, ALU.mult)
            with nc.Block() as block:
                @block.scalar
                def _(act):
                    for i in range(RWKV_TILES):
                        act.activation(work[:, i, :], banks[4 + i][:, 0:T], ACT.Sqrt)
                    for i in range(RWKV_TILES):
                        act.copy(w["gate"][:, i, :], banks[i][:, 0:T])
            with nc.Block() as block:
                @block.vector
                def _(dve):
                    link = Link(dve, core.dve_done)
                    link(dve.tensor_scalar(work, work, L2_EPS, None, ALU.max))
                    link(dve.reciprocal(work, work))
                    link(dve.tensor_tensor(w["kk"], w["kk"], work, ALU.mult))
                    dve.tensor_tensor(w["b"], w["kk"], w["rate"], ALU.mult)
                    for i in range(RWKV_TILES):
                        dve.scalar_tensor_tensor(work[:, i, :], m[:, i, :], par("r_k", i), w["key"][:, i, :],
                                                 ALU.mult, ALU.mult)
            sum_features(core, core.block_ones, work, banks, RWKV_TILES)
            with nc.Block() as block:
                @block.vector
                def _(dve):
                    for i in range(RWKV_TILES):
                        dve.tensor_tensor(w["bonus"][:, i, :], banks[i][:, 0:T], m[:, 8 + i, :], ALU.mult)


def rwkv_prompt(core, mask, w, out, state_out):
    nc = core.nc
    combos = [(hp, tile, half) for hp in range(2) for tile in range(RWKV_TILES) for half in range(HALVES)]
    combo_of = {c: n for n, c in enumerate(combos)}
    with ExitStack() as ctx:
        ar = core.sb(ctx, "ar", [P, RWKV_TILES, HALVES, 2, P])
        bh = core.sb(ctx, "bh", [P, RWKV_TILES, SEQ])
        kh = core.sb(ctx, "kh", [P, RWKV_TILES, SEQ])
        end_decay = core.sb(ctx, "end_decay", [P, CHUNKS, RWKV_TILES, P])
        prompt = lambda name: w[name][:, :, 0:SEQ]
        with ExitStack() as local:
            decay = core.sb(local, "decay", [P, RWKV_TILES, SEQ])
            grow = core.sb(local, "grow", [P, RWKV_TILES, SEQ])
            before = core.sb(local, "before", [P, RWKV_TILES, SEQ])
            logs = core.sb(local, "logs", [P, RWKV_TILES, SEQ])
            with nc.Block() as block:
                @block.vector
                def _(dve):
                    link = Link(dve, core.dve_done)
                    for i in range(RWKV_TILES):
                        last = dve.tensor_tensor_scan(logs[:, i, :], mask[:, MASK_SCAN64:MASK_SCAN64 + 2, :].rearrange(
                            "p a b -> p (a b)"), w["logw"][:, i, 0:SEQ], 0.0, ALU.mult, ALU.add)
                    link(last)
                    dve.tensor_tensor(before, logs, prompt("logw"), ALU.subtract)
            with nc.Block() as block:
                @block.scalar
                def _(act):
                    act.activation(decay, logs, ACT.Exp)
                    act.activation(grow, logs, ACT.Exp, scale=-1.0)
                    act.activation(before, before, ACT.Exp)
            with nc.Block() as block:
                @block.vector
                def _(dve):
                    for i in range(RWKV_TILES):
                        split = lambda a: a.rearrange("p (h j) -> p h j", h=HALVES)
                        dve.scalar_tensor_tensor(ar[:, i, :, 0, :], split(before[:, i, :]), -1.0,
                                                 split(w["kk"][:, i, 0:SEQ]), ALU.mult, ALU.mult)
                        dve.tensor_tensor(ar[:, i, :, 1, :], split(decay[:, i, :]), split(w["m"][:, i, 0:SEQ]), ALU.mult)
                    dve.tensor_tensor(bh, grow, prompt("b"), ALU.mult)
                    dve.tensor_tensor(kh, grow, prompt("key"), ALU.mult)

                @block.gpsimd
                def _(pool):
                    for c in range(CHUNKS):
                        at = c * CHUNK + CHUNK - 1
                        pool.tensor_tensor(end_decay[:, c], decay[:, :, at:at + 1].broadcast_to((P, RWKV_TILES, P)),
                                           core.block_ones.unsqueeze(1).broadcast_to((P, RWKV_TILES, P)), ALU.mult)
        quad = core.sb(ctx, "quad", [P, 16, 4, P])
        lower = core.sb(ctx, "lower", [P, 16, P])
        tu = core.sb(ctx, "tu", [P, 16, 2, P])
        toks = core.sb(ctx, "toks", [P, 3, HALVES, 512])
        with ExitStack() as ps:
            banks = core.banks(ps, "inside", 4)
            lows = core.banks(ps, "lower", 4)
            done0, out0 = core.pe_done.at, core.dve_done.at
            with nc.Block() as block:
                @block.tensor
                def _(pe):
                    for n, (hp, tile, half) in enumerate(combos):
                        rows, cols = slice(64 * hp, 64 * hp + 64), slice(half * P, half * P + P)
                        if n >= 4:
                            pe.wait_ge(core.dve_done.sem, out0 + n - 3)
                        rhs = ar[rows, tile, half].rearrange("p a j -> p (a j)")
                        pe.matmul(banks[n % 4][:, 0:256], bh[rows, tile, cols], rhs, start=True, stop=True)
                        core.pe_done.inc(pe.matmul(banks[n % 4][:, 256:512], kh[rows, tile, cols], rhs,
                                                   start=True, stop=True))
                    for n, (hp, tile, half) in enumerate(combos):
                        rows, cols = slice(64 * hp, 64 * hp + 64), slice(half * P, half * P + P)
                        last = pe.matmul(lows[n // 4][:, (n % 4) * P:(n % 4 + 1) * P], ar[rows, tile, half, 0, :],
                                         bh[rows, tile, cols], start=True, stop=True)
                    core.pe_done.inc(last)

                @block.vector
                def _(dve):
                    for n in range(16):
                        dve.wait_ge(core.pe_done.sem, done0 + n + 1)
                        core.dve_done.inc(dve.tensor_tensor(
                            quad[:, n].rearrange("p a j -> p (a j)"), banks[n % 4][:, :],
                            mask[:, MASK_QUAD:MASK_QUAD + 4, :].rearrange("p a j -> p (a j)"), ALU.mult))
                    dve.wait_ge(core.pe_done.sem, done0 + 17)
                    for g in range(4):
                        dve.tensor_tensor(lower[:, 4 * g:4 * g + 4, :],
                                          lows[g][:, :].rearrange("p (a j) -> p a j", a=4),
                                          mask[:, MASK_LOWER:MASK_LOWER + 1, :].broadcast_to((P, 4, P)), ALU.mult)
        with ExitStack() as ps:
            banks = core.banks(ps, "turned", 6)
            done0 = core.pe_done.at
            with nc.Block() as block:
                @block.tensor
                def _(pe):
                    for kind, src in enumerate((w["m"][:, 8:12, :], bh, kh)):
                        for half in range(HALVES):
                            for tile in range(RWKV_TILES):
                                last = pe.transpose(banks[kind * 2 + half][:, tile * P:(tile + 1) * P],
                                                    src[:, tile, half * P:(half + 1) * P], core.ident)
                            core.pe_done.inc(last)

                @block.scalar
                def _(act):
                    for n in range(6):
                        act.wait_ge(core.pe_done.sem, done0 + n + 1)
                        act.copy(toks[:, n // 2, n % 2, :], banks[n][:, :])

                @block.vector
                def _(dve):
                    link = Link(dve, core.dve_done)
                    wide = lambda k: mask[:, k:k + 1, :].broadcast_to((P, 16, P))
                    dve.tensor_tensor(tu[:, :, 0, :], lower, wide(MASK_FIRST), ALU.mult)
                    link(dve.tensor_tensor(tu[:, :, 1, :], quad[:, :, 0, :], wide(MASK_LEVEL), ALU.mult))
                    eye = core.ident.unsqueeze(1).broadcast_to((P, 16, P))
                    dve.tensor_tensor(tu[:, :, 0, :], tu[:, :, 0, :], eye, ALU.add)
                    dve.tensor_tensor(tu[:, :, 1, :], tu[:, :, 1, :], eye, ALU.add)
        with ExitStack() as ps:
            part = core.sb(ps, "part", [P, 2, 16, P])
            product = core.sb(ps, "product", [P, 4, 4 * P])
            first = core.banks(ps, "first", 4)
            second = core.banks(ps, "second", 4)
            levels = 5
            part0, first0, copied0, second0, added0 = (core.pool_done.at, core.pe_done.at, core.act_done.at,
                                                       core.tile_multiplied.at, core.dve_done.at)
            with nc.Block() as block:
                @block.gpsimd
                def _(pool):
                    for level in range(levels):
                        if level >= 2:
                            pool.wait_ge(core.pe_done.sem, first0 + 4 * (level - 1))
                        core.pool_done.inc(pool.tensor_tensor(
                            part[:, level % 2], quad[:, :, 0, :],
                            mask[:, MASK_LEVEL + 1 + level:MASK_LEVEL + 2 + level, :].broadcast_to((P, 16, P)),
                            ALU.mult))

                @block.tensor
                def _(pe):
                    for level in range(levels):
                        pe.wait_ge(core.pool_done.sem, part0 + level + 1)
                        for g in range(4):
                            if level:
                                pe.wait_ge(core.dve_done.sem, added0 + (level - 1) * 8 + 2 * g + 2)
                            for c in range(4 * g, 4 * g + 4):
                                last = pe.matmul(first[g][:, (c % 4) * P:(c % 4 + 1) * P], part[:, level % 2, c, :],
                                                 tu[:, c, 0, :], start=True, stop=True)
                            core.pe_done.inc(last)
                        for g in range(4):
                            pe.wait_ge(core.act_done.sem, copied0 + level * 4 + g + 1)
                            for c in range(4 * g, 4 * g + 4):
                                n = (level * 16 + c) // 2
                                if c % 2 == 0 and n >= 4:
                                    pe.wait_ge(core.dve_done.sem, added0 + n - 3)
                                o = (c % 2) * 256
                                y = product[:, g, (c % 4) * P:(c % 4 + 1) * P]
                                pe.matmul(second[n % 4][:, o:o + P], tu[:, c, 1, :], y, start=True, stop=True)
                                last = pe.matmul(second[n % 4][:, o + P:o + 2 * P], y, tu[:, c, 1, :],
                                                 start=True, stop=True)
                                if c % 2:
                                    core.tile_multiplied.inc(last)

                @block.scalar
                def _(act):
                    for level in range(levels):
                        for g in range(4):
                            act.wait_ge(core.pe_done.sem, first0 + level * 4 + g + 1)
                            if level:
                                act.wait_ge(core.tile_multiplied.sem, second0 + (level - 1) * 8 + 2 * g + 2)
                            core.act_done.inc(act.copy(product[:, g, :], first[g][:, :]))

                @block.vector
                def _(dve):
                    for n in range(levels * 8):
                        c = (2 * n) % 16
                        dve.wait_ge(core.tile_multiplied.sem, second0 + n + 1)
                        to = tu[:, c:c + 2].rearrange("p c a j -> p (c a j)")
                        core.dve_done.inc(dve.tensor_tensor(to, second[n % 4][:, :], to, ALU.add))
        with ExitStack() as ps:
            state = core.sb(ps, "state", [P, RWKV_TILES, P])
            grown = core.sb(ps, "grown", [P, RWKV_TILES, P])
            rhs = core.sb(ps, "rhs", [P, 512])
            sa = core.sb(ps, "sa", [P, 512])
            b_rhs, b_sa, b_out, b_state = core.banks(ps, "chunk", 4)
            with nc.Block() as block:
                @block.gpsimd
                def _(pool):
                    pool.memset(state, 0.0)
                    pool.memset(rhs, 0.0)
                    pool.memset(sa, 0.0)
            pe0, act0, dve0 = core.pe_done.at, core.act_done.at, core.dve_done.at
            v_tok, b_tok, k_tok = 0, 1, 2
            with nc.Block() as block:
                @block.tensor
                def _(pe):
                    for c in range(CHUNKS):
                        half, base = c // 2, CHUNK * (c % 2)
                        at = slice(base, base + CHUNK)
                        if c:
                            pe.wait_ge(core.dve_done.sem, dve0 + 2 * c)
                        for tile in range(RWKV_TILES):
                            pe.matmul(b_rhs[at, tile * P:(tile + 1) * P], ar[:, tile, half, 0, at], state[:, tile, :],
                                      start=True, stop=False, skip_group_check=True)
                            for hp in range(2):
                                cols = slice(tile * P + 64 * hp, tile * P + 64 * hp + 64)
                                last = pe.matmul(b_rhs[at, cols], quad[:, combo_of[hp, tile, half], 2, at],
                                                 toks[:, v_tok, half, cols], start=False, stop=hp == 1,
                                                 skip_group_check=True)
                        core.pe_done.inc(last)
                        pe.wait_ge(core.act_done.sem, act0 + 3 * c + 1)
                        for tile in range(RWKV_TILES):
                            for hp in range(2):
                                cols = slice(tile * P + 64 * hp, tile * P + 64 * hp + 64)
                                last = pe.matmul(b_sa[at, cols], tu[:, combo_of[hp, tile, half], 1, at], rhs[:, cols],
                                                 start=True, stop=True)
                        core.pe_done.inc(last)
                        pe.wait_ge(core.act_done.sem, act0 + 3 * c + 2)
                        for tile in range(RWKV_TILES):
                            cols = slice(tile * P, (tile + 1) * P)
                            pe.matmul(b_state[:, cols], toks[at, b_tok, half, cols], sa[at, cols],
                                      start=True, stop=False)
                            last = pe.matmul(b_state[:, cols], toks[at, k_tok, half, cols],
                                             toks[at, v_tok, half, cols], start=False, stop=True)
                        core.pe_done.inc(last)
                        for tile in range(RWKV_TILES):
                            to = slice(tile * CHUNK, (tile + 1) * CHUNK)
                            pe.matmul(b_out[:, to], state[:, tile, :], ar[:, tile, half, 1, at],
                                      start=True, stop=False, skip_group_check=True)
                            for hp in range(2):
                                cols = slice(tile * P + 64 * hp, tile * P + 64 * hp + 64)
                                head = slice(64 * hp, 64 * hp + 64)
                                n = combo_of[hp, tile, half]
                                pe.matmul(b_out[head, to], sa[:, cols], quad[:, n, 1, at],
                                          start=False, stop=False, skip_group_check=True)
                                last = pe.matmul(b_out[head, to], toks[:, v_tok, half, cols], quad[:, n, 3, at],
                                                 start=False, stop=True, skip_group_check=True)
                        core.pe_done.inc(last)

                @block.scalar
                def _(act):
                    for c in range(CHUNKS):
                        at = slice(CHUNK * (c % 2), CHUNK * (c % 2) + CHUNK)
                        act.wait_ge(core.pe_done.sem, pe0 + 4 * c + 1)
                        core.act_done.inc(act.copy(rhs[at, :], b_rhs[at, :]))
                        act.wait_ge(core.pe_done.sem, pe0 + 4 * c + 2)
                        core.act_done.inc(act.copy(sa[at, :], b_sa[at, :]))
                        act.wait_ge(core.pe_done.sem, pe0 + 4 * c + 4)
                        core.act_done.inc(act.copy(out[:, 0:4, c * CHUNK:(c + 1) * CHUNK],
                                                   b_out[:, 0:256].rearrange("p (a j) -> p a j", a=4)))

                @block.vector
                def _(dve):
                    for c in range(CHUNKS):
                        dve.wait_ge(core.pe_done.sem, pe0 + 4 * c + 3)
                        link = Link(dve, core.dve_done)
                        link(dve.tensor_tensor(grown, b_state[:, :].rearrange("p (a j) -> p a j", a=4), state, ALU.add))
                        dve.wait_ge(core.pe_done.sem, pe0 + 4 * c + 4)
                        core.dve_done.inc(dve.tensor_tensor(state, grown, end_decay[:, c], ALU.mult))
            with nc.Block() as block:
                @block.sync
                def _(sp):
                    core.stored.inc(sp.dma_start(state_out, state), 16)
                    sp.wait_ge(core.stored.sem, core.stored.at)


def rwkv_sample(core, mask, w, out, state_in, state_out):
    nc = core.nc
    wide = [P, RWKV_TILES, DEC, 64]
    with ExitStack() as ctx:
        state = core.sb(ctx, "state", wide)
        new = core.sb(ctx, "new", wide)
        work = core.sb(ctx, "work", wide)
        values = core.sb(ctx, "values", wide)
        decay = core.sb(ctx, "decay", [P, RWKV_TILES, DEC])
        reads = core.banks(ctx, "reads", 4)
        spread = core.banks(ctx, "spread", 4)
        each = lambda a: a.unsqueeze(3).broadcast_to(tuple(wide))
        sample = lambda name: each(w[name][:, :, SEQ:T])
        mixed = lambda i: each(w["m"][:, i:i + 4, SEQ:T])
        eye = mask[:, MASK_EYE64, 0:64].unsqueeze(1).unsqueeze(1).broadcast_to(tuple(wide))
        got = lambda bank: bank[:, :].rearrange("p (b v) -> p b v", b=DEC)
        flat = lambda a, tile: a[:, tile].rearrange("p b v -> p (b v)")
        with nc.Block() as block:
            @block.sync
            def _(sp):
                core.load(sp, state, state_in)

            @block.scalar
            def _(act):
                act.activation(decay, w["logw"][:, :, SEQ:T], ACT.Exp)

            @block.vector
            def _(dve):
                dve.tensor_tensor(values, eye, mixed(8), ALU.mult)
                core.wait_loads(dve)
                dve.tensor_tensor(work, state, sample("kk"), ALU.mult)
        with nc.Block() as block:
            @block.tensor
            def _(pe):
                for tile in range(RWKV_TILES):
                    pe.matmul(reads[tile][:, :], core.block_ones, flat(work, tile), start=True, stop=True)
                    pe.matmul(spread[tile][:, :], core.block_ones, flat(values, tile), start=True, stop=True)

            @block.vector
            def _(dve):
                dve.tensor_tensor(new, state, each(decay), ALU.mult)
        with nc.Block() as block:
            @block.vector
            def _(dve):
                link = Link(dve, core.dve_done)
                for tile in range(RWKV_TILES):
                    dve.tensor_tensor(work[:, tile], got(reads[tile]), sample("b")[:, tile], ALU.mult)
                    last = dve.tensor_tensor(values[:, tile], got(spread[tile]), sample("key")[:, tile], ALU.mult)
                link(last)
                link(dve.tensor_tensor(new, new, work, ALU.subtract))
                link(dve.tensor_tensor(new, new, values, ALU.add))
                dve.tensor_tensor(work, new, mixed(0), ALU.mult)
        with nc.Block() as block:
            @block.tensor
            def _(pe):
                for tile in range(RWKV_TILES):
                    pe.matmul(reads[tile][:, :], core.block_ones, flat(work, tile), start=True, stop=True)

            @block.sync
            def _(sp):
                core.stored.inc(sp.dma_start(state_out, new), 16)
                sp.wait_ge(core.stored.sem, core.stored.at)
        with nc.Block() as block:
            @block.vector
            def _(dve):
                link = Link(dve, core.dve_done)
                for tile in range(RWKV_TILES):
                    last = dve.tensor_tensor(values[:, tile], got(reads[tile]), eye[:, tile], ALU.mult)
                link(last)
                dve.tensor_reduce(out[:, 0:4, SEQ:T], values, AX_X, ALU.add)


def rwkv_output(core, par, w, out):
    nc = core.nc
    o = out[:, 0:4, :]
    with ExitStack() as ctx:
        work = core.sb(ctx, "work", [P, RWKV_TILES, T])
        rstd = core.sb(ctx, "rstd", [P, RWKV_TILES, T])
        banks = core.banks(ctx, "norm", 4)
        sum_features(core, core.block_ones, o, banks, RWKV_TILES)
        with nc.Block() as block:
            @block.vector
            def _(dve):
                link = Link(dve, core.dve_done)
                for i in range(RWKV_TILES):
                    last = dve.scalar_tensor_tensor(out[:, i, :], banks[i][:, 0:T], -1.0 / 64, out[:, i, :],
                                                    ALU.mult, ALU.add)
                link(last)
                dve.tensor_tensor(work, o, o, ALU.mult)
        sum_features(core, core.block_ones, work, banks, RWKV_TILES)
        inverse_root(core, banks, RWKV_TILES, rstd, 1.0 / 64, GN_EPS)
        with nc.Block() as block:
            @block.vector
            def _(dve):
                link = Link(dve, core.dve_done)
                link(dve.tensor_tensor(o, o, rstd, ALU.mult))
                for i in range(RWKV_TILES):
                    last = dve.tensor_scalar(out[:, i, :], out[:, i, :], par("gn_w", i), par("gn_b", i),
                                             ALU.mult, ALU.add)
                link(last)
                link(dve.tensor_tensor(o, o, w["bonus"], ALU.add))
                dve.tensor_tensor(o, o, w["gate"], ALU.mult)


HGRN_TILES = 4
LEVELS = 7
SMALLEST_LOG = 1.0842021724855044e-19


def hgrn_prompt(core, mask, values, q, key, logs, out, state_out):
    nc = core.nc
    flat = lambda a: a.rearrange("p t n -> p (t n)")
    with ExitStack() as ctx:
        att = core.sb(ctx, "att", [P, HALVES, HGRN_TILES, P])
        with ExitStack() as local:
            gap = core.sb(local, "gap", [P, 2, HGRN_TILES * SEQ])
            left = core.sb(local, "left", [P, 2, HGRN_TILES, SEQ])
            right = core.sb(local, "right", [P, 2, HGRN_TILES, SEQ])
            masked = core.sb(local, "masked", [P, 2, HALVES, HGRN_TILES, P])
            banks = core.banks(local, "level", 4)
            with nc.Block() as block:
                @block.gpsimd
                def _(pool):
                    pool.memset(left, 0.0)
                    pool.memset(right, 0.0)
            gap0, exp0, scaled0, mult0 = core.dve_done.at, core.act_done.at, core.tile_evicted.at, core.pe_done.at
            masked0, added0 = core.tile_multiplied.at, core.pool_done.at
            with nc.Block() as block:
                @block.vector
                def _(dve):
                    def gaps(level):
                        w = 1 << level
                        if level >= 2:
                            dve.wait_ge(core.tile_evicted.sem, scaled0 + level - 1)
                        g = flat(logs).rearrange("p (n j) -> p n j", j=2 * w)
                        to = gap[:, level % 2, :].rearrange("p (n j) -> p n j", j=2 * w)
                        middle = g[:, :, w - 1:w].broadcast_to((P, HGRN_TILES * SEQ // (2 * w), w))
                        dve.tensor_tensor(to[:, :, 0:w], middle, g[:, :, 0:w], ALU.subtract)
                        core.dve_done.inc(dve.tensor_tensor(to[:, :, w:2 * w], g[:, :, w:2 * w], middle, ALU.subtract))

                    def scale(level):
                        w, slot = 1 << level, level % 2
                        dve.wait_ge(core.act_done.sem, exp0 + level + 1)
                        if level >= 2:
                            dve.wait_ge(core.pe_done.sem, mult0 + 1 + level - 1)
                        cut = lambda a: a.rearrange("p (n j) -> p n j", j=2 * w)
                        e = cut(gap[:, slot, :])
                        dve.tensor_tensor(cut(flat(left[:, slot]))[:, :, 0:w], cut(flat(key))[:, :, 0:w],
                                          e[:, :, 0:w], ALU.mult)
                        core.tile_evicted.inc(dve.tensor_tensor(
                            cut(flat(right[:, slot]))[:, :, w:2 * w], cut(flat(q))[:, :, w:2 * w],
                            e[:, :, w:2 * w], ALU.mult))

                    def cover(level, to, which):
                        slot = (level + 1) % 2
                        dve.wait_ge(core.pe_done.sem, mult0 + level + 2)
                        if level >= 2:
                            dve.wait_ge(core.pool_done.sem, added0 + level - 1)
                        for half in range(HALVES):
                            last = dve.tensor_tensor(to[:, half], banks[2 * slot + half][:, :].rearrange(
                                "p (a j) -> p a j", a=4), which.broadcast_to((P, 4, P)), ALU.mult)
                        core.tile_multiplied.inc(last)

                    gaps(0)
                    cover(-1, att, core.ident.unsqueeze(1))
                    gaps(1)
                    for level in range(LEVELS):
                        scale(level)
                        if level + 2 < LEVELS:
                            gaps(level + 2)
                        if level:
                            cover(level - 1, masked[:, (level - 1) % 2],
                                  mask[:, MASK_LEVEL + level - 1:MASK_LEVEL + level, :])
                    cover(LEVELS - 1, masked[:, (LEVELS - 1) % 2], mask[:, MASK_LEVEL + LEVELS - 1:MASK_LEVEL + LEVELS, :])

                @block.scalar
                def _(act):
                    for level in range(LEVELS):
                        act.wait_ge(core.dve_done.sem, gap0 + level + 1)
                        core.act_done.inc(act.activation(gap[:, level % 2, :], gap[:, level % 2, :], ACT.Exp))

                @block.tensor
                def _(pe):
                    for n in range(LEVELS + 1):
                        if n:
                            pe.wait_ge(core.tile_evicted.sem, scaled0 + n)
                        if n >= 2:
                            pe.wait_ge(core.tile_multiplied.sem, masked0 + n - 1)
                        for half in range(HALVES):
                            for tile in range(HGRN_TILES):
                                cols = slice(half * P, (half + 1) * P)
                                a, b = (key, q) if n == 0 else (left[:, (n - 1) % 2], right[:, (n - 1) % 2])
                                last = pe.matmul(banks[2 * (n % 2) + half][:, tile * P:(tile + 1) * P],
                                                 a[:, tile, cols], b[:, tile, cols], start=True, stop=True)
                        core.pe_done.inc(last)

                @block.gpsimd
                def _(pool):
                    for level in range(LEVELS):
                        pool.wait_ge(core.tile_multiplied.sem, masked0 + level + 2)
                        if level:
                            pool.wait_ge(core.pool_done.sem, added0 + level)
                        core.pool_done.inc(pool.tensor_tensor(att, att, masked[:, level % 2], ALU.add))
        decay = core.sb(ctx, "decay", [P, HGRN_TILES, SEQ])
        late = core.sb(ctx, "late", [P, HGRN_TILES, SEQ])
        toks = core.sb(ctx, "toks", [P, 2, HALVES, 512])
        state = core.sb(ctx, "state", [P, HGRN_TILES, P])
        halves = lambda a: a.rearrange("p t (h j) -> p (t h) j", h=HALVES)
        with nc.Block() as block:
            @block.vector
            def _(dve):
                g = halves(logs)
                dve.tensor_tensor(halves(late), g[:, :, P - 1:P].broadcast_to((P, 8, P)), g, ALU.subtract)
        with nc.Block() as block:
            @block.scalar
            def _(act):
                act.activation(decay, logs, ACT.Exp)
                act.activation(late, late, ACT.Exp)
        with nc.Block() as block:
            @block.vector
            def _(dve):
                dve.tensor_tensor(late, late, key, ALU.mult)
                dve.tensor_tensor(q, q, decay, ALU.mult)
        turned = core.banks(ctx, "turned", 4)
        done0 = core.pe_done.at
        with nc.Block() as block:
            @block.tensor
            def _(pe):
                for kind, src in enumerate((values, late)):
                    for half in range(HALVES):
                        for tile in range(HGRN_TILES):
                            last = pe.transpose(turned[kind * 2 + half][:, tile * P:(tile + 1) * P],
                                                src[:, tile, half * P:(half + 1) * P], core.ident)
                        core.pe_done.inc(last)

            @block.scalar
            def _(act):
                for n in range(4):
                    act.wait_ge(core.pe_done.sem, done0 + n + 1)
                    act.copy(toks[:, n // 2, n % 2, :], turned[n][:, :])
        b_out = core.banks(ctx, "outputs", 2)
        b_state = core.banks(ctx, "states", 2)
        done0, first_state = core.pe_done.at, core.dve_done.at
        with nc.Block() as block:
            @block.tensor
            def _(pe):
                for half in range(HALVES):
                    for tile in range(HGRN_TILES):
                        cols = slice(tile * P, (tile + 1) * P)
                        last = pe.matmul(b_state[half][:, cols], toks[:, 1, half, cols], toks[:, 0, half, cols],
                                         start=True, stop=True)
                    core.pe_done.inc(last)
                for half in range(HALVES):
                    if half:
                        pe.wait_ge(core.dve_done.sem, first_state + 1)
                    for tile in range(HGRN_TILES):
                        cols = slice(tile * P, (tile + 1) * P)
                        last = pe.matmul(b_out[half][:, cols], toks[:, 0, half, cols], att[:, half, tile, :],
                                         start=True, stop=half == 0)
                        if half:
                            last = pe.matmul(b_out[half][:, cols], state[:, tile, :], q[:, tile, half * P:(half + 1) * P],
                                             start=False, stop=True)
                    core.pe_done.inc(last)

            @block.vector
            def _(dve):
                dve.wait_ge(core.pe_done.sem, done0 + 1)
                core.dve_done.inc(dve.tensor_copy(state, b_state[0][:, :].rearrange("p (a j) -> p a j", a=4)))
                dve.wait_ge(core.pe_done.sem, done0 + 4)
                for tile in range(HGRN_TILES):
                    dve.scalar_tensor_tensor(state[:, tile, :], state[:, tile, :], decay[:, tile, SEQ - 1:SEQ],
                                             b_state[1][:, tile * P:(tile + 1) * P], ALU.mult, ALU.add)

            @block.scalar
            def _(act):
                for half in range(HALVES):
                    act.wait_ge(core.pe_done.sem, done0 + 3 + half)
                    act.copy(out[:, 4:8, half * P:(half + 1) * P],
                             b_out[half][:, :].rearrange("p (a j) -> p a j", a=4))
        with nc.Block() as block:
            @block.sync
            def _(sp):
                core.stored.inc(sp.dma_start(state_out, state), 16)
                sp.wait_ge(core.stored.sem, core.stored.at)


def hgrn_sample(core, values, q, key, forget, out, state_in, state_out):
    nc = core.nc
    wide = [P, HGRN_TILES, DEC, P]
    with ExitStack() as ctx:
        state = core.sb(ctx, "state", wide)
        work = core.sb(ctx, "work", wide)
        each = lambda a: a.unsqueeze(3).broadcast_to(tuple(wide))
        with ExitStack() as ps:
            banks = core.banks(ps, "spread", 8)
            done0 = core.pe_done.at
            with nc.Block() as block:
                @block.sync
                def _(sp):
                    core.load(sp, state, state_in)
                @block.tensor
                def _(pe):
                    for n in range(8):
                        for s in range(4 * n, 4 * n + 4):
                            last = pe.matmul(banks[n][:, (s % 4) * P:(s % 4 + 1) * P],
                                             values[:, s // DEC, s % DEC:s % DEC + 1].broadcast_to((P, P)),
                                             core.ident, start=True, stop=True)
                        core.pe_done.inc(last)

                @block.vector
                def _(dve):
                    core.wait_loads(dve)
                    link = Link(dve, core.dve_done)
                    link(dve.tensor_tensor(state, state, each(forget), ALU.mult))
                    for n in range(8):
                        dve.wait_ge(core.pe_done.sem, done0 + n + 1)
                        tile, b = n // 2, 4 * (n % 2)
                        last = dve.tensor_tensor(work[:, tile, b:b + 4, :], banks[n][:, :].rearrange(
                            "p (b v) -> p b v", b=4), each(key)[:, tile, b:b + 4, :], ALU.mult)
                    link(last)
                    dve.tensor_tensor(state, state, work, ALU.add)
        (bank,) = core.banks(ctx, "reads", 1)
        with nc.Block() as block:
            @block.tensor
            def _(pe):
                for s in range(HGRN_TILES * DEC):
                    pe.matmul(bank[:, s:s + 1], state[:, s // DEC, s % DEC, :], q[:, s // DEC, s % DEC:s % DEC + 1],
                              start=True, stop=True)

            @block.sync
            def _(sp):
                core.stored.inc(sp.dma_start(state_out, state), 16)
                sp.wait_ge(core.stored.sem, core.stored.at)
        with nc.Block() as block:
            @block.vector
            def _(dve):
                dve.tensor_copy(out[:, 4:8, SEQ:T], bank[:, 0:HGRN_TILES * DEC].rearrange("p (a b) -> p a b", b=DEC))


def hgrn(core, par, mask, p, out, state_in, prompt_state, sample_state):
    nc = core.nc
    whole = [P, HGRN_TILES, T]
    prompt = [P, HGRN_TILES, SEQ]
    with ExitStack() as ctx:
        gate = core.sb(ctx, "out_gate", whole)
        q = core.sb(ctx, "q", prompt)
        key = core.sb(ctx, "key", prompt)
        logs = core.sb(ctx, "logs", prompt)
        small = core.sb(ctx, "small", [P, 3, HGRN_TILES, DEC])
        with ExitStack() as local:
            forget = core.sb(local, "forget", whole)
            logf = core.sb(local, "logf", prompt)
            bound = core.sb(local, "bound", [P, 4, HGRN_TILES])
            with nc.Block() as block:
                @block.scalar
                def _(act):
                    act.activation(gate, p[:, 26:30, :], ACT.Silu)
                    act.activation(q, p[:, 14:18, 0:SEQ], ACT.Silu)
                    act.activation(small[:, 0], p[:, 14:18, SEQ:T], ACT.Silu)
                    act.activation(forget, p[:, 18:22, :], ACT.Sigmoid)

                @block.vector
                def _(dve):
                    dve.tensor_tensor(bound[:, 0], par("bound"), par("bound"), ALU.subtract)
            with nc.Block() as block:
                @block.scalar
                def _(act):
                    act.activation(bound[:, 1], bound[:, 0], ACT.Exp)
            with nc.Block() as block:
                @block.vector
                def _(dve):
                    link = Link(dve, core.dve_done)
                    link(dve.reciprocal(bound[:, 0], bound[:, 1]))
                    link(dve.tensor_tensor(bound[:, 0], bound[:, 0], bound[:, 1], ALU.mult))
                    link(dve.tensor_tensor(bound[:, 2], bound[:, 0], bound[:, 0], ALU.subtract))
                    link(dve.tensor_scalar(bound[:, 3], bound[:, 2], -1.0, 1.0, ALU.mult, ALU.add))
                    for i in range(HGRN_TILES):
                        last = dve.tensor_scalar(forget[:, i, :], forget[:, i, :], bound[:, 3, i:i + 1],
                                                 bound[:, 2, i:i + 1], ALU.mult, ALU.add)
                    link(last)
                    dve.tensor_scalar(key, forget[:, :, 0:SEQ], -1.0, 1.0, ALU.mult, ALU.add)
                    dve.tensor_scalar(small[:, 1], forget[:, :, SEQ:T], -1.0, 1.0, ALU.mult, ALU.add)
                    dve.tensor_copy(small[:, 2], forget[:, :, SEQ:T])
                    dve.tensor_scalar(logf, forget[:, :, 0:SEQ], SMALLEST_LOG, None, ALU.max)
            with nc.Block() as block:
                @block.scalar
                def _(act):
                    act.activation(logf, logf, ACT.Ln)
            with nc.Block() as block:
                @block.vector
                def _(dve):
                    for i in range(HGRN_TILES):
                        dve.tensor_tensor_scan(logs[:, i, :], mask[:, MASK_SCAN128:MASK_SCAN128 + 2, :].rearrange(
                            "p a b -> p (a b)"), logf[:, i, :], 0.0, ALU.mult, ALU.add)
        hgrn_sample(core, p[:, 22:26, SEQ:T], small[:, 0], small[:, 1], small[:, 2], out, state_in, sample_state)
        hgrn_prompt(core, mask, p[:, 22:26, 0:SEQ], q, key, logs, out, prompt_state)
        work = core.sb(ctx, "work", whole)
        rstd = core.sb(ctx, "rstd", whole)
        banks = core.banks(ctx, "norm", 4)
        with nc.Block() as block:
            @block.scalar
            def _(act):
                act.activation(work, out[:, 4:8, :], ACT.Square)
        sum_features(core, core.ones, work, banks, HGRN_TILES)
        inverse_root(core, banks, HGRN_TILES, rstd, 1.0 / P, RMS_EPS)
        with nc.Block() as block:
            @block.vector
            def _(dve):
                link = Link(dve, core.dve_done)
                for i in range(HGRN_TILES):
                    last = dve.scalar_tensor_tensor(out[:, 4 + i, :], out[:, 4 + i, :], par("hgrn_norm", 0),
                                                    rstd[:, i, :], ALU.mult, ALU.mult)
                link(last)
                dve.tensor_tensor(out[:, 4:8, :], out[:, 4:8, :], gate, ALU.mult)


def mixer_ab(core, x, d, mask):
    nc = core.nc
    with ExitStack() as ctx:
        params = core.sb(ctx, "params", [P, AB_PARAMS])

        def par(name, i=None):
            at = AB_PARAM[name]
            return params[:, at] if i is None else params[:, at.start + i:at.start + i + 1]

        p = core.sb(ctx, "p", [P, AB_TILES, T])
        out = core.sb(ctx, "mixer_out", [P, KC, T])
        with nc.Block() as block:
            @block.sync
            def _(sp):
                core.load(sp, params, d["ab_params"])
                core.wait_loads(sp)
        with ExitStack() as local:
            h = core.sb(local, "mix_in", [P, KC, T])
            rms_norm(core, x, par("norm"), h)
            project(core, d["ab_w_in"], AB_TILES, KC, h, p)
        with nc.Block() as block:
            @block.sync
            def _(sp):
                core.stored.inc(sp.dma_start(d["last_shift"], p[:, 0:SHIFT_TILES, SEQ - 1:T]), 16)
                sp.wait_ge(core.stored.sem, core.stored.at)
        with ExitStack() as local:
            w = {}
            rwkv_inputs(core, local, p, par, mask, d["shift_in"], d["lora_up"], d["gate_up"], w)
            rwkv_sample(core, mask, w, out, d["rwkv_in"], d["rwkv_sample"])
            rwkv_prompt(core, mask, w, out, d["rwkv_prompt"])
            rwkv_output(core, par, w, out)
        hgrn(core, par, mask, p, out, d["hgrn_in"], d["hgrn_prompt"], d["hgrn_sample"])
        project(core, d["ab_w_out"], KC, KC, out, x, residual=True)


HEADS = 32
GROUPS = 4
INNER_TILES = 16
CONV_TILES = 24
SSM_TILES = INNER_TILES + CONV_TILES
INNER = INNER_TILES * P
TAPS = 4
SSM_PARAM = {}
_at = 0
for _name, _n in (("norm", 8), ("conv_w", TAPS * CONV_TILES), ("conv_b", CONV_TILES), ("out_norm", INNER_TILES),
                  ("skip", INNER_TILES)):
    SSM_PARAM[_name] = slice(_at, _at + _n)
    _at += _n
SSM_PARAMS = _at
SSM_OUT = {"conv_prompt": (P, CONV_TILES, TAPS - 1), "conv_sample": (P, CONV_TILES, TAPS - 1, DEC),
           "ssm_prompt": (P, INNER), "ssm_sample": (P, DEC, INNER)}


def ssm_steps(core, h, w_dt, heads_in, mask, dt, log_a, log_sum):
    nc = core.nc
    row = [HEADS, T]
    with ExitStack() as ctx:
        weights = core.sb(ctx, "w_dt", [P, KC, HEADS])
        heads = core.sb(ctx, "heads", [HEADS, 2])
        rate = core.sb(ctx, "rate", [HEADS, 1])
        z = core.sb(ctx, "z", row)
        u = core.sb(ctx, "u", row)
        r = core.sb(ctx, "r", row)
        square = core.sb(ctx, "square", row)
        series = core.sb(ctx, "series", row)
        (bank,) = core.banks(ctx, "dt", 1)
        with nc.Block() as block:
            @block.sync
            def _(sp):
                core.load(sp, weights, w_dt)
                core.load(sp, heads, heads_in)

            @block.tensor
            def _(pe):
                core.wait_loads(pe)
                for k in range(KC):
                    pe.matmul(bank[0:HEADS, 0:T], weights[:, k, :], h[:, k, :], start=k == 0, stop=k == KC - 1)
        with nc.Block() as block:
            @block.vector
            def _(dve):
                link = Link(dve, core.dve_done)
                link(dve.tensor_scalar(z, bank[0:HEADS, 0:T], heads[:, 0:1], None, ALU.add))
                link(dve.tensor_scalar(r, z, -1.0, None, ALU.mult))
                dve.tensor_tensor(u, z, r, ALU.max)

            @block.scalar
            def _(act):
                act.activation(rate, heads[:, 1:2], ACT.Exp)
        with nc.Block() as block:
            @block.scalar
            def _(act):
                act.activation(u, u, ACT.Exp, scale=-1.0)
        with nc.Block() as block:
            @block.vector
            def _(dve):
                link = Link(dve, core.dve_done)
                link(dve.tensor_scalar(r, u, 2.0, None, ALU.add))
                link(dve.reciprocal(r, r))
                link(dve.tensor_tensor(r, r, u, ALU.mult))
                link(dve.tensor_tensor(square, r, r, ALU.mult))
                link(dve.tensor_scalar(series, square, 1.0 / 17, None, ALU.mult))
                for n in range(15, 1, -2):
                    link(dve.scalar_tensor_tensor(series, series, 1.0 / n, square, ALU.add, ALU.mult))
                link(dve.scalar_tensor_tensor(series, series, 1.0, r, ALU.add, ALU.mult))
                link(dve.tensor_scalar(z, z, 0.0, None, ALU.max))
                link(dve.scalar_tensor_tensor(dt, series, 2.0, z, ALU.mult, ALU.add))
                link(dve.tensor_scalar(log_a, dt, rate, -1.0, ALU.mult, ALU.mult))
                dve.tensor_tensor_scan(log_sum, mask[0:HEADS, MASK_SCAN128:MASK_SCAN128 + 2, :].rearrange(
                    "p a b -> p (a b)"), log_a[:, 0:SEQ], 0.0, ALU.mult, ALU.add)


def ssm_conv(core, par, p, c, conv_in, conv_prompt, conv_sample):
    nc = core.nc
    with ExitStack() as ctx:
        rows = core.sb(ctx, "conv_rows", [P, CONV_TILES, TAPS - 1, DEC])
        term = core.sb(ctx, "term", [P, TAPS - 1, CONV_TILES, DEC])
        x = p[:, INNER_TILES:SSM_TILES, :]
        tap = lambda j, i: par("conv_w", j * CONV_TILES + i)
        with nc.Block() as block:
            @block.sync
            def _(sp):
                core.load(sp, rows, conv_in)
                core.stored.inc(sp.dma_start(conv_prompt, x[:, :, SEQ - 3:SEQ]), 16)
                core.stored.inc(sp.dma_start(conv_sample[:, :, 2, :], x[:, :, SEQ:T]), 16)
                core.wait_loads(sp)
                core.stored.inc(sp.dma_start(conv_sample[:, :, 0:2, :], rows[:, :, 1:3, :]), 16)
                sp.wait_ge(core.stored.sem, core.stored.at)

            @block.scalar
            def _(act):
                for i in range(CONV_TILES):
                    act.activation(c[:, i, :], x[:, i, :], ACT.Identity, bias=par("conv_b", i), scale=tap(3, i))
        with nc.Block() as block:
            @block.vector
            def _(dve):
                link = Link(dve, core.dve_done)
                for back in range(1, TAPS):
                    for i in range(CONV_TILES):
                        last = dve.scalar_tensor_tensor(c[:, i, back:SEQ], x[:, i, 0:SEQ - back], tap(3 - back, i),
                                                        c[:, i, back:SEQ], ALU.mult, ALU.add)
                    link(last)

            @block.gpsimd
            def _(pool):
                link = Link(pool, core.pool_done)
                for j in range(TAPS - 1):
                    w = par("conv_w")[:, j * CONV_TILES:(j + 1) * CONV_TILES].unsqueeze(2)
                    link(pool.tensor_tensor(term[:, j], rows[:, :, j, :], w.broadcast_to((P, CONV_TILES, DEC)),
                                            ALU.mult))
                for j in range(TAPS - 1):
                    link(pool.tensor_tensor(c[:, :, SEQ:T], c[:, :, SEQ:T], term[:, j], ALU.add))
        with nc.Block() as block:
            @block.scalar
            def _(act):
                act.activation(c, c, ACT.Silu)


def ssm_sample(core, c, xdt, log_a, y, state_in, state_out):
    nc = core.nc
    slots = 3
    with ExitStack() as ctx:
        ring = core.sb(ctx, "states", [P, slots, INNER])
        a = core.sb(ctx, "a", [HEADS, DEC])
        diagonal = core.sb(ctx, "diagonal", [HEADS, DEC, HEADS])
        a_all = core.sb(ctx, "a_all", [P, DEC, HEADS])
        spread = core.banks(ctx, "spread", 4)
        reads, decays = core.banks(ctx, "reads", 2)
        with nc.Block() as block:
            @block.scalar
            def _(act):
                act.activation(a, log_a[:, SEQ:T], ACT.Exp)
        with nc.Block() as block:
            @block.vector
            def _(dve):
                dve.tensor_tensor(diagonal, a.unsqueeze(2).broadcast_to((HEADS, DEC, HEADS)),
                                  core.ident[0:HEADS, 0:HEADS].unsqueeze(1).broadcast_to((HEADS, DEC, HEADS)), ALU.mult)
        with nc.Block() as block:
            @block.tensor
            def _(pe):
                pe.matmul(decays[:, 0:DEC * HEADS], core.ones[0:HEADS, :], diagonal.rearrange("p b h -> p (b h)"),
                          start=True, stop=True)
        with nc.Block() as block:
            @block.scalar
            def _(act):
                act.copy(a_all, decays[:, 0:DEC * HEADS].rearrange("p (b h) -> p b h", b=DEC))
        loaded0 = [k.at for k in core.tile_loaded[0:slots]]
        stored0 = [k.at for k in core.tile_loaded[4:4 + slots]]
        decayed0, spread0, updated0, read0 = (core.pool_done.at, core.pe_done.at, core.dve_done.at,
                                              core.tile_multiplied.at)
        with nc.Block() as block:
            @block.sync
            def _(sp):
                def load(b):
                    if b >= slots:
                        sp.wait_ge(core.tile_loaded[4 + b % slots].sem, stored0[b % slots] + 16 * (b // slots))
                        sp.wait_ge(core.tile_multiplied.sem, read0 + b - slots + 1)
                    core.tile_loaded[b % slots].inc(sp.dma_start(ring[:, b % slots, :], state_in[:, b, :]), 16)

                for b in range(slots - 1):
                    load(b)
                for b in range(DEC):
                    if b + slots - 1 < DEC:
                        load(b + slots - 1)
                    sp.wait_ge(core.dve_done.sem, updated0 + b + 1)
                    core.tile_loaded[4 + b % slots].inc(sp.dma_start(state_out[:, b, :], ring[:, b % slots, :]), 16)
                for k in range(slots):
                    sp.wait_ge(core.tile_loaded[4 + k].sem, core.tile_loaded[4 + k].at)

            @block.gpsimd
            def _(pool):
                for b in range(DEC):
                    pool.wait_ge(core.tile_loaded[b % slots].sem, loaded0[b % slots] + 16 * (b // slots + 1))
                    s = ring[:, b % slots, :].rearrange("p (h v) -> p h v", h=HEADS)
                    core.pool_done.inc(pool.tensor_tensor(
                        s, s, a_all[:, b, :].unsqueeze(2).broadcast_to((P, HEADS, 64)), ALU.mult))

            @block.tensor
            def _(pe):
                def rows(b):
                    for g in range(GROUPS):
                        if b:
                            pe.wait_ge(core.dve_done.sem, updated0 + b)
                        for tile in range(4 * g, 4 * g + 4):
                            last = pe.matmul(spread[g][:, (tile % 4) * P:(tile % 4 + 1) * P],
                                             xdt[:, tile, SEQ + b:SEQ + b + 1].broadcast_to((P, P)), core.ident,
                                             start=True, stop=True)
                    core.pe_done.inc(last)

                def outputs(b):
                    pe.wait_ge(core.dve_done.sem, updated0 + b + 1)
                    for tile in range(INNER_TILES):
                        last = pe.matmul(reads[:, tile * DEC + b:tile * DEC + b + 1],
                                         ring[:, b % slots, tile * P:(tile + 1) * P],
                                         c[:, 20 + tile // 4, SEQ + b:SEQ + b + 1], start=True, stop=True)
                    core.tile_multiplied.inc(last)

                rows(0)
                for b in range(DEC):
                    if b + 1 < DEC:
                        rows(b + 1)
                    outputs(b)

            @block.vector
            def _(dve):
                for b in range(DEC):
                    dve.wait_ge(core.pool_done.sem, decayed0 + b + 1)
                    dve.wait_ge(core.pe_done.sem, spread0 + b + 1)
                    for g in range(GROUPS):
                        s = ring[:, b % slots, g * 512:(g + 1) * 512]
                        last = dve.scalar_tensor_tensor(s, spread[g][:, :], c[:, 16 + g, SEQ + b:SEQ + b + 1], s,
                                                        ALU.mult, ALU.add)
                    core.dve_done.inc(last)
        with nc.Block() as block:
            @block.vector
            def _(dve):
                dve.tensor_copy(y[:, :, SEQ:T], reads[:, 0:INNER_TILES * DEC].rearrange("p (a b) -> p a b", b=DEC))


def ssm_prompt(core, mask, expand, c, xdt, log_sum, y, state_out):
    nc = core.nc
    with ExitStack() as ctx:
        x_tok = core.sb(ctx, "x_tok", [P, HALVES, INNER])
        x_late = core.sb(ctx, "x_late", [P, HALVES, INNER])
        b_tok = core.sb(ctx, "b_tok", [P, HALVES, 512])
        sum_tok = core.sb(ctx, "sum_tok", [P, HALVES, HEADS])
        late = core.sb(ctx, "late", [P, HALVES, HEADS])
        end = core.sb(ctx, "end", [P, HALVES, HEADS])
        diagonal = core.sb(ctx, "diagonal", [HEADS, HALVES, HEADS])
        inside = core.sb(ctx, "inside", [P, HALVES, GROUPS, P])
        grown = core.sb(ctx, "grown", [P, INNER_TILES, P])
        state = core.sb(ctx, "state", [P, INNER])
        halves = [slice(0, P), slice(P, 2 * P)]
        with ExitStack() as ps:
            banks = core.banks(ps, "turned", 4)
            sums, ends = core.banks(ps, "sums", 2)
            cb = core.banks(ps, "cb", 2)
            done0, out0 = core.pe_done.at, core.act_done.at
            jobs = [(x_tok, half, q, xdt, 4 * q) for half in range(HALVES) for q in range(4)]
            jobs += [(b_tok, half, 0, c, 16) for half in range(HALVES)]
            with nc.Block() as block:
                @block.tensor
                def _(pe):
                    for n, (dst, half, q, src, first) in enumerate(jobs):
                        if n >= 4:
                            pe.wait_ge(core.act_done.sem, out0 + n - 3)
                        for i in range(4):
                            last = pe.transpose(banks[n % 4][:, i * P:(i + 1) * P], src[:, first + i, halves[half]],
                                                core.ident)
                        core.pe_done.inc(last)
                    for half in range(HALVES):
                        pe.transpose(sums[:, half * HEADS:(half + 1) * HEADS], log_sum[:, halves[half]],
                                     core.ident[0:HEADS, 0:HEADS])
                        for g in range(GROUPS):
                            pe.matmul(cb[half][:, g * P:(g + 1) * P], c[:, 16 + g, halves[half]],
                                      c[:, 20 + g, halves[half]], start=True, stop=True)

                @block.scalar
                def _(act):
                    for n, (dst, half, q, src, first) in enumerate(jobs):
                        act.wait_ge(core.pe_done.sem, done0 + n + 1)
                        core.act_done.inc(act.copy(dst[:, half, q * 512:(q + 1) * 512], banks[n % 4][:, :]))

                @block.vector
                def _(dve):
                    for half in range(HALVES):
                        at = half * P + P - 1
                        dve.tensor_scalar(diagonal[:, half, :], core.ident[0:HEADS, 0:HEADS],
                                          log_sum[:, at:at + 1], None, ALU.mult)
            with nc.Block() as block:
                @block.tensor
                def _(pe):
                    pe.matmul(ends[:, 0:HALVES * HEADS], core.ones[0:HEADS, :],
                              diagonal.rearrange("p a h -> p (a h)"), start=True, stop=True)

                @block.vector
                def _(dve):
                    dve.tensor_copy(sum_tok, sums[:, 0:HALVES * HEADS].rearrange("p (a h) -> p a h", a=HALVES))
                    for half in range(HALVES):
                        dve.tensor_tensor(inside[:, half], cb[half][:, :].rearrange("p (g j) -> p g j", g=GROUPS),
                                          mask[:, MASK_CAUSAL:MASK_CAUSAL + 1, :].broadcast_to((P, GROUPS, P)),
                                          ALU.mult)
            with nc.Block() as block:
                @block.vector
                def _(dve):
                    dve.tensor_tensor(late, ends[:, 0:HALVES * HEADS].rearrange("p (a h) -> p a h", a=HALVES),
                                      sum_tok, ALU.subtract)
            with nc.Block() as block:
                @block.scalar
                def _(act):
                    act.activation(end, ends[:, 0:HALVES * HEADS].rearrange("p (a h) -> p a h", a=HALVES), ACT.Exp)
                    act.activation(late, late, ACT.Exp)
            with nc.Block() as block:
                @block.vector
                def _(dve):
                    for half in range(HALVES):
                        dve.tensor_tensor(x_late[:, half].rearrange("p (h v) -> p h v", h=HEADS),
                                          x_tok[:, half].rearrange("p (h v) -> p h v", h=HEADS),
                                          late[:, half].unsqueeze(2).broadcast_to((P, HEADS, 64)), ALU.mult)
        with ExitStack() as ps:
            adds = core.banks(ps, "adds", 4)
            grows = core.banks(ps, "grows", 4)
            with nc.Block() as block:
                @block.tensor
                def _(pe):
                    for g in range(GROUPS):
                        pe.matmul(adds[g][:, :], b_tok[:, 0, g * P:(g + 1) * P], x_late[:, 0, g * 512:(g + 1) * 512],
                                  start=True, stop=True)
                    for tile in range(INNER_TILES):
                        pick = expand[:, tile * P:(tile + 1) * P]
                        pe.matmul(grows[tile // 4][:, (tile % 4) * P:(tile % 4 + 1) * P], pick,
                                  log_sum[:, halves[1]], start=True, stop=True)
            with nc.Block() as block:
                @block.vector
                def _(dve):
                    for g in range(GROUPS):
                        dve.tensor_copy(state[:, g * 512:(g + 1) * 512], adds[g][:, :])

                @block.scalar
                def _(act):
                    for g in range(GROUPS):
                        act.activation(grown[:, 4 * g:4 * g + 4, :],
                                       grows[g][:, :].rearrange("p (a j) -> p a j", a=4), ACT.Exp)
        with ExitStack() as ps:
            decay = core.sb(ps, "decay", [P, 2, 8, P])
            carried = core.sb(ps, "carried", [P, 512])
            sum_banks = core.banks(ps, "sum", 4)
            y_banks = core.banks(ps, "y", 2)
            (carry_bank,) = core.banks(ps, "carry", 1)
            work = [(half, g) for half in range(HALVES) for g in range(GROUPS)]
            row0, y0, gap0, exp0, weight0, out0 = (core.pe_done.at, core.tile_multiplied.at, core.dve_done.at,
                                                   core.act_done.at, core.pool_done.at, core.tile_evicted.at)
            with nc.Block() as block:
                @block.tensor
                def _(pe):
                    def rows(n):
                        half, g = work[n]
                        if n >= 2:
                            pe.wait_ge(core.dve_done.sem, gap0 + n - 1)
                        for h in range(8):
                            last = pe.matmul(sum_banks[2 * (n % 2) + h // 4][:, (h % 4) * P:(h % 4 + 1) * P],
                                             core.ident[0:HEADS, 8 * g + h:8 * g + h + 1].broadcast_to((HEADS, P)),
                                             log_sum[:, halves[half]], start=True, stop=True)
                        core.pe_done.inc(last)

                    rows(0)
                    for n, (half, g) in enumerate(work):
                        if n + 1 < len(work):
                            rows(n + 1)
                        if n >= 2:
                            pe.wait_ge(core.tile_evicted.sem, out0 + n - 1)
                        if half:
                            if g:
                                pe.wait_ge(core.tile_evicted.sem, out0 + n)
                            for tile in range(4 * g, 4 * g + 4):
                                pe.matmul(carry_bank[:, (tile % 4) * P:(tile % 4 + 1) * P],
                                          state[:, tile * P:(tile + 1) * P], c[:, 20 + g, halves[1]],
                                          start=True, stop=True)
                        pe.wait_ge(core.pool_done.sem, weight0 + n + 1)
                        for h in range(8):
                            last = pe.matmul(
                                y_banks[n % 2][64 * (h % 2):64 * (h % 2) + 64, (h // 2) * P:(h // 2 + 1) * P],
                                x_tok[:, half, (8 * g + h) * 64:(8 * g + h + 1) * 64], decay[:, n % 2, h, :],
                                start=True, stop=True)
                        core.tile_multiplied.inc(last)

                @block.vector
                def _(dve):
                    def gaps(n):
                        half, g = work[n]
                        dve.wait_ge(core.pe_done.sem, row0 + n + 1)
                        if n >= 2:
                            dve.wait_ge(core.tile_multiplied.sem, y0 + n - 1)
                        for h in range(8):
                            last = dve.tensor_scalar(
                                decay[:, n % 2, h, :],
                                sum_banks[2 * (n % 2) + h // 4][:, (h % 4) * P:(h % 4 + 1) * P],
                                sum_tok[:, half, 8 * g + h:8 * g + h + 1], 0.0, ALU.subtract, ALU.min)
                        core.dve_done.inc(last)

                    def finish(n):
                        half, g = work[n]
                        dve.wait_ge(core.tile_multiplied.sem, y0 + n + 1)
                        to = y[:, 4 * g:4 * g + 4, halves[half]]
                        four = lambda a: a.rearrange("p (a j) -> p a j", a=4)
                        if half:
                            link = Link(dve, core.carry_done)
                            link(dve.tensor_tensor(four(carried), four(carry_bank[:, :]), grown[:, 4 * g:4 * g + 4, :],
                                                   ALU.mult))
                            core.tile_evicted.inc(dve.tensor_tensor(to, four(y_banks[n % 2][:, :]), four(carried),
                                                                    ALU.add))
                        else:
                            core.tile_evicted.inc(dve.tensor_copy(to, four(y_banks[n % 2][:, :])))

                    gaps(0)
                    for n in range(len(work)):
                        if n + 1 < len(work):
                            gaps(n + 1)
                        finish(n)

                @block.scalar
                def _(act):
                    for n in range(len(work)):
                        act.wait_ge(core.dve_done.sem, gap0 + n + 1)
                        core.act_done.inc(act.activation(decay[:, n % 2], decay[:, n % 2], ACT.Exp))

                @block.gpsimd
                def _(pool):
                    for n, (half, g) in enumerate(work):
                        pool.wait_ge(core.act_done.sem, exp0 + n + 1)
                        core.pool_done.inc(pool.tensor_tensor(
                            decay[:, n % 2], decay[:, n % 2],
                            inside[:, half, g:g + 1, :].broadcast_to((P, 8, P)), ALU.mult))
        with ExitStack() as ps:
            adds = core.banks(ps, "adds", 4)
            with nc.Block() as block:
                @block.tensor
                def _(pe):
                    for g in range(GROUPS):
                        pe.matmul(adds[g][:, :], b_tok[:, 1, g * P:(g + 1) * P], x_late[:, 1, g * 512:(g + 1) * 512],
                                  start=True, stop=True)

                @block.vector
                def _(dve):
                    s = state.rearrange("p (h v) -> p h v", h=HEADS)
                    dve.tensor_tensor(s, s, end[:, 1].unsqueeze(2).broadcast_to((P, HEADS, 64)), ALU.mult)
            with nc.Block() as block:
                @block.vector
                def _(dve):
                    for g in range(GROUPS):
                        at = slice(g * 512, (g + 1) * 512)
                        dve.tensor_tensor(state[:, at], adds[g][:, :], state[:, at], ALU.add)
            with nc.Block() as block:
                @block.sync
                def _(sp):
                    core.stored.inc(sp.dma_start(state_out, state), 16)
                    sp.wait_ge(core.stored.sem, core.stored.at)


def mixer_ssm(core, x, d, mask):
    nc = core.nc
    core.carry_done = Count(nc, "carry_done")
    with ExitStack() as ctx:
        params = core.sb(ctx, "params", [P, SSM_PARAMS])

        def par(name, i=None):
            at = SSM_PARAM[name]
            return params[:, at] if i is None else params[:, at.start + i:at.start + i + 1]

        y = core.sb(ctx, "y", [P, INNER_TILES, T])
        with ExitStack() as local:
            p = core.sb(local, "p", [P, SSM_TILES, T])
            c = core.sb(local, "c", [P, CONV_TILES, T])
            xdt = core.sb(local, "xdt", [P, INNER_TILES, T])
            dt = core.sb(local, "dt", [HEADS, T])
            log_a = core.sb(local, "log_a", [HEADS, T])
            log_sum = core.sb(local, "log_sum", [HEADS, SEQ])
            expand = core.sb(local, "expand", [HEADS, INNER])
            with nc.Block() as block:
                @block.vector
                def _(dve):
                    dve.tensor_copy(expand.rearrange("p (h v) -> p h v", h=HEADS),
                                    core.ident[0:HEADS, 0:HEADS].unsqueeze(2).broadcast_to((HEADS, HEADS, 64)))
            with nc.Block() as block:
                @block.sync
                def _(sp):
                    core.load(sp, params, d["ssm_params"])
                    core.wait_loads(sp)
            with ExitStack() as inner:
                h = core.sb(inner, "mix_in", [P, KC, T])
                rms_norm(core, x, par("norm"), h)
                project(core, d["ssm_w_in"], SSM_TILES, KC, h, p)
                ssm_steps(core, h, d["ssm_w_dt"], d["ssm_heads"], mask, dt, log_a, log_sum)
            ssm_conv(core, par, p, c, d["conv_in"], d["conv_prompt"], d["conv_sample"])
            with ExitStack() as ps:
                banks = core.banks(ps, "dt", 8)
                done0, used0 = core.pe_done.at, core.dve_done.at
                with nc.Block() as block:
                    @block.tensor
                    def _(pe):
                        for tile in range(INNER_TILES):
                            if tile >= 8:
                                pe.wait_ge(core.dve_done.sem, used0 + tile - 7)
                            pick = expand[:, tile * P:(tile + 1) * P]
                            core.pe_done.inc(pe.matmul(banks[tile % 8][:, 0:T], pick, dt, start=True, stop=True))

                    @block.vector
                    def _(dve):
                        for tile in range(INNER_TILES):
                            dve.wait_ge(core.pe_done.sem, done0 + tile + 1)
                            core.dve_done.inc(dve.tensor_tensor(xdt[:, tile, :], banks[tile % 8][:, 0:T],
                                                                c[:, tile, :], ALU.mult))
            ssm_sample(core, c, xdt, log_a, y, d["ssm_in"], d["ssm_sample"])
            ssm_prompt(core, mask, expand, c, xdt, log_sum, y, d["ssm_prompt"])
            with nc.Block() as block:
                @block.scalar
                def _(act):
                    act.activation(p[:, 0:INNER_TILES, :], p[:, 0:INNER_TILES, :], ACT.Silu)

                @block.vector
                def _(dve):
                    for i in range(INNER_TILES):
                        dve.scalar_tensor_tensor(y[:, i, :], c[:, i, :], par("skip", i), y[:, i, :],
                                                 ALU.mult, ALU.add)
            with nc.Block() as block:
                @block.vector
                def _(dve):
                    dve.tensor_tensor(y, y, p[:, 0:INNER_TILES, :], ALU.mult)
        with ExitStack() as local:
            squares = core.sb(local, "squares", [P, INNER_TILES, T])
            rstd = core.sb(local, "rstd", [P, GROUPS, T])
            banks = core.banks(local, "norm", GROUPS)
            with nc.Block() as block:
                @block.scalar
                def _(act):
                    act.activation(squares, y, ACT.Square)
            with nc.Block() as block:
                @block.tensor
                def _(pe):
                    for g in range(GROUPS):
                        for i in range(4):
                            pe.matmul(banks[g][:, 0:T], core.ones, squares[:, 4 * g + i, :], start=i == 0, stop=i == 3)
            inverse_root(core, banks, GROUPS, rstd, 1.0 / 512, RMS_EPS)
            with nc.Block() as block:
                @block.vector
                def _(dve):
                    for i in range(INNER_TILES):
                        dve.scalar_tensor_tensor(y[:, i, :], y[:, i, :], par("out_norm", i), rstd[:, i // 4, :],
                                                 ALU.mult, ALU.mult)
        project(core, d["ssm_w_out"], KC, INNER_TILES, y, x, residual=True)


def lay_out(inputs):
    import numpy as np
    c = np.ascontiguousarray

    def tiles(w, kc):
        return c(np.transpose(np.reshape(w, (kc, P, -1, P)), (2, 1, 0, 3)).reshape(-1, P, kc * P))

    def columns(*vectors):
        return c(np.concatenate([np.reshape(v, (-1, P)).T for v in vectors], axis=1))

    i = inputs
    tokens = np.concatenate([i["x_prompt"][0], i["x_sample"][:, 0]], axis=0)
    d = {"x": c(np.transpose(np.reshape(tokens, (T, KC, P)), (2, 1, 0))), "masks": masks()}
    if "ab_w_in" in i:
        d["ab_params"] = columns(i["norm_mix"][0], i["rwkv_mu"][0], i["rwkv_w0"][0], i["rwkv_a0"][0], i["rwkv_k_k"][0],
                                 i["rwkv_k_a"][0], i["rwkv_r_k"][0], i["rwkv_gn_w"][0], i["rwkv_gn_b"][0],
                                 i["hgrn_lower_bounds"][0], i["hgrn_norm_w"][0])
        d["ab_w_in"] = tiles(i["ab_w_in"][0], KC)
        d["ab_w_out"] = tiles(i["ab_w_out"][0], KC)
        d["lora_up"] = c(np.concatenate([i["rwkv_w_up"][0], i["rwkv_a_up"][0]], axis=0))
        d["gate_up"] = c(i["rwkv_g_up"][0])
        d["shift_in"] = c(np.transpose(np.reshape(i["state_rwkv_shift"][0], (DEC, SHIFT_TILES, P)), (2, 1, 0)))
        d["rwkv_in"] = c(np.transpose(np.reshape(i["state_rwkv"][0], (DEC, 4, 2, 64, 64)), (2, 4, 1, 0, 3)
                                      ).reshape(P, 4, DEC, 64))
        d["hgrn_in"] = c(np.transpose(i["state_hgrn"][0], (2, 1, 0, 3)))
    if "ssm_w_in" in i:
        w = i["ssm_w_in"][0]
        d["ssm_params"] = columns(i["norm_mix"][1], i["ssm_conv_w"][0], i["ssm_conv_b"][0], i["ssm_norm_w"][0],
                                  np.repeat(i["ssm_d"][0], 64))
        d["ssm_heads"] = c(np.stack([i["ssm_dt_bias"][0], i["ssm_a_log"][0]], axis=1))
        d["ssm_w_in"] = tiles(w[:, 0:SSM_TILES * P], KC)
        d["ssm_w_dt"] = c(np.transpose(np.reshape(w[:, SSM_TILES * P:], (KC, P, 32)), (1, 0, 2)))
        d["ssm_w_out"] = tiles(i["ssm_w_out"][0], 2 * KC)
        d["conv_in"] = c(np.transpose(np.reshape(i["state_conv"][0], (DEC, 3, CONV_TILES, P)), (3, 2, 1, 0)))
        d["ssm_in"] = c(np.transpose(i["state_ssm"][0], (3, 0, 1, 2)).reshape(P, DEC, 2048))
    if "peer_w_q" in i:
        for n in range(2):
            d[f"norm_ffn{n}"] = columns(i["norm_ffn"][n])
            d[f"w_q{n}"] = tiles(i["peer_w_q"][n], KC)
            d[f"sub_keys{n}"] = c(np.transpose(i["peer_sub_keys"][n], (3, 1, 0, 2)).reshape(P, SETS, KEYS))
            d[f"up{n}"] = c(np.transpose(np.reshape(i["peer_u"][n], (KEYS, KEYS, KC, P)), (1, 3, 2, 0)
                                         ).reshape(KEYS, P, D_MODEL))
            d[f"down{n}"] = c(np.transpose(np.reshape(i["peer_v"][n], (KEYS, KEYS, D_MODEL)), (1, 0, 2)))
        d["norm_final"] = columns(i["norm_final"])
    return d


def tokens_back(y):
    import numpy as np
    return np.transpose(y, (2, 1, 0)).reshape(T, -1)


def ab_back(r):
    import numpy as np
    c = np.ascontiguousarray
    shift = np.transpose(r["last_shift"], (2, 1, 0)).reshape(DEC + 1, SHIFT_TILES * P)
    s = np.reshape(r["rwkv_prompt"], (2, 64, 4, 2, 64))
    rwkv = np.stack([s[0, :, :, 0, :], s[1, :, :, 1, :]], axis=0)
    rwkv = np.transpose(rwkv, (2, 0, 3, 1)).reshape(1, 1, 8, 64, 64)
    hgrn = np.transpose(r["hgrn_prompt"], (1, 0, 2)).reshape(1, 1, 4, P, P)
    s_rwkv = np.transpose(np.reshape(r["rwkv_sample"], (2, 64, 4, DEC, 64)), (3, 2, 0, 4, 1)).reshape(1, DEC, 8, 64, 64)
    s_hgrn = np.transpose(r["hgrn_sample"], (2, 1, 0, 3)).reshape(1, DEC, 4, P, P)
    return (c(shift[None, 0:1]), c(rwkv), c(hgrn)), (c(shift[None, 1:]), c(s_rwkv), c(s_hgrn))


AB_OUT = {"last_shift": (P, SHIFT_TILES, DEC + 1), "rwkv_prompt": (P, 4, P), "rwkv_sample": (P, 4, DEC, 64),
          "hgrn_prompt": (P, 4, P), "hgrn_sample": (P, 4, DEC, P)}


def ssm_back(r):
    import numpy as np
    c = np.ascontiguousarray
    conv = np.transpose(r["conv_prompt"], (2, 1, 0)).reshape(1, 1, TAPS - 1, CONV_TILES * P)
    s_conv = np.transpose(r["conv_sample"], (3, 2, 1, 0)).reshape(1, DEC, TAPS - 1, CONV_TILES * P)
    ssm = np.transpose(np.reshape(r["ssm_prompt"], (P, HEADS, 64)), (1, 2, 0))[None, None]
    s_ssm = np.transpose(np.reshape(r["ssm_sample"], (P, DEC, HEADS, 64)), (1, 2, 3, 0))[None]
    return (c(ssm), c(conv)), (c(s_ssm), c(s_conv))


def program(nc, d):
    with ExitStack() as ctx:
        core = Core(nc, ctx)
        constants(core, ctx)
        x = core.sb(ctx, "x", [P, KC, T])
        norms = core.sb(ctx, "norms", [P, 3, KC])

        def mixer(build):
            with ExitStack() as local:
                mask = core.sb(local, "mask", [P, MASKS, P])
                with nc.Block() as block:
                    @block.sync
                    def _(sp):
                        core.load(sp, mask, d["masks"])
                        core.wait_loads(sp)
                build(core, x, d, mask)

        with nc.Block() as block:
            @block.sync
            def _(sp):
                core.load(sp, x, d["x"])
                for n, name in enumerate(("norm_ffn0", "norm_ffn1", "norm_final")):
                    core.load(sp, norms[:, n, :], d[name])
                core.wait_loads(sp)
        mixer(mixer_ab)
        peer(core, x, norms[:, 0, :], d["w_q0"], d["sub_keys0"], d["up0"], d["down0"])
        mixer(mixer_ssm)
        peer(core, x, norms[:, 1, :], d["w_q1"], d["sub_keys1"], d["up1"], d["down1"])
        with ExitStack() as local:
            y = core.sb(local, "y", [P, KC, T])
            rms_norm(core, x, norms[:, 2, :], y)
            with nc.Block() as block:
                @block.sync
                def _(sp):
                    core.stored.inc(sp.dma_start(d["y"], y), 16)
                    sp.wait_ge(core.stored.sem, core.stored.at)


def kernel(**inputs):
    import numpy as np
    import concourse.bacc as bacc
    from concourse.bass_utils import run_bass_kernel_spmd as run

    nc = bacc.Bacc("TRN2", target_bir_lowering=False, num_devices=1)
    arrays = lay_out(inputs)
    d = {k: nc.dram_tensor("in_" + k, a.shape, F32, kind="ExternalInput").ap() for k, a in arrays.items()}
    for k, shape in {**AB_OUT, **SSM_OUT, "y": (P, KC, T)}.items():
        d[k] = nc.dram_tensor(k, shape, F32, kind="ExternalOutput").ap()
    program(nc, d)
    r = run(nc, [{"in_" + k: a for k, a in arrays.items()}], core_ids=[0]).results[0]
    (p_shift, p_rwkv, p_hgrn), (s_shift, s_rwkv, s_hgrn) = ab_back(r)
    (p_ssm, p_conv), (s_ssm, s_conv) = ssm_back(r)
    y = np.ascontiguousarray(tokens_back(r["y"]))
    return (y[None, 0:SEQ], y[SEQ:T, None], p_shift, p_rwkv, p_hgrn, p_ssm, p_conv,
            s_shift, s_rwkv, s_hgrn, s_ssm, s_conv)
```

```python
from contextlib import ExitStack

import concourse.bass as bass
from concourse import mybir

F32 = mybir.dt.float32
F32R = mybir.dt.float32r
U32 = mybir.dt.uint32
ACT = mybir.ActivationFunctionType
ALU = mybir.AluOpType
AX_X = mybir.AxisListType.X

P = 128
D_MODEL = 1024
SEQ = 256
DEC = 8
T = SEQ + DEC
KC = D_MODEL // P
RMS_EPS = 1e-6


class Count:

    def __init__(self, nc, name):
        self.sem = nc.alloc_semaphore(name)
        self.at = 0

    def inc(self, ins, by=1):
        ins.then_inc(self.sem, by)
        self.at += by
        return self.at


class Link:

    def __init__(self, eng, count):
        self.eng, self.count = eng, count

    def __call__(self, ins):
        self.eng.wait_ge(self.count.sem, self.count.inc(ins))


class Core:

    def __init__(self, nc, ctx):
        self.nc, self.ctx = nc, ctx
        self.names = 0
        self.dve_done = Count(nc, "dve_done")
        self.act_done = Count(nc, "act_done")
        self.pool_done = Count(nc, "pool_done")
        self.pe_done = Count(nc, "pe_done")
        self.loaded = Count(nc, "loaded")
        self.stored = Count(nc, "stored")
        self.tile_loaded = [Count(nc, f"tile_loaded{i}") for i in range(RING)]
        self.state_loaded = [Count(nc, f"state_loaded{i}") for i in range(RING)]
        self.state_stored = [Count(nc, f"state_stored{i}") for i in range(RING)]
        self.tile_multiplied = Count(nc, "tile_multiplied")
        self.tile_evicted = Count(nc, "tile_evicted")
        self.hi_made = Count(nc, "hi_made")
        self.lo_made = Count(nc, "lo_made")
        self.gate_equal = Count(nc, "gate_equal")
        self.gate_summed = Count(nc, "gate_summed")
        self.gate_copied = Count(nc, "gate_copied")
        self.gated_hi = Count(nc, "gated_hi")
        self.gated_lo = Count(nc, "gated_lo")

    def sb(self, ctx, name, shape, dt=F32):
        self.names += 1
        return ctx.enter_context(self.nc.sbuf_tensor(f"{name}_{self.names}", shape, dt))[:]

    def banks(self, ctx, name, n):
        self.names += 1
        return [ctx.enter_context(self.nc.psum_tensor(f"{name}_{self.names}_{i}", [P, 512], F32)) for i in range(n)]

    def load(self, eng, dst, src):
        self.loaded.inc(eng.dma_start(dst, src), 16)

    def wait_loads(self, eng):
        eng.wait_ge(self.loaded.sem, self.loaded.at)


def constants(core, ctx):
    nc = core.nc
    core.ident = core.sb(ctx, "ident", [P, P])
    core.ones = core.sb(ctx, "ones", [P, P])
    core.index_row = core.sb(ctx, "index_row", [P, P])
    with nc.Block() as block:
        @block.gpsimd
        def _(pool):
            link = Link(pool, core.pool_done)
            link(pool.iota(core.index_row, [[1, P]], base=0, channel_multiplier=0,
                           allow_small_or_imprecise_dtypes=True))
            link(pool.memset(core.ident, 0.0))
            link(pool.affine_select(core.ident, core.ident, [[-1, P]], ALU.not_equal, 1.0, 0, 1))
            link(pool.memset(core.ones, 1.0))


def rms_norm(core, x, weight, out):
    nc = core.nc
    with ExitStack() as ctx:
        squares = core.sb(ctx, "squares", [P, KC, T])
        rstd = core.sb(ctx, "rstd", [P, T])
        (total,) = core.banks(ctx, "square_sum", 1)
        squared, summed, mean_ready, root_ready = (
            core.act_done.at, core.pe_done.at, core.dve_done.at, core.act_done.at + 1)
        with nc.Block() as block:
            @block.scalar
            def _(act):
                core.act_done.inc(act.activation(squares[:], x, ACT.Square))
                act.wait_ge(core.dve_done.sem, mean_ready + 1)
                core.act_done.inc(act.activation(rstd[:], rstd[:], ACT.Sqrt))

            @block.tensor
            def _(pe):
                pe.wait_ge(core.act_done.sem, squared + 1)
                for k in range(KC):
                    last = pe.matmul(total[:, 0:T], core.ones, squares[:, k, :], start=k == 0, stop=k == KC - 1)
                core.pe_done.inc(last)

            @block.vector
            def _(dve):
                link = Link(dve, core.dve_done)
                dve.wait_ge(core.pe_done.sem, summed + 1)
                core.dve_done.inc(dve.tensor_scalar(rstd[:], total[:, 0:T], 1.0 / D_MODEL, RMS_EPS, ALU.mult, ALU.add))
                dve.wait_ge(core.act_done.sem, root_ready + 1)
                link(dve.reciprocal(rstd[:], rstd[:]))
                for k in range(KC):
                    dve.scalar_tensor_tensor(out[:, k, :], x[:, k, :], weight[:, k:k + 1], rstd[:],
                                             ALU.mult, ALU.mult)


UNROLL = 6
RING = 3


def tile_loop(eng, n, one):
    for u in range(min(n, UNROLL)):
        one(0, u)
    if n // UNROLL > 1:
        with eng.Fori(1, n // UNROLL) as i:
            for u in range(UNROLL):
                one(i, u)
    if n > UNROLL:
        for u in range(n % UNROLL):
            one(n // UNROLL, u)


def fresh(i, u, ring=RING):
    return isinstance(i, int) and i * UNROLL + u < ring


def split(core, src, hi, lo):
    with core.nc.Block() as block:
        @block.scalar
        def _(act):
            act.copy(hi, src)
    with core.nc.Block() as block:
        @block.vector
        def _(dve):
            dve.tensor_tensor(lo, src, hi.bitcast(F32), ALU.subtract)


class Stream:

    def __init__(self, dram, first=0, cols=slice(0, D_MODEL)):
        self.dram, self.first, self.cols = dram, first, cols
        self.parts = dram.shape[2] if len(dram.shape) == 4 else 1
        self.width = self.parts * (cols.stop - cols.start)
        self.loading = False

    def load(self, core, sp, i, u):
        at = bass.ds(i * UNROLL + (u + self.first), 1)
        dst = core.weights_raw[:, u % RING, 0:self.width]
        if self.parts > 1:
            tile = self.dram[at].rearrange("a p g f -> p (a g) f")[:, :, self.cols]
            dst = dst.rearrange("p (g f) -> p g f", g=self.parts)
        else:
            tile = self.dram[at].rearrange("a p f -> p (a f)")[:, self.cols]
        sp.dma_start(dst, tile).then_inc(core.tile_loaded[u % RING].sem, 16)


def first_loads(core, sp, stream):
    for s in range(RING):
        stream.load(core, sp, 0, s)
    stream.loading = True


class Weights:

    def __init__(self, core, ctx):
        self.core = core
        self.hi = core.sb(ctx, "weights_hi", [P, RING, D_MODEL], F32R)
        self.lo = core.sb(ctx, "weights_lo", [P, RING, D_MODEL], F32R)
        self.raw = core.weights_raw

    def begin(self, stream, then=None):
        core = self.core
        self.stream, self.then, self.width = stream, then, stream.width
        self.loaded0 = [c.at for c in core.tile_loaded[0:RING]]
        self.hi0, self.lo0, self.used0 = core.hi_made.at, core.lo_made.at, core.tile_multiplied.at

    def load_all(self, sp, n):
        def load(i, u):
            if fresh(i, u):
                if not self.stream.loading:
                    self.stream.load(self.core, sp, i, u)
            else:
                sp.wait_ge(self.core.lo_made.sem, i * UNROLL + (u - 2 + self.lo0))
                self.stream.load(self.core, sp, i, u)
        tile_loop(sp, n, load)
        if self.then:
            for s in range(RING):
                sp.wait_ge(self.core.lo_made.sem, self.lo0 + n - (n - 1 - s) % RING)
                self.then.load(self.core, sp, 0, s)
            self.then.loading = True

    def make_hi(self, act, i, u):
        act.wait_ge(self.core.tile_loaded[u % RING].sem, i * (16 * UNROLL // RING) + (16 * (u // RING + 1) + self.loaded0[u % RING]))
        if not fresh(i, u):
            act.wait_ge(self.core.tile_multiplied.sem, i * UNROLL + (u - 2 + self.used0))
        act.copy(self.hi[:, u % RING, 0:self.width], self.raw[:, u % RING, 0:self.width]
                 ).then_inc(self.core.hi_made.sem, 1)

    def make_lo(self, pool, i, u):
        pool.wait_ge(self.core.hi_made.sem, i * UNROLL + (u + 1 + self.hi0))
        pool.tensor_tensor(self.lo[:, u % RING, 0:self.width], self.raw[:, u % RING, 0:self.width],
                           self.hi[:, u % RING, 0:self.width].bitcast(F32), ALU.subtract
                           ).then_inc(self.core.lo_made.sem, 1)

    def ready(self, pe, i, u):
        pe.wait_ge(self.core.lo_made.sem, i * UNROLL + (u + 1 + self.lo0))

    def product(self, pe, out, u, cols, rhs_hi, rhs_lo, start, stop):
        hi, lo = self.hi[:, u % RING, cols], self.lo[:, u % RING, cols]
        pe.matmul(out, hi, rhs_hi, start=start, stop=False, skip_group_check=True)
        pe.matmul(out, hi, rhs_lo, start=False, stop=False, skip_group_check=True)
        return pe.matmul(out, lo, rhs_hi, start=False, stop=stop, skip_group_check=True)

    def end(self, n):
        core = self.core
        for s in range(RING):
            core.tile_loaded[s].at += 16 * ((n - s + RING - 1) // RING)
        core.hi_made.at += n
        core.lo_made.at += n
        core.tile_multiplied.at += n


def project(core, weights, stream, n, rhs_hi, rhs_lo, dst, parts=1, residual=False, then=None):
    nc = core.nc
    total = n * parts
    weights.begin(stream, then)
    with ExitStack() as ctx:
        banks = core.banks(ctx, "projected", RING)
        used0, out0 = core.tile_multiplied.at, core.tile_evicted.at
        bank_of = lambda u: banks[(u // parts) % RING]

        def evict(eng, i, u):
            eng.wait_ge(core.tile_multiplied.sem, i * UNROLL + (u + 1 + used0))
            to = dst[:, bass.ds(i * (UNROLL // parts) + u // parts, 1), :]
            got = bank_of(u)[:, 0:T].rearrange("p (a f) -> p a f", a=1)
            ins = eng.tensor_tensor(to, got, to, ALU.add) if residual else eng.copy(to, got)
            ins.then_inc(core.tile_evicted.sem, 1)

        with nc.Block() as block:
            @block.sync
            def _(sp):
                weights.load_all(sp, total)

            @block.gpsimd
            def _(pool):
                tile_loop(pool, total, lambda i, u: weights.make_lo(pool, i, u))

            @block.tensor
            def _(pe):
                def multiply(i, u):
                    weights.ready(pe, i, u)
                    part = u % parts
                    if part == 0 and not fresh(i, u, RING * parts):
                        pe.wait_ge(core.tile_evicted.sem, i * (UNROLL // parts) + (u // parts - 2 + out0))
                    for k in range(KC):
                        last = weights.product(pe, bank_of(u)[:, 0:T], u, slice(k * P, (k + 1) * P),
                                               rhs_hi[:, part * KC + k, :], rhs_lo[:, part * KC + k, :],
                                               start=part == 0 and k == 0, stop=part == parts - 1 and k == KC - 1)
                    last.then_inc(core.tile_multiplied.sem, 1)
                tile_loop(pe, total, multiply)

            @block.scalar
            def _(act):
                def body(i, u):
                    weights.make_hi(act, i, u)
                    if not residual and not fresh(i, u, 2):
                        evict(act, i, u - 2)
                tile_loop(act, total, body)
                if not residual:
                    for t in (total - 2, total - 1):
                        evict(act, t // UNROLL, t % UNROLL)

            if residual:
                @block.vector
                def _(dve):
                    tile_loop(dve, total, lambda i, u: evict(dve, i, u) if u % parts == parts - 1 else None)
        core.tile_evicted.at += n
    weights.end(total)


PEER_HEADS = 8
KEYS = 128
TOPK = 16
SETS = 2 * PEER_HEADS
TOKEN_TILES = [(0, P), (P, P), (2 * P, DEC)]
LOWEST = -3.0e38


def peer_scores(core, weights, streams, h_hi, h_lo, sub_keys, scores):
    nc = core.nc
    with ExitStack() as ctx:
        queries = core.sb(ctx, "queries", [P, SETS, T])
        keys = core.sb(ctx, "keys", [P, SETS, KEYS])
        with nc.Block() as block:
            @block.sync
            def _(sp):
                core.load(sp, keys[:], sub_keys)

            @block.gpsimd
            def _(pool):
                core.pool_done.inc(pool.memset(scores[:, 2, :, :], 0.0))
        project(core, weights, streams[0], SETS, h_hi, h_lo, queries, then=streams[1])
        banks = core.banks(ctx, "score", 4)
        per_tile = SETS // 4
        done0, out0 = core.pe_done.at, core.act_done.at
        with nc.Block() as block:
            @block.tensor
            def _(pe):
                core.wait_loads(pe)
                for tile, (t0, rows) in enumerate(TOKEN_TILES):
                    for q in range(per_tile):
                        n = tile * per_tile + q
                        if n >= 4:
                            pe.wait_ge(core.act_done.sem, out0 + n - 3)
                        for s in range(4):
                            last = pe.matmul(banks[n % 4][0:rows, s * KEYS:(s + 1) * KEYS],
                                             queries[:, 4 * q + s, t0:t0 + rows], keys[:, 4 * q + s, :],
                                             start=True, stop=True)
                        core.pe_done.inc(last)

            @block.scalar
            def _(act):
                for tile, (t0, rows) in enumerate(TOKEN_TILES):
                    for q in range(per_tile):
                        n = tile * per_tile + q
                        act.wait_ge(core.pe_done.sem, done0 + n + 1)
                        core.act_done.inc(act.copy(scores[0:rows, tile, 4 * q:4 * q + 4, :],
                                                   banks[n % 4][0:rows, :].rearrange("p (s k) -> p s k", s=4)))


def top16(dve, link, values, sets, top, index):
    for s in range(sets):
        last = dve.max(top[:, s, 0:8], values(s))
    link(last)
    for s in range(sets):
        dve.max_index(index[:, s, 0:8], top[:, s, 0:8], values(s))
    for s in range(sets):
        last = dve.match_replace(values(s), top[:, s, 0:8], values(s), LOWEST)
    link(last)
    for s in range(sets):
        last = dve.max(top[:, s, 8:16], values(s))
    link(last)
    for s in range(sets):
        last = dve.max_index(index[:, s, 8:16], top[:, s, 8:16], values(s))
    link(last)


QUADS = T // 4
HALF = KEYS // 2
GROUP = 8


class Gates:

    def __init__(self, core, ctx, first_t, second_t, gate_hi, gate_lo):
        self.core, self.first_t, self.second_t = core, first_t, second_t
        self.gate_parts = (gate_hi.bitcast(F32), gate_lo.bitcast(F32))
        self.one_hot = core.sb(ctx, "one_hot", [P, 2, 4, KEYS], F32R)
        self.weighted = core.sb(ctx, "weighted", [P, 2, 4, 2, HALF], F32R)
        self.equal = core.sb(ctx, "equal", [P, 4, HALF], mybir.dt.uint8)
        self.low = core.sb(ctx, "low", [P, 4, HALF])

    def begin(self, half, banks, activations):
        self.half, self.banks, self.activations = half, banks, activations
        self.built0, self.made0, self.applied0 = self.core.dve_done.at, self.core.pe_done.at, self.core.pool_done.at
        self.equal0, self.summed0, self.copied0 = (self.core.gate_equal.at, self.core.gate_summed.at,
                                                   self.core.gate_copied.at)

    def build(self, dve, i, u):
        if not fresh(i, u, 2):
            dve.wait_ge(self.core.pe_done.sem, i * UNROLL + (u - 1 + self.made0))
        tokens = bass.ds(i * (4 * UNROLL) + u * 4, 4)
        each = lambda a, n: a[:, tokens].unsqueeze(2).broadcast_to((P, 4, n))
        keys = lambda first, n: self.core.index_row[:, first:first + n].unsqueeze(1).broadcast_to((P, 4, n))
        if not fresh(i, u, 1):
            dve.wait_ge(self.core.dve_done.sem, i * UNROLL + (u + self.built0))
        dve.tensor_tensor(self.equal, keys(self.half * HALF, HALF), each(self.second_t, HALF), ALU.is_equal
                          ).then_inc(self.core.gate_equal.sem, 1)
        dve.tensor_tensor(self.one_hot[:, u % 2], keys(0, KEYS), each(self.first_t, KEYS), ALU.is_equal)
        dve.wait_ge(self.core.gate_equal.sem, i * UNROLL + (u + 1 + self.equal0))
        for part, gate in enumerate(self.gate_parts):
            last = dve.tensor_tensor(self.weighted[:, u % 2, :, part], self.equal, each(gate, HALF), ALU.mult)
        last.then_inc(self.core.dve_done.sem, 1)

    def multiply(self, pe, i, u):
        pe.wait_ge(self.core.dve_done.sem, i * UNROLL + (u + 1 + self.built0))
        slots = len(self.banks)
        if not fresh(i, u, slots):
            pe.wait_ge(self.core.pool_done.sem, i * UNROLL + (u + 1 - slots + self.applied0))
        for t in range(4):
            last = pe.matmul(self.banks[u % slots][:, t * KEYS:(t + 1) * KEYS], self.one_hot[:, u % 2, t, :],
                             self.weighted[:, u % 2, t].rearrange("p a k -> p (a k)"), start=True, stop=True)
        last.then_inc(self.core.pe_done.sem, 1)

    def products(self, u):
        return self.banks[u % len(self.banks)][:, :].rearrange("p (t a k) -> p t a k", t=4, a=2)

    def copy_low(self, act, i, u):
        act.wait_ge(self.core.pe_done.sem, i * UNROLL + (u + 1 + self.made0))
        if not fresh(i, u, 1):
            act.wait_ge(self.core.gate_summed.sem, i * UNROLL + (u + self.summed0))
        act.copy(self.low, self.products(u)[:, :, 1]).then_inc(self.core.gate_copied.sem, 1)

    def apply(self, dve, i, u):
        dve.wait_ge(self.core.gate_copied.sem, i * UNROLL + (u + 1 + self.copied0))
        high = self.products(u)[:, :, 0]
        dve.tensor_tensor(high, high, self.low, ALU.add).then_inc(self.core.gate_summed.sem, 1)
        dve.wait_ge(self.core.gate_summed.sem, i * UNROLL + (u + 1 + self.summed0))
        to = self.activations[:, :, bass.ds(i * (4 * UNROLL) + u * 4, 4)].rearrange("p k t -> p t k")
        dve.tensor_tensor(to, high, to, ALU.mult).then_inc(self.core.pool_done.sem, 1)

    def step(self, dve, i, u):
        if not fresh(i, u, 2):
            self.apply(dve, i, u - 2)
        self.build(dve, i, u)

    def rest_multiplied(self, pe):
        for n in range(HALF, QUADS):
            self.multiply(pe, n // UNROLL, n % UNROLL)

    def rest_copied(self, act):
        for n in range(HALF - 3, QUADS):
            self.copy_low(act, n // UNROLL, n % UNROLL)

    def rest_applied(self, dve):
        for n in range(HALF, QUADS):
            self.step(dve, n // UNROLL, n % UNROLL)
        for n in range(QUADS - 2, QUADS):
            self.apply(dve, n // UNROLL, n % UNROLL)

    def ended(self):
        for c in (self.core.dve_done, self.core.pe_done, self.core.pool_done, self.core.gate_equal,
                  self.core.gate_summed, self.core.gate_copied):
            c.at += QUADS


def peer_select(core, select, scores):
    top, index, index_f, pairs, best, place, rank, rank_f, hit, chosen = select

    def program(dve):
        link = Link(dve, core.dve_done)
        for tile in range(3):
            top16(dve, link, lambda s: scores[:, tile, s, :], SETS, top, index)
            dve.tensor_copy(index_f, index)
            by_head = top.rearrange("p (h c) k -> p h c k", c=2)
            link(dve.tensor_tensor(
                pairs, by_head[:, :, 0, :].unsqueeze(3).broadcast_to((P, PEER_HEADS, TOPK, TOPK)),
                by_head[:, :, 1, :].unsqueeze(2).broadcast_to((P, PEER_HEADS, TOPK, TOPK)), ALU.add))
            top16(dve, link, lambda s: pairs[:, s, :, :].rearrange("p i j -> p (i j)"), PEER_HEADS, best, place)
            dve.tensor_single_scalar(rank[:, 0], place, 4, ALU.logical_shift_right)
            dve.tensor_single_scalar(rank[:, 1], place, 15, ALU.bitwise_and)
            link(dve.tensor_tensor(chosen[:, tile, 2], best,
                                   best[:, :, 0:1].broadcast_to((P, PEER_HEADS, TOPK)), ALU.subtract))
            link(dve.tensor_copy(rank_f, rank))
            for c in range(2):
                steps = core.index_row[:, 0:TOPK].unsqueeze(1).unsqueeze(1).broadcast_to((P, PEER_HEADS, TOPK, TOPK))
                link(dve.tensor_tensor(hit, rank_f[:, c].unsqueeze(3).broadcast_to(
                    (P, PEER_HEADS, TOPK, TOPK)), steps, ALU.is_equal))
                ids = index_f.rearrange("p (h c) k -> p h c k", c=2)[:, :, c, :]
                link(dve.tensor_tensor(hit, hit, ids.unsqueeze(2).broadcast_to(
                    (P, PEER_HEADS, TOPK, TOPK)), ALU.mult))
                link(dve.tensor_reduce(chosen[:, tile, c], hit, AX_X, ALU.add))
    return program


def select_buffers(core, ctx):
    return (core.sb(ctx, "top", [P, SETS, TOPK]), core.sb(ctx, "index", [P, SETS, TOPK], U32),
            core.sb(ctx, "index_f", [P, SETS, TOPK]), core.sb(ctx, "pairs", [P, PEER_HEADS, TOPK, TOPK]),
            core.sb(ctx, "best", [P, PEER_HEADS, TOPK]), core.sb(ctx, "place", [P, PEER_HEADS, TOPK], U32),
            core.sb(ctx, "rank", [P, 2, PEER_HEADS, TOPK], U32), core.sb(ctx, "rank_f", [P, 2, PEER_HEADS, TOPK]),
            core.sb(ctx, "hit", [P, PEER_HEADS, TOPK, TOPK]), core.sb(ctx, "chosen", [P, 3, 3, PEER_HEADS, TOPK]))


def peer_turn(core, chosen, first_t, second_t, gate_hi, gate_lo):
    nc = core.nc
    with ExitStack() as ctx:
        total = core.sb(ctx, "total", [P, 3, PEER_HEADS])
        banks = core.banks(ctx, "turned", 3)
        turned = core.pe_done.at
        with nc.Block() as block:
            @block.scalar
            def _(act):
                act.activation(chosen[:, :, 2], chosen[:, :, 2], ACT.Exp)
        with nc.Block() as block:
            @block.vector
            def _(dve):
                link = Link(dve, core.dve_done)
                for tile in range(3):
                    last = dve.tensor_reduce(total[:, tile], chosen[:, tile, 2], AX_X, ALU.add)
                link(last)
                link(dve.reciprocal(total, total))
                for tile in range(3):
                    dve.tensor_tensor(chosen[:, tile, 2], chosen[:, tile, 2],
                                      total[:, tile].unsqueeze(2).broadcast_to((P, PEER_HEADS, TOPK)), ALU.mult)
        with nc.Block() as block:
            @block.tensor
            def _(pe):
                for kind in range(3):
                    for tile, (t0, rows) in enumerate(TOKEN_TILES):
                        last = pe.transpose(banks[kind][:, t0:t0 + rows],
                                            chosen[0:rows, tile, kind].rearrange("p h k -> p (h k)"),
                                            core.ident[0:rows, 0:rows])
                    core.pe_done.inc(last)

            @block.vector
            def _(dve):
                for kind, dst in enumerate((first_t, second_t)):
                    dve.wait_ge(core.pe_done.sem, turned + kind + 1)
                    dve.tensor_copy(dst, banks[kind][:, 0:T])

            @block.scalar
            def _(act):
                act.wait_ge(core.pe_done.sem, turned + 3)
                act.copy(gate_hi, banks[2][:, 0:T])
        with nc.Block() as block:
            @block.vector
            def _(dve):
                dve.tensor_tensor(gate_lo, banks[2][:, 0:T], gate_hi.bitcast(F32), ALU.subtract)


def peer_up(core, weights, stream, then, h_hi, h_lo, banks, dst, beside):
    nc = core.nc
    up0, gelu0 = core.tile_multiplied.at, core.act_done.at
    gates = beside if isinstance(beside, Gates) else None
    weights.begin(stream, then)
    with nc.Block() as block:
        @block.sync
        def _(sp):
            weights.load_all(sp, HALF)

        @block.gpsimd
        def _(pool):
            tile_loop(pool, HALF, lambda i, u: weights.make_lo(pool, i, u))

        @block.tensor
        def _(pe):
            def body(i, u):
                weights.ready(pe, i, u)
                if not fresh(i, u):
                    pe.wait_ge(core.act_done.sem, i * UNROLL + (u - 2 + gelu0))
                for k in range(KC):
                    last = weights.product(pe, banks[u % RING][:, 0:T], u, slice(k * P, (k + 1) * P),
                                           h_hi[:, k, :], h_lo[:, k, :], start=k == 0, stop=k == KC - 1)
                last.then_inc(core.tile_multiplied.sem, 1)
                if gates:
                    gates.multiply(pe, i, u)
            tile_loop(pe, HALF, body)
            if gates:
                gates.rest_multiplied(pe)

        @block.scalar
        def _(act):
            def gelu(i, u):
                act.wait_ge(core.tile_multiplied.sem, i * UNROLL + (u + 1 + up0))
                act.activation(dst[:, bass.ds(i * UNROLL + u, 1), :],
                               banks[u % RING][:, 0:T].rearrange("p (a t) -> p a t", a=1), ACT.Gelu
                               ).then_inc(core.act_done.sem, 1)

            def body(i, u):
                weights.make_hi(act, i, u)
                if not fresh(i, u):
                    if gates:
                        gates.copy_low(act, i, u - 3)
                    gelu(i, u - 3)
            tile_loop(act, HALF, body)
            for n in range(HALF - 3, HALF):
                gelu(n // UNROLL, n % UNROLL)
            if gates:
                gates.rest_copied(act)

        @block.vector
        def _(dve):
            if gates:
                tile_loop(dve, HALF, lambda i, u: gates.step(dve, i, u))
                gates.rest_applied(dve)
            else:
                beside(dve)
    weights.end(HALF)
    core.act_done.at += HALF
    if gates:
        gates.ended()


def peer_down(core, weights, stream, then, activations, a_hi, a_lo, sums, tiles, opens, gates=None):
    nc = core.nc
    hi0, lo0 = core.gated_hi.at, core.gated_lo.at
    weights.begin(stream, then)
    with nc.Block() as block:
        @block.sync
        def _(sp):
            weights.load_all(sp, HALF)

        @block.gpsimd
        def _(pool):
            tile_loop(pool, HALF, lambda i, u: weights.make_lo(pool, i, u))

        @block.scalar
        def _(act):
            def body(i, u):
                weights.make_hi(act, i, u)
                if gates and not fresh(i, u):
                    gates.copy_low(act, i, u - 3)
                act.copy(a_hi[:, u % RING:u % RING + 1, :], activations[:, bass.ds(i * UNROLL + u, 1), :]
                         ).then_inc(core.gated_hi.sem, 1)
            tile_loop(act, HALF, body)
            if gates:
                gates.rest_copied(act)

        @block.vector
        def _(dve):
            def body(i, u):
                slot = slice(u % RING, u % RING + 1)
                dve.wait_ge(core.gated_hi.sem, i * UNROLL + (u + 1 + hi0))
                dve.tensor_tensor(a_lo[:, slot, :], activations[:, bass.ds(i * UNROLL + u, 1), :],
                                  a_hi[:, slot, :].bitcast(F32), ALU.subtract).then_inc(core.gated_lo.sem, 1)
                if gates:
                    gates.step(dve, i, u)
            tile_loop(dve, HALF, body)
            if gates:
                gates.rest_applied(dve)

        @block.tensor
        def _(pe):
            def body(i, u):
                weights.ready(pe, i, u)
                pe.wait_ge(core.gated_lo.sem, i * UNROLL + (u + 1 + lo0))
                for n, d in enumerate(tiles):
                    last = weights.product(pe, sums[d][:, 0:T], u, slice(n * P, (n + 1) * P), a_hi[:, u % RING, :],
                                           a_lo[:, u % RING, :], start=fresh(i, u, 1) and d in opens, stop=False)
                last.then_inc(core.tile_multiplied.sem, 1)
                if gates:
                    gates.multiply(pe, i, u)
            tile_loop(pe, HALF, body)
            if gates:
                gates.rest_multiplied(pe)
    weights.end(HALF)
    core.gated_hi.at += HALF
    core.gated_lo.at += HALF
    if gates:
        gates.ended()


def peer_down_last(core, weights, stream, then, activations, a_hi, a_lo, total):
    nc = core.nc
    groups = HALF // GROUP
    hi0, lo0 = core.gated_hi.at, core.gated_lo.at
    weights.begin(stream, then)
    group = lambda u: activations[:, u * GROUP:(u + 1) * GROUP, :]
    with nc.Block() as block:
        @block.sync
        def _(sp):
            weights.load_all(sp, groups)

        @block.gpsimd
        def _(pool):
            for g in range(groups):
                weights.make_lo(pool, 0, g)

        @block.scalar
        def _(act):
            for g in range(groups):
                weights.make_hi(act, 0, g)
                act.copy(a_hi[:, g % RING], group(g)).then_inc(core.gated_hi.sem, 1)

        @block.vector
        def _(dve):
            for g in range(groups):
                dve.wait_ge(core.gated_hi.sem, hi0 + g + 1)
                dve.tensor_tensor(a_lo[:, g % RING], group(g), a_hi[:, g % RING].bitcast(F32), ALU.subtract
                                  ).then_inc(core.gated_lo.sem, 1)

        @block.tensor
        def _(pe):
            for g in range(groups):
                weights.ready(pe, 0, g)
                pe.wait_ge(core.gated_lo.sem, lo0 + g + 1)
                for j in range(GROUP):
                    last = weights.product(pe, total[:, 0:T], g, slice(j * P, (j + 1) * P), a_hi[:, g % RING, j, :],
                                           a_lo[:, g % RING, j, :], start=False, stop=False)
                last.then_inc(core.tile_multiplied.sem, 1)
    weights.end(groups)
    core.gated_hi.at += groups
    core.gated_lo.at += groups


def peer(core, x, norm_w, w_q, sub_keys, up_w, down_w, then=None):
    nc = core.nc
    lower_up, upper_up = Stream(up_w, 0), Stream(up_w, HALF)
    lower_down, upper_down = Stream(down_w, 0, slice(0, D_MODEL - P)), Stream(down_w, HALF)
    last_down = Stream(down_w.rearrange("(a g) p f -> a p g f", g=GROUP), 0, slice(D_MODEL - P, D_MODEL))
    with ExitStack() as ctx:
        h_hi = core.sb(ctx, "ffn_in_hi", [P, KC, T], F32R)
        h_lo = core.sb(ctx, "ffn_in_lo", [P, KC, T], F32R)
        first_t = core.sb(ctx, "first_t", [P, T])
        second_t = core.sb(ctx, "second_t", [P, T])
        gate_hi = core.sb(ctx, "gate_hi", [P, T], F32R)
        gate_lo = core.sb(ctx, "gate_lo", [P, T], F32R)
        lower_half = core.sb(ctx, "lower_half", [P, HALF, T])
        weights = Weights(core, ctx)
        with ExitStack() as select, ExitStack() as ps:
            with ExitStack() as local:
                h = core.sb(local, "ffn_in", [P, KC, T])
                rms_norm(core, x, norm_w, h)
                split(core, h, h_hi, h_lo)
            scores = core.sb(select, "scores", [P, 3, SETS, KEYS])
            peer_scores(core, weights, (w_q, lower_up), h_hi, h_lo, sub_keys, scores)
            buffers = select_buffers(core, select)
            banks = core.banks(ps, "up", RING)
            peer_up(core, weights, lower_up, upper_up, h_hi, h_lo, banks, lower_half,
                    peer_select(core, buffers, scores))
            peer_turn(core, buffers[-1], first_t, second_t, gate_hi, gate_lo)
        gates = Gates(core, ctx, first_t, second_t, gate_hi, gate_lo)
        with ExitStack() as local:
            upper_half = core.sb(local, "upper_half", [P, HALF, T])
            with ExitStack() as ps:
                banks = core.banks(ps, "up", RING)
                gates.begin(0, core.banks(ps, "gates", 2), lower_half)
                peer_up(core, weights, upper_up, lower_down, h_hi, h_lo, banks, upper_half, gates)
            sums = core.banks(ctx, "down", KC)
            gates.begin(1, sums[KC - 1:], upper_half)
            a_hi, a_lo = h_hi[:, 0:RING, :], h_lo[:, 0:RING, :]
            peer_down(core, weights, lower_down, upper_down, lower_half, a_hi, a_lo, sums, range(KC - 1),
                      range(KC - 1), gates)
            peer_down(core, weights, upper_down, last_down, upper_half, a_hi, a_lo, sums, range(KC), (KC - 1,))
        with ExitStack() as local:
            groups_hi = core.sb(local, "groups_hi", [P, RING, GROUP, T], F32R)
            groups_lo = core.sb(local, "groups_lo", [P, RING, GROUP, T], F32R)
            peer_down_last(core, weights, last_down, then, lower_half, groups_hi, groups_lo, sums[KC - 1])
        with nc.Block() as block:
            @block.vector
            def _(dve):
                for d in range(KC):
                    dve.tensor_tensor(x[:, d, :], sums[d][:, 0:T], x[:, d, :], ALU.add)


HALVES = SEQ // P
CHUNK = 64
CHUNKS = SEQ // CHUNK
RWKV_TILES = 4
SHIFT_TILES = 14
AB_TILES = 30
GN_EPS = 64e-5
L2_EPS = 1e-12
DECAY_SCALE = -0.6065306597126334

AB_PARAM = {}
_at = 0
for _name, _n in (("norm", 8), ("mu", 14), ("w0", 4), ("a0", 4), ("k_k", 4), ("k_a", 4), ("r_k", 4), ("gn_w", 4),
                  ("gn_b", 4), ("bound", 4), ("hgrn_norm", 1)):
    AB_PARAM[_name] = slice(_at, _at + _n)
    _at += _n
AB_PARAMS = _at

MASK_QUAD = 0
MASK_LOWER = 4
MASK_LEVEL = 5
MASK_FIRST = 12
MASK_CAUSAL = 13
MASK_EYE64 = 14
MASK_SCAN64 = 15
MASK_SCAN128 = 17
MASK_BLOCKS = 19
MASKS = 20


def masks():
    import numpy as np
    s, t = np.arange(P)[:, None], np.arange(P)[None, :]
    m = np.zeros((P, MASKS, P), np.float32)
    same = s // CHUNK == t // CHUNK
    m[:, 0], m[:, 1], m[:, 2], m[:, 3] = same & (s < t), same & (s <= t), same & (s < t), same & (s <= t)
    m[:, MASK_LOWER] = same & (t < s)
    for level in range(7):
        w = 1 << level
        m[:, MASK_LEVEL + level] = (s // (2 * w) == t // (2 * w)) & (s % (2 * w) < w) & (t % (2 * w) >= w)
    m[:, MASK_FIRST] = m[:, MASK_LEVEL].T
    m[:, MASK_CAUSAL] = s <= t
    m[:, MASK_EYE64] = (s % 64 == t) & (t < 64)
    m[:, MASK_SCAN64:MASK_SCAN64 + 2] = (np.arange(SEQ) % 64 != 0).reshape(2, P)
    m[:, MASK_SCAN128:MASK_SCAN128 + 2] = (np.arange(SEQ) % 128 != 0).reshape(2, P)
    m[:, MASK_BLOCKS] = same
    return m


def sum_features(core, weights, src, banks, n, start=0, width=T):
    with core.nc.Block() as block:
        @block.tensor
        def _(pe):
            for i in range(n):
                pe.matmul(banks[start + i][:, 0:width], weights, src[:, i, :], start=True, stop=True)


def inverse_root(core, banks, n, out, scale, eps):
    nc = core.nc
    with nc.Block() as block:
        @block.vector
        def _(dve):
            for i in range(n):
                dve.tensor_scalar(out[:, i, :], banks[i][:, 0:T], scale, eps, ALU.mult, ALU.add)
    with nc.Block() as block:
        @block.scalar
        def _(act):
            act.activation(out, out, ACT.Sqrt)
    with nc.Block() as block:
        @block.vector
        def _(dve):
            dve.reciprocal(out, out)


def rwkv_inputs(core, ctx, p, par, mask, shift_in, lora_up, gate_up, w):
    nc = core.nc
    tile4 = [P, RWKV_TILES, T]
    for name in ("logw", "gate", "kk", "b", "bonus"):
        w[name] = core.sb(ctx, name, tile4)
    w["m"] = m = p[:, 0:SHIFT_TILES, :]
    w["key"] = m[:, 4:8, :]
    with ExitStack() as local:
        diff = core.sb(local, "diff", [P, SHIFT_TILES, T])
        lora = core.sb(local, "lora", [P, 512])
        gup = core.sb(local, "gup", [P, 512])
        shift = core.sb(local, "shift", [P, SHIFT_TILES, DEC])
        hidden = core.sb(local, "hidden", [P, 2, T])
        work = core.sb(local, "work", tile4)
        rate = core.sb(local, "rate", tile4)
        key_scale = core.sb(local, "key_scale", tile4)
        with nc.Block() as block:
            @block.sync
            def _(sp):
                core.load(sp, lora, lora_up)
                core.load(sp, gup, gate_up)
                core.load(sp, shift, shift_in)
                core.wait_loads(sp)
        with nc.Block() as block:
            @block.vector
            def _(dve):
                link = Link(dve, core.dve_done)
                old = p[:, 0:SHIFT_TILES, :]
                dve.tensor_tensor(diff[:, :, 1:SEQ], old[:, :, 0:SEQ - 1], old[:, :, 1:SEQ], ALU.subtract)
                dve.tensor_scalar(diff[:, :, 0:1], old[:, :, 0:1], -1.0, None, ALU.mult)
                link(dve.tensor_tensor(diff[:, :, SEQ:T], shift, old[:, :, SEQ:T], ALU.subtract))
                for i in range(SHIFT_TILES):
                    dve.scalar_tensor_tensor(m[:, i, :], diff[:, i, :], par("mu", i), old[:, i, :],
                                             ALU.mult, ALU.add)
        with nc.Block() as block:
            @block.scalar
            def _(act):
                act.activation(hidden[0:64, 0, :], m[0:64, 12, :], ACT.Tanh)
                act.copy(hidden[64:128, 0, :], m[64:128, 12, :])
                act.activation(hidden[:, 1, :], m[:, 13, :], ACT.Sigmoid)
        with ExitStack() as ps:
            banks = core.banks(ps, "lora", 8)
            with nc.Block() as block:
                @block.tensor
                def _(pe):
                    for i in range(RWKV_TILES):
                        pe.matmul(banks[i][:, 0:T], lora[0:64, i * P:(i + 1) * P], hidden[0:64, 0, :],
                                  start=True, stop=True)
                        pe.matmul(banks[4 + i][:, 0:T], lora[64:128, i * P:(i + 1) * P], hidden[64:128, 0, :],
                                  start=True, stop=True)
            with nc.Block() as block:
                @block.scalar
                def _(act):
                    for i in range(RWKV_TILES):
                        act.activation(w["logw"][:, i, :], banks[i][:, 0:T], ACT.Sigmoid, bias=par("w0", i))
                        act.activation(rate[:, i, :], banks[4 + i][:, 0:T], ACT.Sigmoid, bias=par("a0", i))

                @block.vector
                def _(dve):
                    link = Link(dve, core.dve_done)
                    for i in range(RWKV_TILES):
                        last = dve.tensor_scalar(w["kk"][:, i, :], m[:, 4 + i, :], par("k_k", i), None, ALU.mult)
                    link(last)
                    dve.tensor_tensor(work, w["kk"], w["kk"], ALU.mult)
            with nc.Block() as block:
                @block.tensor
                def _(pe):
                    for i in range(RWKV_TILES):
                        pe.matmul(banks[i][:, 0:T], gup[:, i * P:(i + 1) * P], hidden[:, 1, :], start=True, stop=True)
                        pe.matmul(banks[4 + i][:, 0:T], core.block_ones, work[:, i, :], start=True, stop=True)

                @block.vector
                def _(dve):
                    link = Link(dve, core.dve_done)
                    dve.tensor_scalar(w["logw"], w["logw"], DECAY_SCALE, None, ALU.mult)
                    for i in range(RWKV_TILES):
                        last = dve.tensor_scalar(key_scale[:, i, :], rate[:, i, :], -1.0, par("k_a", i),
                                                 ALU.add, ALU.mult)
                    link(last)
                    dve.scalar_tensor_tensor(w["key"], key_scale, 1.0, m[:, 4:8, :], ALU.add, ALU.mult)
            with nc.Block() as block:
                @block.scalar
                def _(act):
                    for i in range(RWKV_TILES):
                        act.activation(work[:, i, :], banks[4 + i][:, 0:T], ACT.Sqrt)
                    for i in range(RWKV_TILES):
                        act.copy(w["gate"][:, i, :], banks[i][:, 0:T])
            with nc.Block() as block:
                @block.vector
                def _(dve):
                    link = Link(dve, core.dve_done)
                    link(dve.tensor_scalar(work, work, L2_EPS, None, ALU.max))
                    link(dve.reciprocal(work, work))
                    link(dve.tensor_tensor(w["kk"], w["kk"], work, ALU.mult))
                    dve.tensor_tensor(w["b"], w["kk"], rate, ALU.mult)
                    for i in range(RWKV_TILES):
                        dve.scalar_tensor_tensor(work[:, i, :], m[:, i, :], par("r_k", i), w["key"][:, i, :],
                                                 ALU.mult, ALU.mult)
            sum_features(core, core.block_ones, work, banks, RWKV_TILES)
            with nc.Block() as block:
                @block.vector
                def _(dve):
                    for i in range(RWKV_TILES):
                        dve.tensor_tensor(w["bonus"][:, i, :], banks[i][:, 0:T], m[:, 8 + i, :], ALU.mult)


def rwkv_prompt(core, mask, w, out, state_out):
    nc = core.nc
    combos = [(hp, tile, half) for hp in range(2) for tile in range(RWKV_TILES) for half in range(HALVES)]
    combo_of = {c: n for n, c in enumerate(combos)}
    with ExitStack() as ctx:
        ar = core.sb(ctx, "ar", [P, RWKV_TILES, HALVES, 2, P])
        bh = core.sb(ctx, "bh", [P, RWKV_TILES, SEQ])
        kh = core.sb(ctx, "kh", [P, RWKV_TILES, SEQ])
        end_decay = core.sb(ctx, "end_decay", [P, CHUNKS, RWKV_TILES, P])
        prompt = lambda name: w[name][:, :, 0:SEQ]
        with ExitStack() as local:
            decay = core.sb(local, "decay", [P, RWKV_TILES, SEQ])
            grow = core.sb(local, "grow", [P, RWKV_TILES, SEQ])
            before = core.sb(local, "before", [P, RWKV_TILES, SEQ])
            logs = core.sb(local, "logs", [P, RWKV_TILES, SEQ])
            with nc.Block() as block:
                @block.vector
                def _(dve):
                    link = Link(dve, core.dve_done)
                    for i in range(RWKV_TILES):
                        last = dve.tensor_tensor_scan(logs[:, i, :], mask[:, MASK_SCAN64:MASK_SCAN64 + 2, :].rearrange(
                            "p a b -> p (a b)"), w["logw"][:, i, 0:SEQ], 0.0, ALU.mult, ALU.add)
                    link(last)
                    dve.tensor_tensor(before, logs, prompt("logw"), ALU.subtract)
            with nc.Block() as block:
                @block.scalar
                def _(act):
                    act.activation(decay, logs, ACT.Exp)
                    act.activation(grow, logs, ACT.Exp, scale=-1.0)
                    act.activation(before, before, ACT.Exp)
            with nc.Block() as block:
                @block.vector
                def _(dve):
                    for i in range(RWKV_TILES):
                        split = lambda a: a.rearrange("p (h j) -> p h j", h=HALVES)
                        dve.scalar_tensor_tensor(ar[:, i, :, 0, :], split(before[:, i, :]), -1.0,
                                                 split(w["kk"][:, i, 0:SEQ]), ALU.mult, ALU.mult)
                        dve.tensor_tensor(ar[:, i, :, 1, :], split(decay[:, i, :]), split(w["m"][:, i, 0:SEQ]), ALU.mult)
                    dve.tensor_tensor(bh, grow, prompt("b"), ALU.mult)
                    dve.tensor_tensor(kh, grow, prompt("key"), ALU.mult)

                @block.gpsimd
                def _(pool):
                    for c in range(CHUNKS):
                        at = c * CHUNK + CHUNK - 1
                        pool.tensor_tensor(end_decay[:, c], decay[:, :, at:at + 1].broadcast_to((P, RWKV_TILES, P)),
                                           core.block_ones.unsqueeze(1).broadcast_to((P, RWKV_TILES, P)), ALU.mult)
        quad = core.sb(ctx, "quad", [P, 16, 4, P])
        lower = core.sb(ctx, "lower", [P, 16, P])
        tu = core.sb(ctx, "tu", [P, 16, 2, P])
        toks = core.sb(ctx, "toks", [P, 3, HALVES, 512])
        with ExitStack() as ps:
            banks = core.banks(ps, "inside", 4)
            lows = core.banks(ps, "lower", 4)
            done0, out0 = core.pe_done.at, core.dve_done.at
            with nc.Block() as block:
                @block.tensor
                def _(pe):
                    for n, (hp, tile, half) in enumerate(combos):
                        rows, cols = slice(64 * hp, 64 * hp + 64), slice(half * P, half * P + P)
                        if n >= 4:
                            pe.wait_ge(core.dve_done.sem, out0 + n - 3)
                        rhs = ar[rows, tile, half].rearrange("p a j -> p (a j)")
                        pe.matmul(banks[n % 4][:, 0:256], bh[rows, tile, cols], rhs, start=True, stop=True)
                        core.pe_done.inc(pe.matmul(banks[n % 4][:, 256:512], kh[rows, tile, cols], rhs,
                                                   start=True, stop=True))
                    for n, (hp, tile, half) in enumerate(combos):
                        rows, cols = slice(64 * hp, 64 * hp + 64), slice(half * P, half * P + P)
                        last = pe.matmul(lows[n // 4][:, (n % 4) * P:(n % 4 + 1) * P], ar[rows, tile, half, 0, :],
                                         bh[rows, tile, cols], start=True, stop=True)
                    core.pe_done.inc(last)

                @block.vector
                def _(dve):
                    for n in range(16):
                        dve.wait_ge(core.pe_done.sem, done0 + n + 1)
                        core.dve_done.inc(dve.tensor_tensor(
                            quad[:, n].rearrange("p a j -> p (a j)"), banks[n % 4][:, :],
                            mask[:, MASK_QUAD:MASK_QUAD + 4, :].rearrange("p a j -> p (a j)"), ALU.mult))
                    dve.wait_ge(core.pe_done.sem, done0 + 17)
                    for g in range(4):
                        dve.tensor_tensor(lower[:, 4 * g:4 * g + 4, :],
                                          lows[g][:, :].rearrange("p (a j) -> p a j", a=4),
                                          mask[:, MASK_LOWER:MASK_LOWER + 1, :].broadcast_to((P, 4, P)), ALU.mult)
        with ExitStack() as ps:
            banks = core.banks(ps, "turned", 6)
            done0 = core.pe_done.at
            with nc.Block() as block:
                @block.tensor
                def _(pe):
                    for kind, src in enumerate((w["m"][:, 8:12, :], bh, kh)):
                        for half in range(HALVES):
                            for tile in range(RWKV_TILES):
                                last = pe.transpose(banks[kind * 2 + half][:, tile * P:(tile + 1) * P],
                                                    src[:, tile, half * P:(half + 1) * P], core.ident)
                            core.pe_done.inc(last)

                @block.scalar
                def _(act):
                    for n in range(6):
                        act.wait_ge(core.pe_done.sem, done0 + n + 1)
                        act.copy(toks[:, n // 2, n % 2, :], banks[n][:, :])

                @block.vector
                def _(dve):
                    link = Link(dve, core.dve_done)
                    wide = lambda k: mask[:, k:k + 1, :].broadcast_to((P, 16, P))
                    dve.tensor_tensor(tu[:, :, 0, :], lower, wide(MASK_FIRST), ALU.mult)
                    link(dve.tensor_tensor(tu[:, :, 1, :], quad[:, :, 0, :], wide(MASK_LEVEL), ALU.mult))
                    eye = core.ident.unsqueeze(1).broadcast_to((P, 16, P))
                    dve.tensor_tensor(tu[:, :, 0, :], tu[:, :, 0, :], eye, ALU.add)
                    dve.tensor_tensor(tu[:, :, 1, :], tu[:, :, 1, :], eye, ALU.add)
        with ExitStack() as ps:
            part = core.sb(ps, "part", [P, 2, 16, P])
            product = lower.rearrange("p (g a) j -> p g (a j)", g=4)
            first = core.banks(ps, "first", 4)
            second = core.banks(ps, "second", 4)
            levels = 5
            part0, first0, copied0, second0, added0 = (core.pool_done.at, core.pe_done.at, core.act_done.at,
                                                       core.tile_multiplied.at, core.dve_done.at)
            with nc.Block() as block:
                @block.gpsimd
                def _(pool):
                    for level in range(levels):
                        if level >= 2:
                            pool.wait_ge(core.pe_done.sem, first0 + 4 * (level - 1))
                        core.pool_done.inc(pool.tensor_tensor(
                            part[:, level % 2], quad[:, :, 0, :],
                            mask[:, MASK_LEVEL + 1 + level:MASK_LEVEL + 2 + level, :].broadcast_to((P, 16, P)),
                            ALU.mult))

                @block.tensor
                def _(pe):
                    for level in range(levels):
                        pe.wait_ge(core.pool_done.sem, part0 + level + 1)
                        for g in range(4):
                            if level:
                                pe.wait_ge(core.dve_done.sem, added0 + (level - 1) * 8 + 2 * g + 2)
                            for c in range(4 * g, 4 * g + 4):
                                last = pe.matmul(first[g][:, (c % 4) * P:(c % 4 + 1) * P], part[:, level % 2, c, :],
                                                 tu[:, c, 0, :], start=True, stop=True)
                            core.pe_done.inc(last)
                        for g in range(4):
                            pe.wait_ge(core.act_done.sem, copied0 + level * 4 + g + 1)
                            for c in range(4 * g, 4 * g + 4):
                                n = (level * 16 + c) // 2
                                if c % 2 == 0 and n >= 4:
                                    pe.wait_ge(core.dve_done.sem, added0 + n - 3)
                                o = (c % 2) * 256
                                y = product[:, g, (c % 4) * P:(c % 4 + 1) * P]
                                pe.matmul(second[n % 4][:, o:o + P], tu[:, c, 1, :], y, start=True, stop=True)
                                last = pe.matmul(second[n % 4][:, o + P:o + 2 * P], y, tu[:, c, 1, :],
                                                 start=True, stop=True)
                                if c % 2:
                                    core.tile_multiplied.inc(last)

                @block.scalar
                def _(act):
                    for level in range(levels):
                        for g in range(4):
                            act.wait_ge(core.pe_done.sem, first0 + level * 4 + g + 1)
                            if level:
                                act.wait_ge(core.tile_multiplied.sem, second0 + (level - 1) * 8 + 2 * g + 2)
                            core.act_done.inc(act.copy(product[:, g, :], first[g][:, :]))

                @block.vector
                def _(dve):
                    for n in range(levels * 8):
                        c = (2 * n) % 16
                        dve.wait_ge(core.tile_multiplied.sem, second0 + n + 1)
                        to = tu[:, c:c + 2].rearrange("p c a j -> p (c a j)")
                        core.dve_done.inc(dve.tensor_tensor(to, second[n % 4][:, :], to, ALU.add))
        with ExitStack() as ps:
            state = core.sb(ps, "state", [P, RWKV_TILES, P])
            grown = core.sb(ps, "grown", [P, RWKV_TILES, P])
            rhs = core.sb(ps, "rhs", [P, 512])
            sa = core.sb(ps, "sa", [P, 512])
            b_rhs, b_sa, b_out, b_state = core.banks(ps, "chunk", 4)
            with nc.Block() as block:
                @block.gpsimd
                def _(pool):
                    pool.memset(state, 0.0)
                    pool.memset(rhs, 0.0)
                    pool.memset(sa, 0.0)
            pe0, act0, dve0 = core.pe_done.at, core.act_done.at, core.dve_done.at
            v_tok, b_tok, k_tok = 0, 1, 2
            with nc.Block() as block:
                @block.tensor
                def _(pe):
                    for c in range(CHUNKS):
                        half, base = c // 2, CHUNK * (c % 2)
                        at = slice(base, base + CHUNK)
                        if c:
                            pe.wait_ge(core.dve_done.sem, dve0 + 2 * c)
                        for tile in range(RWKV_TILES):
                            pe.matmul(b_rhs[at, tile * P:(tile + 1) * P], ar[:, tile, half, 0, at], state[:, tile, :],
                                      start=True, stop=False, skip_group_check=True)
                            for hp in range(2):
                                cols = slice(tile * P + 64 * hp, tile * P + 64 * hp + 64)
                                last = pe.matmul(b_rhs[at, cols], quad[:, combo_of[hp, tile, half], 2, at],
                                                 toks[:, v_tok, half, cols], start=False, stop=hp == 1,
                                                 skip_group_check=True)
                        core.pe_done.inc(last)
                        pe.wait_ge(core.act_done.sem, act0 + 3 * c + 1)
                        for tile in range(RWKV_TILES):
                            for hp in range(2):
                                cols = slice(tile * P + 64 * hp, tile * P + 64 * hp + 64)
                                last = pe.matmul(b_sa[at, cols], tu[:, combo_of[hp, tile, half], 1, at], rhs[:, cols],
                                                 start=True, stop=True)
                        core.pe_done.inc(last)
                        pe.wait_ge(core.act_done.sem, act0 + 3 * c + 2)
                        for tile in range(RWKV_TILES):
                            cols = slice(tile * P, (tile + 1) * P)
                            pe.matmul(b_state[:, cols], toks[at, b_tok, half, cols], sa[at, cols],
                                      start=True, stop=False)
                            last = pe.matmul(b_state[:, cols], toks[at, k_tok, half, cols],
                                             toks[at, v_tok, half, cols], start=False, stop=True)
                        core.pe_done.inc(last)
                        for tile in range(RWKV_TILES):
                            to = slice(tile * CHUNK, (tile + 1) * CHUNK)
                            pe.matmul(b_out[:, to], state[:, tile, :], ar[:, tile, half, 1, at],
                                      start=True, stop=False, skip_group_check=True)
                            for hp in range(2):
                                cols = slice(tile * P + 64 * hp, tile * P + 64 * hp + 64)
                                head = slice(64 * hp, 64 * hp + 64)
                                n = combo_of[hp, tile, half]
                                pe.matmul(b_out[head, to], sa[:, cols], quad[:, n, 1, at],
                                          start=False, stop=False, skip_group_check=True)
                                last = pe.matmul(b_out[head, to], toks[:, v_tok, half, cols], quad[:, n, 3, at],
                                                 start=False, stop=True, skip_group_check=True)
                        core.pe_done.inc(last)

                @block.scalar
                def _(act):
                    for c in range(CHUNKS):
                        at = slice(CHUNK * (c % 2), CHUNK * (c % 2) + CHUNK)
                        act.wait_ge(core.pe_done.sem, pe0 + 4 * c + 1)
                        core.act_done.inc(act.copy(rhs[at, :], b_rhs[at, :]))
                        act.wait_ge(core.pe_done.sem, pe0 + 4 * c + 2)
                        core.act_done.inc(act.copy(sa[at, :], b_sa[at, :]))
                        act.wait_ge(core.pe_done.sem, pe0 + 4 * c + 4)
                        core.act_done.inc(act.copy(out[:, 0:4, c * CHUNK:(c + 1) * CHUNK],
                                                   b_out[:, 0:256].rearrange("p (a j) -> p a j", a=4)))

                @block.vector
                def _(dve):
                    for c in range(CHUNKS):
                        dve.wait_ge(core.pe_done.sem, pe0 + 4 * c + 3)
                        link = Link(dve, core.dve_done)
                        link(dve.tensor_tensor(grown, b_state[:, :].rearrange("p (a j) -> p a j", a=4), state, ALU.add))
                        dve.wait_ge(core.pe_done.sem, pe0 + 4 * c + 4)
                        core.dve_done.inc(dve.tensor_tensor(state, grown, end_decay[:, c], ALU.mult))
            with nc.Block() as block:
                @block.sync
                def _(sp):
                    core.stored.inc(sp.dma_start(state_out, state), 16)
                    sp.wait_ge(core.stored.sem, core.stored.at)


def rwkv_sample(core, mask, w, out, state_in, state_out):
    nc = core.nc
    wide = [P, RWKV_TILES, DEC, 64]
    with ExitStack() as ctx:
        state = core.sb(ctx, "state", wide)
        new = core.sb(ctx, "new", wide)
        work = core.sb(ctx, "work", wide)
        values = core.sb(ctx, "values", wide)
        decay = core.sb(ctx, "decay", [P, RWKV_TILES, DEC])
        reads = core.banks(ctx, "reads", 4)
        spread = core.banks(ctx, "spread", 4)
        each = lambda a: a.unsqueeze(3).broadcast_to(tuple(wide))
        sample = lambda name: each(w[name][:, :, SEQ:T])
        mixed = lambda i: each(w["m"][:, i:i + 4, SEQ:T])
        eye = mask[:, MASK_EYE64, 0:64].unsqueeze(1).unsqueeze(1).broadcast_to(tuple(wide))
        got = lambda bank: bank[:, :].rearrange("p (b v) -> p b v", b=DEC)
        flat = lambda a, tile: a[:, tile].rearrange("p b v -> p (b v)")
        with nc.Block() as block:
            @block.sync
            def _(sp):
                core.load(sp, state, state_in)

            @block.scalar
            def _(act):
                act.activation(decay, w["logw"][:, :, SEQ:T], ACT.Exp)

            @block.vector
            def _(dve):
                dve.tensor_tensor(values, eye, mixed(8), ALU.mult)
                core.wait_loads(dve)
                dve.tensor_tensor(work, state, sample("kk"), ALU.mult)
        with nc.Block() as block:
            @block.tensor
            def _(pe):
                for tile in range(RWKV_TILES):
                    pe.matmul(reads[tile][:, :], core.block_ones, flat(work, tile), start=True, stop=True)
                    pe.matmul(spread[tile][:, :], core.block_ones, flat(values, tile), start=True, stop=True)

            @block.vector
            def _(dve):
                dve.tensor_tensor(new, state, each(decay), ALU.mult)
        with nc.Block() as block:
            @block.vector
            def _(dve):
                link = Link(dve, core.dve_done)
                for tile in range(RWKV_TILES):
                    dve.tensor_tensor(work[:, tile], got(reads[tile]), sample("b")[:, tile], ALU.mult)
                    last = dve.tensor_tensor(values[:, tile], got(spread[tile]), sample("key")[:, tile], ALU.mult)
                link(last)
                link(dve.tensor_tensor(new, new, work, ALU.subtract))
                link(dve.tensor_tensor(new, new, values, ALU.add))
                dve.tensor_tensor(work, new, mixed(0), ALU.mult)
        with nc.Block() as block:
            @block.tensor
            def _(pe):
                for tile in range(RWKV_TILES):
                    pe.matmul(reads[tile][:, :], core.block_ones, flat(work, tile), start=True, stop=True)

            @block.sync
            def _(sp):
                core.stored.inc(sp.dma_start(state_out, new), 16)
                sp.wait_ge(core.stored.sem, core.stored.at)
        with nc.Block() as block:
            @block.vector
            def _(dve):
                link = Link(dve, core.dve_done)
                for tile in range(RWKV_TILES):
                    last = dve.tensor_tensor(values[:, tile], got(reads[tile]), eye[:, tile], ALU.mult)
                link(last)
                dve.tensor_reduce(out[:, 0:4, SEQ:T], values, AX_X, ALU.add)


def rwkv_output(core, par, w, out):
    nc = core.nc
    o = out[:, 0:4, :]
    with ExitStack() as ctx:
        work = core.sb(ctx, "work", [P, RWKV_TILES, T])
        rstd = core.sb(ctx, "rstd", [P, RWKV_TILES, T])
        banks = core.banks(ctx, "norm", 4)
        sum_features(core, core.block_ones, o, banks, RWKV_TILES)
        with nc.Block() as block:
            @block.vector
            def _(dve):
                link = Link(dve, core.dve_done)
                for i in range(RWKV_TILES):
                    last = dve.scalar_tensor_tensor(out[:, i, :], banks[i][:, 0:T], -1.0 / 64, out[:, i, :],
                                                    ALU.mult, ALU.add)
                link(last)
                dve.tensor_tensor(work, o, o, ALU.mult)
        sum_features(core, core.block_ones, work, banks, RWKV_TILES)
        inverse_root(core, banks, RWKV_TILES, rstd, 1.0 / 64, GN_EPS)
        with nc.Block() as block:
            @block.vector
            def _(dve):
                link = Link(dve, core.dve_done)
                link(dve.tensor_tensor(o, o, rstd, ALU.mult))
                for i in range(RWKV_TILES):
                    last = dve.tensor_scalar(out[:, i, :], out[:, i, :], par("gn_w", i), par("gn_b", i),
                                             ALU.mult, ALU.add)
                link(last)
                link(dve.tensor_tensor(o, o, w["bonus"], ALU.add))
                dve.tensor_tensor(o, o, w["gate"], ALU.mult)


HGRN_TILES = 4
LEVELS = 7
SMALLEST_LOG = 1.0842021724855044e-19


def hgrn_prompt(core, mask, values, q, key, logs, out, state_out):
    nc = core.nc
    flat = lambda a: a.rearrange("p t n -> p (t n)")
    with ExitStack() as ctx:
        att = core.sb(ctx, "att", [P, HALVES, HGRN_TILES, P])
        with ExitStack() as local:
            gap = core.sb(local, "gap", [P, 2, HGRN_TILES * SEQ])
            left = core.sb(local, "left", [P, 2, HGRN_TILES, SEQ])
            right = core.sb(local, "right", [P, 2, HGRN_TILES, SEQ])
            masked = core.sb(local, "masked", [P, 2, HALVES, HGRN_TILES, P])
            banks = core.banks(local, "level", 4)
            with nc.Block() as block:
                @block.gpsimd
                def _(pool):
                    pool.memset(left, 0.0)
                    pool.memset(right, 0.0)
            gap0, exp0, scaled0, mult0 = core.dve_done.at, core.act_done.at, core.tile_evicted.at, core.pe_done.at
            masked0, added0 = core.tile_multiplied.at, core.pool_done.at
            with nc.Block() as block:
                @block.vector
                def _(dve):
                    def gaps(level):
                        w = 1 << level
                        if level >= 2:
                            dve.wait_ge(core.tile_evicted.sem, scaled0 + level - 1)
                        g = flat(logs).rearrange("p (n j) -> p n j", j=2 * w)
                        to = gap[:, level % 2, :].rearrange("p (n j) -> p n j", j=2 * w)
                        middle = g[:, :, w - 1:w].broadcast_to((P, HGRN_TILES * SEQ // (2 * w), w))
                        dve.tensor_tensor(to[:, :, 0:w], middle, g[:, :, 0:w], ALU.subtract)
                        core.dve_done.inc(dve.tensor_tensor(to[:, :, w:2 * w], g[:, :, w:2 * w], middle, ALU.subtract))

                    def scale(level):
                        w, slot = 1 << level, level % 2
                        dve.wait_ge(core.act_done.sem, exp0 + level + 1)
                        if level >= 2:
                            dve.wait_ge(core.pe_done.sem, mult0 + 1 + level - 1)
                        cut = lambda a: a.rearrange("p (n j) -> p n j", j=2 * w)
                        e = cut(gap[:, slot, :])
                        dve.tensor_tensor(cut(flat(left[:, slot]))[:, :, 0:w], cut(flat(key))[:, :, 0:w],
                                          e[:, :, 0:w], ALU.mult)
                        core.tile_evicted.inc(dve.tensor_tensor(
                            cut(flat(right[:, slot]))[:, :, w:2 * w], cut(flat(q))[:, :, w:2 * w],
                            e[:, :, w:2 * w], ALU.mult))

                    def cover(level, to, which):
                        slot = (level + 1) % 2
                        dve.wait_ge(core.pe_done.sem, mult0 + level + 2)
                        if level >= 2:
                            dve.wait_ge(core.pool_done.sem, added0 + level - 1)
                        for half in range(HALVES):
                            last = dve.tensor_tensor(to[:, half], banks[2 * slot + half][:, :].rearrange(
                                "p (a j) -> p a j", a=4), which.broadcast_to((P, 4, P)), ALU.mult)
                        core.tile_multiplied.inc(last)

                    gaps(0)
                    cover(-1, att, core.ident.unsqueeze(1))
                    gaps(1)
                    for level in range(LEVELS):
                        scale(level)
                        if level + 2 < LEVELS:
                            gaps(level + 2)
                        if level:
                            cover(level - 1, masked[:, (level - 1) % 2],
                                  mask[:, MASK_LEVEL + level - 1:MASK_LEVEL + level, :])
                    cover(LEVELS - 1, masked[:, (LEVELS - 1) % 2], mask[:, MASK_LEVEL + LEVELS - 1:MASK_LEVEL + LEVELS, :])

                @block.scalar
                def _(act):
                    for level in range(LEVELS):
                        act.wait_ge(core.dve_done.sem, gap0 + level + 1)
                        core.act_done.inc(act.activation(gap[:, level % 2, :], gap[:, level % 2, :], ACT.Exp))

                @block.tensor
                def _(pe):
                    for n in range(LEVELS + 1):
                        if n:
                            pe.wait_ge(core.tile_evicted.sem, scaled0 + n)
                        if n >= 2:
                            pe.wait_ge(core.tile_multiplied.sem, masked0 + n - 1)
                        for half in range(HALVES):
                            for tile in range(HGRN_TILES):
                                cols = slice(half * P, (half + 1) * P)
                                a, b = (key, q) if n == 0 else (left[:, (n - 1) % 2], right[:, (n - 1) % 2])
                                last = pe.matmul(banks[2 * (n % 2) + half][:, tile * P:(tile + 1) * P],
                                                 a[:, tile, cols], b[:, tile, cols], start=True, stop=True)
                        core.pe_done.inc(last)

                @block.gpsimd
                def _(pool):
                    for level in range(LEVELS):
                        pool.wait_ge(core.tile_multiplied.sem, masked0 + level + 2)
                        if level:
                            pool.wait_ge(core.pool_done.sem, added0 + level)
                        core.pool_done.inc(pool.tensor_tensor(att, att, masked[:, level % 2], ALU.add))
        decay = core.sb(ctx, "decay", [P, HGRN_TILES, SEQ])
        late = core.sb(ctx, "late", [P, HGRN_TILES, SEQ])
        toks = core.sb(ctx, "toks", [P, 2, HALVES, 512])
        state = core.sb(ctx, "state", [P, HGRN_TILES, P])
        halves = lambda a: a.rearrange("p t (h j) -> p (t h) j", h=HALVES)
        with nc.Block() as block:
            @block.vector
            def _(dve):
                g = halves(logs)
                dve.tensor_tensor(halves(late), g[:, :, P - 1:P].broadcast_to((P, 8, P)), g, ALU.subtract)
        with nc.Block() as block:
            @block.scalar
            def _(act):
                act.activation(decay, logs, ACT.Exp)
                act.activation(late, late, ACT.Exp)
        with nc.Block() as block:
            @block.vector
            def _(dve):
                dve.tensor_tensor(late, late, key, ALU.mult)
                dve.tensor_tensor(q, q, decay, ALU.mult)
        turned = core.banks(ctx, "turned", 4)
        done0 = core.pe_done.at
        with nc.Block() as block:
            @block.tensor
            def _(pe):
                for kind, src in enumerate((values, late)):
                    for half in range(HALVES):
                        for tile in range(HGRN_TILES):
                            last = pe.transpose(turned[kind * 2 + half][:, tile * P:(tile + 1) * P],
                                                src[:, tile, half * P:(half + 1) * P], core.ident)
                        core.pe_done.inc(last)

            @block.scalar
            def _(act):
                for n in range(4):
                    act.wait_ge(core.pe_done.sem, done0 + n + 1)
                    act.copy(toks[:, n // 2, n % 2, :], turned[n][:, :])
        b_out = core.banks(ctx, "outputs", 2)
        b_state = core.banks(ctx, "states", 2)
        done0, first_state = core.pe_done.at, core.dve_done.at
        with nc.Block() as block:
            @block.tensor
            def _(pe):
                for half in range(HALVES):
                    for tile in range(HGRN_TILES):
                        cols = slice(tile * P, (tile + 1) * P)
                        last = pe.matmul(b_state[half][:, cols], toks[:, 1, half, cols], toks[:, 0, half, cols],
                                         start=True, stop=True)
                    core.pe_done.inc(last)
                for half in range(HALVES):
                    if half:
                        pe.wait_ge(core.dve_done.sem, first_state + 1)
                    for tile in range(HGRN_TILES):
                        cols = slice(tile * P, (tile + 1) * P)
                        last = pe.matmul(b_out[half][:, cols], toks[:, 0, half, cols], att[:, half, tile, :],
                                         start=True, stop=half == 0)
                        if half:
                            last = pe.matmul(b_out[half][:, cols], state[:, tile, :], q[:, tile, half * P:(half + 1) * P],
                                             start=False, stop=True)
                    core.pe_done.inc(last)

            @block.vector
            def _(dve):
                dve.wait_ge(core.pe_done.sem, done0 + 1)
                core.dve_done.inc(dve.tensor_copy(state, b_state[0][:, :].rearrange("p (a j) -> p a j", a=4)))
                dve.wait_ge(core.pe_done.sem, done0 + 4)
                for tile in range(HGRN_TILES):
                    dve.scalar_tensor_tensor(state[:, tile, :], state[:, tile, :], decay[:, tile, SEQ - 1:SEQ],
                                             b_state[1][:, tile * P:(tile + 1) * P], ALU.mult, ALU.add)

            @block.scalar
            def _(act):
                for half in range(HALVES):
                    act.wait_ge(core.pe_done.sem, done0 + 3 + half)
                    act.copy(out[:, 4:8, half * P:(half + 1) * P],
                             b_out[half][:, :].rearrange("p (a j) -> p a j", a=4))
        with nc.Block() as block:
            @block.sync
            def _(sp):
                core.stored.inc(sp.dma_start(state_out, state), 16)
                sp.wait_ge(core.stored.sem, core.stored.at)


def hgrn_sample(core, values, q, key, forget, out, state_in, state_out):
    nc = core.nc
    wide = [P, HGRN_TILES, DEC, P]
    with ExitStack() as ctx:
        state = core.sb(ctx, "state", wide)
        work = core.sb(ctx, "work", wide)
        each = lambda a: a.unsqueeze(3).broadcast_to(tuple(wide))
        with ExitStack() as ps:
            banks = core.banks(ps, "spread", 8)
            done0 = core.pe_done.at
            with nc.Block() as block:
                @block.sync
                def _(sp):
                    core.load(sp, state, state_in)
                @block.tensor
                def _(pe):
                    for n in range(8):
                        for s in range(4 * n, 4 * n + 4):
                            last = pe.matmul(banks[n][:, (s % 4) * P:(s % 4 + 1) * P],
                                             values[:, s // DEC, s % DEC:s % DEC + 1].broadcast_to((P, P)),
                                             core.ident, start=True, stop=True)
                        core.pe_done.inc(last)

                @block.vector
                def _(dve):
                    core.wait_loads(dve)
                    link = Link(dve, core.dve_done)
                    link(dve.tensor_tensor(state, state, each(forget), ALU.mult))
                    for n in range(8):
                        dve.wait_ge(core.pe_done.sem, done0 + n + 1)
                        tile, b = n // 2, 4 * (n % 2)
                        last = dve.tensor_tensor(work[:, tile, b:b + 4, :], banks[n][:, :].rearrange(
                            "p (b v) -> p b v", b=4), each(key)[:, tile, b:b + 4, :], ALU.mult)
                    link(last)
                    dve.tensor_tensor(state, state, work, ALU.add)
        (bank,) = core.banks(ctx, "reads", 1)
        with nc.Block() as block:
            @block.tensor
            def _(pe):
                for s in range(HGRN_TILES * DEC):
                    pe.matmul(bank[:, s:s + 1], state[:, s // DEC, s % DEC, :], q[:, s // DEC, s % DEC:s % DEC + 1],
                              start=True, stop=True)

            @block.sync
            def _(sp):
                core.stored.inc(sp.dma_start(state_out, state), 16)
                sp.wait_ge(core.stored.sem, core.stored.at)
        with nc.Block() as block:
            @block.vector
            def _(dve):
                dve.tensor_copy(out[:, 4:8, SEQ:T], bank[:, 0:HGRN_TILES * DEC].rearrange("p (a b) -> p a b", b=DEC))


def hgrn(core, par, mask, p, out, state_in, prompt_state, sample_state):
    nc = core.nc
    whole = [P, HGRN_TILES, T]
    prompt = [P, HGRN_TILES, SEQ]
    with ExitStack() as ctx:
        gate = core.sb(ctx, "out_gate", whole)
        q = core.sb(ctx, "q", prompt)
        key = core.sb(ctx, "key", prompt)
        logs = core.sb(ctx, "logs", prompt)
        small = core.sb(ctx, "small", [P, 3, HGRN_TILES, DEC])
        with ExitStack() as local:
            forget = core.sb(local, "forget", whole)
            logf = core.sb(local, "logf", prompt)
            bound = core.sb(local, "bound", [P, 4, HGRN_TILES])
            with nc.Block() as block:
                @block.scalar
                def _(act):
                    act.activation(gate, p[:, 26:30, :], ACT.Silu)
                    act.activation(q, p[:, 14:18, 0:SEQ], ACT.Silu)
                    act.activation(small[:, 0], p[:, 14:18, SEQ:T], ACT.Silu)
                    act.activation(forget, p[:, 18:22, :], ACT.Sigmoid)

                @block.vector
                def _(dve):
                    dve.tensor_tensor(bound[:, 0], par("bound"), par("bound"), ALU.subtract)
            with nc.Block() as block:
                @block.scalar
                def _(act):
                    act.activation(bound[:, 1], bound[:, 0], ACT.Exp)
            with nc.Block() as block:
                @block.vector
                def _(dve):
                    link = Link(dve, core.dve_done)
                    link(dve.reciprocal(bound[:, 0], bound[:, 1]))
                    link(dve.tensor_tensor(bound[:, 0], bound[:, 0], bound[:, 1], ALU.mult))
                    link(dve.tensor_tensor(bound[:, 2], bound[:, 0], bound[:, 0], ALU.subtract))
                    link(dve.tensor_scalar(bound[:, 3], bound[:, 2], -1.0, 1.0, ALU.mult, ALU.add))
                    for i in range(HGRN_TILES):
                        last = dve.tensor_scalar(forget[:, i, :], forget[:, i, :], bound[:, 3, i:i + 1],
                                                 bound[:, 2, i:i + 1], ALU.mult, ALU.add)
                    link(last)
                    dve.tensor_scalar(key, forget[:, :, 0:SEQ], -1.0, 1.0, ALU.mult, ALU.add)
                    dve.tensor_scalar(small[:, 1], forget[:, :, SEQ:T], -1.0, 1.0, ALU.mult, ALU.add)
                    dve.tensor_copy(small[:, 2], forget[:, :, SEQ:T])
                    dve.tensor_scalar(logf, forget[:, :, 0:SEQ], SMALLEST_LOG, None, ALU.max)
            with nc.Block() as block:
                @block.scalar
                def _(act):
                    act.activation(logf, logf, ACT.Ln)
            with nc.Block() as block:
                @block.vector
                def _(dve):
                    for i in range(HGRN_TILES):
                        dve.tensor_tensor_scan(logs[:, i, :], mask[:, MASK_SCAN128:MASK_SCAN128 + 2, :].rearrange(
                            "p a b -> p (a b)"), logf[:, i, :], 0.0, ALU.mult, ALU.add)
        hgrn_sample(core, p[:, 22:26, SEQ:T], small[:, 0], small[:, 1], small[:, 2], out, state_in, sample_state)
        hgrn_prompt(core, mask, p[:, 22:26, 0:SEQ], q, key, logs, out, prompt_state)
        work = core.sb(ctx, "work", whole)
        rstd = core.sb(ctx, "rstd", whole)
        banks = core.banks(ctx, "norm", 4)
        with nc.Block() as block:
            @block.scalar
            def _(act):
                act.activation(work, out[:, 4:8, :], ACT.Square)
        sum_features(core, core.ones, work, banks, HGRN_TILES)
        inverse_root(core, banks, HGRN_TILES, rstd, 1.0 / P, RMS_EPS)
        with nc.Block() as block:
            @block.vector
            def _(dve):
                link = Link(dve, core.dve_done)
                for i in range(HGRN_TILES):
                    last = dve.scalar_tensor_tensor(out[:, 4 + i, :], out[:, 4 + i, :], par("hgrn_norm", 0),
                                                    rstd[:, i, :], ALU.mult, ALU.mult)
                link(last)
                dve.tensor_tensor(out[:, 4:8, :], out[:, 4:8, :], gate, ALU.mult)


def mixer_ab(core, x, d, norm, w_in, then=None):
    nc = core.nc
    w_out = Stream(d["ab_w_out"])
    with ExitStack() as ctx:
        mask = core.sb(ctx, "mask", [P, MASKS, P])
        params = core.sb(ctx, "params", [P, AB_PARAMS])

        def par(name, i=None):
            at = AB_PARAM[name]
            return params[:, at] if i is None else params[:, at.start + i:at.start + i + 1]

        p = core.sb(ctx, "p", [P, AB_TILES, T])
        out = core.sb(ctx, "mixer_out", [P, KC, T])
        with nc.Block() as block:
            @block.sync
            def _(sp):
                core.load(sp, params, d["ab_params"])
                core.load(sp, mask, d["masks"])
        core.block_ones = mask[:, MASK_BLOCKS, :]
        with ExitStack() as local:
            h = core.sb(local, "mix_in", [P, KC, T])
            h_hi = core.sb(local, "mix_in_hi", [P, KC, T], F32R)
            h_lo = core.sb(local, "mix_in_lo", [P, KC, T], F32R)
            rms_norm(core, x, norm, h)
            split(core, h, h_hi, h_lo)
            project(core, Weights(core, local), w_in, AB_TILES, h_hi, h_lo, p, then=w_out)
        with nc.Block() as block:
            @block.sync
            def _(sp):
                core.wait_loads(sp)
                core.stored.inc(sp.dma_start(d["last_shift"], p[:, 0:SHIFT_TILES, SEQ - 1:T]), 16)
                sp.wait_ge(core.stored.sem, core.stored.at)
        with ExitStack() as local:
            w = {}
            rwkv_inputs(core, local, p, par, mask, d["shift_in"], d["lora_up"], d["gate_up"], w)
            rwkv_sample(core, mask, w, out, d["rwkv_in"], d["rwkv_sample"])
            rwkv_prompt(core, mask, w, out, d["rwkv_prompt"])
            rwkv_output(core, par, w, out)
        hgrn(core, par, mask, p, out, d["hgrn_in"], d["hgrn_prompt"], d["hgrn_sample"])
        with ExitStack() as local:
            out_hi = core.sb(local, "out_hi", [P, KC, T], F32R)
            out_lo = core.sb(local, "out_lo", [P, KC, T], F32R)
            split(core, out, out_hi, out_lo)
            project(core, Weights(core, local), w_out, KC, out_hi, out_lo, x, residual=True, then=then)


HEADS = 32
GROUPS = 4
INNER_TILES = 16
CONV_TILES = 24
SSM_TILES = INNER_TILES + CONV_TILES
INNER = INNER_TILES * P
TAPS = 4
SSM_PARAM = {}
_at = 0
for _name, _n in (("norm", 8), ("conv_w", TAPS * CONV_TILES), ("conv_b", CONV_TILES), ("out_norm", INNER_TILES),
                  ("skip", INNER_TILES)):
    SSM_PARAM[_name] = slice(_at, _at + _n)
    _at += _n
SSM_PARAMS = _at
SSM_OUT = {"conv_prompt": (P, CONV_TILES, TAPS - 1), "conv_sample": (P, CONV_TILES, TAPS - 1, DEC),
           "ssm_prompt": (P, INNER), "ssm_sample": (P, DEC, INNER)}


def ssm_steps(core, h, w_dt, heads_in, mask, dt, log_a, log_sum):
    nc = core.nc
    row = [HEADS, T]
    with ExitStack() as ctx:
        weights = core.sb(ctx, "w_dt", [P, KC, HEADS])
        heads = core.sb(ctx, "heads", [HEADS, 2])
        rate = core.sb(ctx, "rate", [HEADS, 1])
        z = core.sb(ctx, "z", row)
        u = core.sb(ctx, "u", row)
        r = core.sb(ctx, "r", row)
        square = core.sb(ctx, "square", row)
        series = core.sb(ctx, "series", row)
        (bank,) = core.banks(ctx, "dt", 1)
        with nc.Block() as block:
            @block.sync
            def _(sp):
                core.load(sp, weights, w_dt)
                core.load(sp, heads, heads_in)

            @block.tensor
            def _(pe):
                core.wait_loads(pe)
                for k in range(KC):
                    pe.matmul(bank[0:HEADS, 0:T], weights[:, k, :], h[:, k, :], start=k == 0, stop=k == KC - 1)
        with nc.Block() as block:
            @block.vector
            def _(dve):
                link = Link(dve, core.dve_done)
                link(dve.tensor_scalar(z, bank[0:HEADS, 0:T], heads[:, 0:1], None, ALU.add))
                link(dve.tensor_scalar(r, z, -1.0, None, ALU.mult))
                dve.tensor_tensor(u, z, r, ALU.max)

            @block.scalar
            def _(act):
                act.activation(rate, heads[:, 1:2], ACT.Exp)
        with nc.Block() as block:
            @block.scalar
            def _(act):
                act.activation(u, u, ACT.Exp, scale=-1.0)
        with nc.Block() as block:
            @block.vector
            def _(dve):
                link = Link(dve, core.dve_done)
                link(dve.tensor_scalar(r, u, 2.0, None, ALU.add))
                link(dve.reciprocal(r, r))
                link(dve.tensor_tensor(r, r, u, ALU.mult))
                link(dve.tensor_tensor(square, r, r, ALU.mult))
                link(dve.tensor_scalar(series, square, 1.0 / 17, None, ALU.mult))
                for n in range(15, 1, -2):
                    link(dve.scalar_tensor_tensor(series, series, 1.0 / n, square, ALU.add, ALU.mult))
                link(dve.scalar_tensor_tensor(series, series, 1.0, r, ALU.add, ALU.mult))
                link(dve.tensor_scalar(z, z, 0.0, None, ALU.max))
                link(dve.scalar_tensor_tensor(dt, series, 2.0, z, ALU.mult, ALU.add))
                link(dve.tensor_scalar(log_a, dt, rate, -1.0, ALU.mult, ALU.mult))
                dve.tensor_tensor_scan(log_sum, mask[0:HEADS, MASK_SCAN128:MASK_SCAN128 + 2, :].rearrange(
                    "p a b -> p (a b)"), log_a[:, 0:SEQ], 0.0, ALU.mult, ALU.add)


def ssm_conv(core, par, p, c, conv_in, conv_prompt, conv_sample):
    nc = core.nc
    with ExitStack() as ctx:
        rows = core.sb(ctx, "conv_rows", [P, CONV_TILES, TAPS - 1, DEC])
        term = core.sb(ctx, "term", [P, TAPS - 1, CONV_TILES, DEC])
        x = p[:, INNER_TILES:SSM_TILES, :]
        tap = lambda j, i: par("conv_w", j * CONV_TILES + i)
        with nc.Block() as block:
            @block.sync
            def _(sp):
                core.load(sp, rows, conv_in)
                core.stored.inc(sp.dma_start(conv_prompt, x[:, :, SEQ - 3:SEQ]), 16)
                core.stored.inc(sp.dma_start(conv_sample[:, :, 2, :], x[:, :, SEQ:T]), 16)
                core.wait_loads(sp)
                core.stored.inc(sp.dma_start(conv_sample[:, :, 0:2, :], rows[:, :, 1:3, :]), 16)
                sp.wait_ge(core.stored.sem, core.stored.at)

            @block.scalar
            def _(act):
                for i in range(CONV_TILES):
                    act.activation(c[:, i, :], x[:, i, :], ACT.Identity, bias=par("conv_b", i), scale=tap(3, i))
        with nc.Block() as block:
            @block.vector
            def _(dve):
                link = Link(dve, core.dve_done)
                for back in range(1, TAPS):
                    for i in range(CONV_TILES):
                        last = dve.scalar_tensor_tensor(c[:, i, back:SEQ], x[:, i, 0:SEQ - back], tap(3 - back, i),
                                                        c[:, i, back:SEQ], ALU.mult, ALU.add)
                    link(last)

            @block.gpsimd
            def _(pool):
                link = Link(pool, core.pool_done)
                for j in range(TAPS - 1):
                    w = par("conv_w")[:, j * CONV_TILES:(j + 1) * CONV_TILES].unsqueeze(2)
                    link(pool.tensor_tensor(term[:, j], rows[:, :, j, :], w.broadcast_to((P, CONV_TILES, DEC)),
                                            ALU.mult))
                for j in range(TAPS - 1):
                    link(pool.tensor_tensor(c[:, :, SEQ:T], c[:, :, SEQ:T], term[:, j], ALU.add))
        with nc.Block() as block:
            @block.scalar
            def _(act):
                act.activation(c, c, ACT.Silu)


def ssm_sample(core, c, xdt, log_a, y, state_in, state_out):
    nc = core.nc
    slots = 3
    with ExitStack() as ctx:
        ring = core.sb(ctx, "states", [P, slots, INNER])
        a = core.sb(ctx, "a", [HEADS, DEC])
        diagonal = core.sb(ctx, "diagonal", [HEADS, DEC, HEADS])
        a_all = core.sb(ctx, "a_all", [P, DEC, HEADS])
        spread = core.banks(ctx, "spread", 4)
        reads, decays = core.banks(ctx, "reads", 2)
        with nc.Block() as block:
            @block.scalar
            def _(act):
                act.activation(a, log_a[:, SEQ:T], ACT.Exp)
        with nc.Block() as block:
            @block.vector
            def _(dve):
                dve.tensor_tensor(diagonal, a.unsqueeze(2).broadcast_to((HEADS, DEC, HEADS)),
                                  core.ident[0:HEADS, 0:HEADS].unsqueeze(1).broadcast_to((HEADS, DEC, HEADS)), ALU.mult)
        with nc.Block() as block:
            @block.tensor
            def _(pe):
                pe.matmul(decays[:, 0:DEC * HEADS], core.ones[0:HEADS, :], diagonal.rearrange("p b h -> p (b h)"),
                          start=True, stop=True)
        with nc.Block() as block:
            @block.scalar
            def _(act):
                act.copy(a_all, decays[:, 0:DEC * HEADS].rearrange("p (b h) -> p b h", b=DEC))
        loaded0 = [k.at for k in core.state_loaded]
        stored0 = [k.at for k in core.state_stored]
        decayed0, spread0, updated0, read0 = (core.pool_done.at, core.pe_done.at, core.dve_done.at,
                                              core.tile_multiplied.at)
        with nc.Block() as block:
            @block.sync
            def _(sp):
                def load(b):
                    if b >= slots:
                        sp.wait_ge(core.state_stored[b % slots].sem, stored0[b % slots] + 16 * (b // slots))
                        sp.wait_ge(core.tile_multiplied.sem, read0 + b - slots + 1)
                    core.state_loaded[b % slots].inc(sp.dma_start(ring[:, b % slots, :], state_in[:, b, :]), 16)

                for b in range(slots - 1):
                    load(b)
                for b in range(DEC):
                    if b + slots - 1 < DEC:
                        load(b + slots - 1)
                    sp.wait_ge(core.dve_done.sem, updated0 + b + 1)
                    core.state_stored[b % slots].inc(sp.dma_start(state_out[:, b, :], ring[:, b % slots, :]), 16)
                for k in range(slots):
                    sp.wait_ge(core.state_stored[k].sem, core.state_stored[k].at)

            @block.gpsimd
            def _(pool):
                for b in range(DEC):
                    pool.wait_ge(core.state_loaded[b % slots].sem, loaded0[b % slots] + 16 * (b // slots + 1))
                    s = ring[:, b % slots, :].rearrange("p (h v) -> p h v", h=HEADS)
                    core.pool_done.inc(pool.tensor_tensor(
                        s, s, a_all[:, b, :].unsqueeze(2).broadcast_to((P, HEADS, 64)), ALU.mult))

            @block.tensor
            def _(pe):
                def rows(b):
                    for g in range(GROUPS):
                        if b:
                            pe.wait_ge(core.dve_done.sem, updated0 + b)
                        for tile in range(4 * g, 4 * g + 4):
                            last = pe.matmul(spread[g][:, (tile % 4) * P:(tile % 4 + 1) * P],
                                             xdt[:, tile, SEQ + b:SEQ + b + 1].broadcast_to((P, P)), core.ident,
                                             start=True, stop=True)
                    core.pe_done.inc(last)

                def outputs(b):
                    pe.wait_ge(core.dve_done.sem, updated0 + b + 1)
                    for tile in range(INNER_TILES):
                        last = pe.matmul(reads[:, tile * DEC + b:tile * DEC + b + 1],
                                         ring[:, b % slots, tile * P:(tile + 1) * P],
                                         c[:, 20 + tile // 4, SEQ + b:SEQ + b + 1], start=True, stop=True)
                    core.tile_multiplied.inc(last)

                rows(0)
                for b in range(DEC):
                    if b + 1 < DEC:
                        rows(b + 1)
                    outputs(b)

            @block.vector
            def _(dve):
                for b in range(DEC):
                    dve.wait_ge(core.pool_done.sem, decayed0 + b + 1)
                    dve.wait_ge(core.pe_done.sem, spread0 + b + 1)
                    for g in range(GROUPS):
                        s = ring[:, b % slots, g * 512:(g + 1) * 512]
                        last = dve.scalar_tensor_tensor(s, spread[g][:, :], c[:, 16 + g, SEQ + b:SEQ + b + 1], s,
                                                        ALU.mult, ALU.add)
                    core.dve_done.inc(last)
        with nc.Block() as block:
            @block.vector
            def _(dve):
                dve.tensor_copy(y[:, :, SEQ:T], reads[:, 0:INNER_TILES * DEC].rearrange("p (a b) -> p a b", b=DEC))


def ssm_prompt(core, mask, expand, c, xdt, log_sum, y, state_out):
    nc = core.nc
    with ExitStack() as ctx:
        x_tok = core.sb(ctx, "x_tok", [P, HALVES, INNER])
        x_late = core.sb(ctx, "x_late", [P, HALVES, INNER])
        b_tok = core.sb(ctx, "b_tok", [P, HALVES, 512])
        sum_tok = core.sb(ctx, "sum_tok", [P, HALVES, HEADS])
        late = core.sb(ctx, "late", [P, HALVES, HEADS])
        end = core.sb(ctx, "end", [P, HALVES, HEADS])
        diagonal = core.sb(ctx, "diagonal", [HEADS, HALVES, HEADS])
        inside = core.sb(ctx, "inside", [P, HALVES, GROUPS, P])
        grown = core.sb(ctx, "grown", [P, INNER_TILES, P])
        state = core.sb(ctx, "state", [P, INNER])
        halves = [slice(0, P), slice(P, 2 * P)]
        with ExitStack() as ps:
            banks = core.banks(ps, "turned", 4)
            sums, ends = core.banks(ps, "sums", 2)
            cb = core.banks(ps, "cb", 2)
            done0, out0 = core.pe_done.at, core.act_done.at
            jobs = [(x_tok, half, q, xdt, 4 * q) for half in range(HALVES) for q in range(4)]
            jobs += [(b_tok, half, 0, c, 16) for half in range(HALVES)]
            with nc.Block() as block:
                @block.tensor
                def _(pe):
                    for n, (dst, half, q, src, first) in enumerate(jobs):
                        if n >= 4:
                            pe.wait_ge(core.act_done.sem, out0 + n - 3)
                        for i in range(4):
                            last = pe.transpose(banks[n % 4][:, i * P:(i + 1) * P], src[:, first + i, halves[half]],
                                                core.ident)
                        core.pe_done.inc(last)
                    for half in range(HALVES):
                        pe.transpose(sums[:, half * HEADS:(half + 1) * HEADS], log_sum[:, halves[half]],
                                     core.ident[0:HEADS, 0:HEADS])
                        for g in range(GROUPS):
                            pe.matmul(cb[half][:, g * P:(g + 1) * P], c[:, 16 + g, halves[half]],
                                      c[:, 20 + g, halves[half]], start=True, stop=True)

                @block.scalar
                def _(act):
                    for n, (dst, half, q, src, first) in enumerate(jobs):
                        act.wait_ge(core.pe_done.sem, done0 + n + 1)
                        core.act_done.inc(act.copy(dst[:, half, q * 512:(q + 1) * 512], banks[n % 4][:, :]))

                @block.vector
                def _(dve):
                    for half in range(HALVES):
                        at = half * P + P - 1
                        dve.tensor_scalar(diagonal[:, half, :], core.ident[0:HEADS, 0:HEADS],
                                          log_sum[:, at:at + 1], None, ALU.mult)
            with nc.Block() as block:
                @block.tensor
                def _(pe):
                    pe.matmul(ends[:, 0:HALVES * HEADS], core.ones[0:HEADS, :],
                              diagonal.rearrange("p a h -> p (a h)"), start=True, stop=True)

                @block.vector
                def _(dve):
                    dve.tensor_copy(sum_tok, sums[:, 0:HALVES * HEADS].rearrange("p (a h) -> p a h", a=HALVES))
                    for half in range(HALVES):
                        dve.tensor_tensor(inside[:, half], cb[half][:, :].rearrange("p (g j) -> p g j", g=GROUPS),
                                          mask[:, MASK_CAUSAL:MASK_CAUSAL + 1, :].broadcast_to((P, GROUPS, P)),
                                          ALU.mult)
            with nc.Block() as block:
                @block.vector
                def _(dve):
                    dve.tensor_tensor(late, ends[:, 0:HALVES * HEADS].rearrange("p (a h) -> p a h", a=HALVES),
                                      sum_tok, ALU.subtract)
            with nc.Block() as block:
                @block.scalar
                def _(act):
                    act.activation(end, ends[:, 0:HALVES * HEADS].rearrange("p (a h) -> p a h", a=HALVES), ACT.Exp)
                    act.activation(late, late, ACT.Exp)
            with nc.Block() as block:
                @block.vector
                def _(dve):
                    for half in range(HALVES):
                        dve.tensor_tensor(x_late[:, half].rearrange("p (h v) -> p h v", h=HEADS),
                                          x_tok[:, half].rearrange("p (h v) -> p h v", h=HEADS),
                                          late[:, half].unsqueeze(2).broadcast_to((P, HEADS, 64)), ALU.mult)
        with ExitStack() as ps:
            adds = core.banks(ps, "adds", 4)
            grows = core.banks(ps, "grows", 4)
            with nc.Block() as block:
                @block.tensor
                def _(pe):
                    for g in range(GROUPS):
                        pe.matmul(adds[g][:, :], b_tok[:, 0, g * P:(g + 1) * P], x_late[:, 0, g * 512:(g + 1) * 512],
                                  start=True, stop=True)
                    for tile in range(INNER_TILES):
                        pick = expand[:, tile * P:(tile + 1) * P]
                        pe.matmul(grows[tile // 4][:, (tile % 4) * P:(tile % 4 + 1) * P], pick,
                                  log_sum[:, halves[1]], start=True, stop=True)
            with nc.Block() as block:
                @block.vector
                def _(dve):
                    for g in range(GROUPS):
                        dve.tensor_copy(state[:, g * 512:(g + 1) * 512], adds[g][:, :])

                @block.scalar
                def _(act):
                    for g in range(GROUPS):
                        act.activation(grown[:, 4 * g:4 * g + 4, :],
                                       grows[g][:, :].rearrange("p (a j) -> p a j", a=4), ACT.Exp)
        with ExitStack() as ps:
            decay = core.sb(ps, "decay", [P, 2, 8, P])
            carried = core.sb(ps, "carried", [P, 512])
            sum_banks = core.banks(ps, "sum", 4)
            y_banks = core.banks(ps, "y", 2)
            (carry_bank,) = core.banks(ps, "carry", 1)
            work = [(half, g) for half in range(HALVES) for g in range(GROUPS)]
            row0, y0, gap0, exp0, weight0, out0 = (core.pe_done.at, core.tile_multiplied.at, core.dve_done.at,
                                                   core.act_done.at, core.pool_done.at, core.tile_evicted.at)
            with nc.Block() as block:
                @block.tensor
                def _(pe):
                    def rows(n):
                        half, g = work[n]
                        if n >= 2:
                            pe.wait_ge(core.dve_done.sem, gap0 + n - 1)
                        for h in range(8):
                            last = pe.matmul(sum_banks[2 * (n % 2) + h // 4][:, (h % 4) * P:(h % 4 + 1) * P],
                                             core.ident[0:HEADS, 8 * g + h:8 * g + h + 1].broadcast_to((HEADS, P)),
                                             log_sum[:, halves[half]], start=True, stop=True)
                        core.pe_done.inc(last)

                    rows(0)
                    for n, (half, g) in enumerate(work):
                        if n + 1 < len(work):
                            rows(n + 1)
                        if n >= 2:
                            pe.wait_ge(core.tile_evicted.sem, out0 + n - 1)
                        if half:
                            if g:
                                pe.wait_ge(core.tile_evicted.sem, out0 + n)
                            for tile in range(4 * g, 4 * g + 4):
                                pe.matmul(carry_bank[:, (tile % 4) * P:(tile % 4 + 1) * P],
                                          state[:, tile * P:(tile + 1) * P], c[:, 20 + g, halves[1]],
                                          start=True, stop=True)
                        pe.wait_ge(core.pool_done.sem, weight0 + n + 1)
                        for h in range(8):
                            last = pe.matmul(
                                y_banks[n % 2][64 * (h % 2):64 * (h % 2) + 64, (h // 2) * P:(h // 2 + 1) * P],
                                x_tok[:, half, (8 * g + h) * 64:(8 * g + h + 1) * 64], decay[:, n % 2, h, :],
                                start=True, stop=True)
                        core.tile_multiplied.inc(last)

                @block.vector
                def _(dve):
                    def gaps(n):
                        half, g = work[n]
                        dve.wait_ge(core.pe_done.sem, row0 + n + 1)
                        if n >= 2:
                            dve.wait_ge(core.tile_multiplied.sem, y0 + n - 1)
                        for h in range(8):
                            last = dve.tensor_scalar(
                                decay[:, n % 2, h, :],
                                sum_banks[2 * (n % 2) + h // 4][:, (h % 4) * P:(h % 4 + 1) * P],
                                sum_tok[:, half, 8 * g + h:8 * g + h + 1], 0.0, ALU.subtract, ALU.min)
                        core.dve_done.inc(last)

                    def finish(n):
                        half, g = work[n]
                        dve.wait_ge(core.tile_multiplied.sem, y0 + n + 1)
                        to = y[:, 4 * g:4 * g + 4, halves[half]]
                        four = lambda a: a.rearrange("p (a j) -> p a j", a=4)
                        if half:
                            link = Link(dve, core.carry_done)
                            link(dve.tensor_tensor(four(carried), four(carry_bank[:, :]), grown[:, 4 * g:4 * g + 4, :],
                                                   ALU.mult))
                            core.tile_evicted.inc(dve.tensor_tensor(to, four(y_banks[n % 2][:, :]), four(carried),
                                                                    ALU.add))
                        else:
                            core.tile_evicted.inc(dve.tensor_copy(to, four(y_banks[n % 2][:, :])))

                    gaps(0)
                    for n in range(len(work)):
                        if n + 1 < len(work):
                            gaps(n + 1)
                        finish(n)

                @block.scalar
                def _(act):
                    for n in range(len(work)):
                        act.wait_ge(core.dve_done.sem, gap0 + n + 1)
                        core.act_done.inc(act.activation(decay[:, n % 2], decay[:, n % 2], ACT.Exp))

                @block.gpsimd
                def _(pool):
                    for n, (half, g) in enumerate(work):
                        pool.wait_ge(core.act_done.sem, exp0 + n + 1)
                        core.pool_done.inc(pool.tensor_tensor(
                            decay[:, n % 2], decay[:, n % 2],
                            inside[:, half, g:g + 1, :].broadcast_to((P, 8, P)), ALU.mult))
        with ExitStack() as ps:
            adds = core.banks(ps, "adds", 4)
            with nc.Block() as block:
                @block.tensor
                def _(pe):
                    for g in range(GROUPS):
                        pe.matmul(adds[g][:, :], b_tok[:, 1, g * P:(g + 1) * P], x_late[:, 1, g * 512:(g + 1) * 512],
                                  start=True, stop=True)

                @block.vector
                def _(dve):
                    s = state.rearrange("p (h v) -> p h v", h=HEADS)
                    dve.tensor_tensor(s, s, end[:, 1].unsqueeze(2).broadcast_to((P, HEADS, 64)), ALU.mult)
            with nc.Block() as block:
                @block.vector
                def _(dve):
                    for g in range(GROUPS):
                        at = slice(g * 512, (g + 1) * 512)
                        dve.tensor_tensor(state[:, at], adds[g][:, :], state[:, at], ALU.add)
            with nc.Block() as block:
                @block.sync
                def _(sp):
                    core.stored.inc(sp.dma_start(state_out, state), 16)
                    sp.wait_ge(core.stored.sem, core.stored.at)


def mixer_ssm(core, x, d, norm, w_in, then=None):
    nc = core.nc
    w_out = Stream(d["ssm_w_out"])
    core.carry_done = Count(nc, "carry_done")
    with ExitStack() as ctx:
        mask = core.sb(ctx, "mask", [P, MASKS, P])
        params = core.sb(ctx, "params", [P, SSM_PARAMS])

        def par(name, i=None):
            at = SSM_PARAM[name]
            return params[:, at] if i is None else params[:, at.start + i:at.start + i + 1]

        p = core.sb(ctx, "p", [P, SSM_TILES, T])
        y = p[:, INNER_TILES:2 * INNER_TILES, :]
        with ExitStack() as local:
            dt = core.sb(local, "dt", [HEADS, T])
            log_a = core.sb(local, "log_a", [HEADS, T])
            log_sum = core.sb(local, "log_sum", [HEADS, SEQ])
            expand = core.sb(local, "expand", [HEADS, INNER])
            with nc.Block() as block:
                @block.vector
                def _(dve):
                    dve.tensor_copy(expand.rearrange("p (h v) -> p h v", h=HEADS),
                                    core.ident[0:HEADS, 0:HEADS].unsqueeze(2).broadcast_to((HEADS, HEADS, 64)))
            with nc.Block() as block:
                @block.sync
                def _(sp):
                    core.load(sp, params, d["ssm_params"])
                    core.load(sp, mask, d["masks"])
            with ExitStack() as inner:
                h = core.sb(inner, "mix_in", [P, KC, T])
                h_hi = core.sb(inner, "mix_in_hi", [P, KC, T], F32R)
                h_lo = core.sb(inner, "mix_in_lo", [P, KC, T], F32R)
                rms_norm(core, x, norm, h)
                split(core, h, h_hi, h_lo)
                with ExitStack() as stream:
                    project(core, Weights(core, stream), w_in, SSM_TILES, h_hi, h_lo, p, then=w_out)
                ssm_steps(core, h, d["ssm_w_dt"], d["ssm_heads"], mask, dt, log_a, log_sum)
            c = core.sb(local, "c", [P, CONV_TILES, T])
            xdt = core.sb(local, "xdt", [P, INNER_TILES, T])
            ssm_conv(core, par, p, c, d["conv_in"], d["conv_prompt"], d["conv_sample"])
            with ExitStack() as ps:
                banks = core.banks(ps, "dt", 8)
                done0, used0 = core.pe_done.at, core.dve_done.at
                with nc.Block() as block:
                    @block.tensor
                    def _(pe):
                        for tile in range(INNER_TILES):
                            if tile >= 8:
                                pe.wait_ge(core.dve_done.sem, used0 + tile - 7)
                            pick = expand[:, tile * P:(tile + 1) * P]
                            core.pe_done.inc(pe.matmul(banks[tile % 8][:, 0:T], pick, dt, start=True, stop=True))

                    @block.vector
                    def _(dve):
                        for tile in range(INNER_TILES):
                            dve.wait_ge(core.pe_done.sem, done0 + tile + 1)
                            core.dve_done.inc(dve.tensor_tensor(xdt[:, tile, :], banks[tile % 8][:, 0:T],
                                                                c[:, tile, :], ALU.mult))
            ssm_sample(core, c, xdt, log_a, y, d["ssm_in"], d["ssm_sample"])
            ssm_prompt(core, mask, expand, c, xdt, log_sum, y, d["ssm_prompt"])
            with nc.Block() as block:
                @block.scalar
                def _(act):
                    act.activation(p[:, 0:INNER_TILES, :], p[:, 0:INNER_TILES, :], ACT.Silu)

                @block.vector
                def _(dve):
                    for i in range(INNER_TILES):
                        dve.scalar_tensor_tensor(y[:, i, :], c[:, i, :], par("skip", i), y[:, i, :],
                                                 ALU.mult, ALU.add)
            with nc.Block() as block:
                @block.vector
                def _(dve):
                    dve.tensor_tensor(y, y, p[:, 0:INNER_TILES, :], ALU.mult)
        with ExitStack() as local:
            squares = core.sb(local, "squares", [P, INNER_TILES, T])
            rstd = core.sb(local, "rstd", [P, GROUPS, T])
            banks = core.banks(local, "norm", GROUPS)
            with nc.Block() as block:
                @block.scalar
                def _(act):
                    act.activation(squares, y, ACT.Square)
            with nc.Block() as block:
                @block.tensor
                def _(pe):
                    for g in range(GROUPS):
                        for i in range(4):
                            pe.matmul(banks[g][:, 0:T], core.ones, squares[:, 4 * g + i, :], start=i == 0, stop=i == 3)
            inverse_root(core, banks, GROUPS, rstd, 1.0 / 512, RMS_EPS)
            with nc.Block() as block:
                @block.vector
                def _(dve):
                    for i in range(INNER_TILES):
                        dve.scalar_tensor_tensor(y[:, i, :], y[:, i, :], par("out_norm", i), rstd[:, i // 4, :],
                                                 ALU.mult, ALU.mult)
        with ExitStack() as local:
            y_hi = core.sb(local, "y_hi", [P, INNER_TILES, T], F32R)
            y_lo = core.sb(local, "y_lo", [P, INNER_TILES, T], F32R)
            split(core, y, y_hi, y_lo)
            project(core, Weights(core, local), w_out, KC, y_hi, y_lo, x, parts=2, residual=True, then=then)


def lay_out(inputs):
    import numpy as np
    c = np.ascontiguousarray

    def tiles(w, kc):
        return c(np.transpose(np.reshape(w, (kc, P, -1, P)), (2, 1, 0, 3)).reshape(-1, P, kc * P))

    def columns(*vectors):
        return c(np.concatenate([np.reshape(v, (-1, P)).T for v in vectors], axis=1))

    i = inputs
    tokens = np.concatenate([i["x_prompt"][0], i["x_sample"][:, 0]], axis=0)
    d = {"x": c(np.transpose(np.reshape(tokens, (T, KC, P)), (2, 1, 0))), "masks": masks()}
    if "ab_w_in" in i:
        d["ab_params"] = columns(i["norm_mix"][0], i["rwkv_mu"][0], i["rwkv_w0"][0], i["rwkv_a0"][0], i["rwkv_k_k"][0],
                                 i["rwkv_k_a"][0], i["rwkv_r_k"][0], i["rwkv_gn_w"][0], i["rwkv_gn_b"][0],
                                 i["hgrn_lower_bounds"][0], i["hgrn_norm_w"][0])
        d["ab_w_in"] = tiles(i["ab_w_in"][0], KC)
        d["ab_w_out"] = tiles(i["ab_w_out"][0], KC)
        d["lora_up"] = c(np.concatenate([i["rwkv_w_up"][0], i["rwkv_a_up"][0]], axis=0))
        d["gate_up"] = c(i["rwkv_g_up"][0])
        d["shift_in"] = c(np.transpose(np.reshape(i["state_rwkv_shift"][0], (DEC, SHIFT_TILES, P)), (2, 1, 0)))
        d["rwkv_in"] = c(np.transpose(np.reshape(i["state_rwkv"][0], (DEC, 4, 2, 64, 64)), (2, 4, 1, 0, 3)
                                      ).reshape(P, 4, DEC, 64))
        d["hgrn_in"] = c(np.transpose(i["state_hgrn"][0], (2, 1, 0, 3)))
    if "ssm_w_in" in i:
        w = i["ssm_w_in"][0]
        d["ssm_params"] = columns(i["norm_mix"][1], i["ssm_conv_w"][0], i["ssm_conv_b"][0], i["ssm_norm_w"][0],
                                  np.repeat(i["ssm_d"][0], 64))
        d["ssm_heads"] = c(np.stack([i["ssm_dt_bias"][0], i["ssm_a_log"][0]], axis=1))
        d["ssm_w_in"] = tiles(w[:, 0:SSM_TILES * P], KC)
        d["ssm_w_dt"] = c(np.transpose(np.reshape(w[:, SSM_TILES * P:], (KC, P, 32)), (1, 0, 2)))
        d["ssm_w_out"] = c(np.transpose(np.reshape(i["ssm_w_out"][0], (2, KC, P, KC, P)), (3, 0, 2, 1, 4)
                                        ).reshape(2 * KC, P, D_MODEL))
        d["conv_in"] = c(np.transpose(np.reshape(i["state_conv"][0], (DEC, 3, CONV_TILES, P)), (3, 2, 1, 0)))
        d["ssm_in"] = c(np.transpose(i["state_ssm"][0], (3, 0, 1, 2)).reshape(P, DEC, 2048))
    if "peer_w_q" in i:
        for n in range(2):
            d[f"norm_ffn{n}"] = columns(i["norm_ffn"][n])
            d[f"w_q{n}"] = tiles(i["peer_w_q"][n], KC)
            d[f"sub_keys{n}"] = c(np.transpose(i["peer_sub_keys"][n], (3, 1, 0, 2)).reshape(P, SETS, KEYS))
            d[f"up{n}"] = c(np.transpose(np.reshape(i["peer_u"][n], (KEYS, KEYS, KC, P)), (1, 3, 2, 0)
                                         ).reshape(KEYS, P, D_MODEL))
            d[f"down{n}"] = c(np.transpose(np.reshape(i["peer_v"][n], (KEYS, KEYS, D_MODEL)), (1, 0, 2)))
        d["norm_final"] = columns(i["norm_final"])
    return d


def tokens_back(y):
    import numpy as np
    return np.transpose(y, (2, 1, 0)).reshape(T, -1)


def ab_back(r):
    import numpy as np
    c = np.ascontiguousarray
    shift = np.transpose(r["last_shift"], (2, 1, 0)).reshape(DEC + 1, SHIFT_TILES * P)
    s = np.reshape(r["rwkv_prompt"], (2, 64, 4, 2, 64))
    rwkv = np.stack([s[0, :, :, 0, :], s[1, :, :, 1, :]], axis=0)
    rwkv = np.transpose(rwkv, (2, 0, 3, 1)).reshape(1, 1, 8, 64, 64)
    hgrn = np.transpose(r["hgrn_prompt"], (1, 0, 2)).reshape(1, 1, 4, P, P)
    s_rwkv = np.transpose(np.reshape(r["rwkv_sample"], (2, 64, 4, DEC, 64)), (3, 2, 0, 4, 1)).reshape(1, DEC, 8, 64, 64)
    s_hgrn = np.transpose(r["hgrn_sample"], (2, 1, 0, 3)).reshape(1, DEC, 4, P, P)
    return (c(shift[None, 0:1]), c(rwkv), c(hgrn)), (c(shift[None, 1:]), c(s_rwkv), c(s_hgrn))


AB_OUT = {"last_shift": (P, SHIFT_TILES, DEC + 1), "rwkv_prompt": (P, 4, P), "rwkv_sample": (P, 4, DEC, 64),
          "hgrn_prompt": (P, 4, P), "hgrn_sample": (P, 4, DEC, P)}


def ssm_back(r):
    import numpy as np
    c = np.ascontiguousarray
    conv = np.transpose(r["conv_prompt"], (2, 1, 0)).reshape(1, 1, TAPS - 1, CONV_TILES * P)
    s_conv = np.transpose(r["conv_sample"], (3, 2, 1, 0)).reshape(1, DEC, TAPS - 1, CONV_TILES * P)
    ssm = np.transpose(np.reshape(r["ssm_prompt"], (P, HEADS, 64)), (1, 2, 0))[None, None]
    s_ssm = np.transpose(np.reshape(r["ssm_sample"], (P, DEC, HEADS, 64)), (1, 2, 3, 0))[None]
    return (c(ssm), c(conv)), (c(s_ssm), c(s_conv))


def program(nc, d):
    with ExitStack() as ctx:
        core = Core(nc, ctx)
        constants(core, ctx)
        x = core.sb(ctx, "x", [P, KC, T])
        norms = core.sb(ctx, "norms", [P, 5, KC])

        core.weights_raw = core.sb(ctx, "weights_raw", [P, RING, D_MODEL])
        ab_in, ssm_in, w_q0, w_q1 = (Stream(d[name]) for name in ("ab_w_in", "ssm_w_in", "w_q0", "w_q1"))

        with nc.Block() as block:
            @block.sync
            def _(sp):
                core.load(sp, x, d["x"])
                for n, src in enumerate((d["norm_ffn0"], d["norm_ffn1"], d["norm_final"],
                                         d["ab_params"][:, AB_PARAM["norm"]], d["ssm_params"][:, SSM_PARAM["norm"]])):
                    core.load(sp, norms[:, n, :], src)
                first_loads(core, sp, ab_in)
                core.wait_loads(sp)
        mixer_ab(core, x, d, norms[:, 3, :], ab_in, then=w_q0)
        peer(core, x, norms[:, 0, :], w_q0, d["sub_keys0"], d["up0"], d["down0"], then=ssm_in)
        mixer_ssm(core, x, d, norms[:, 4, :], ssm_in, then=w_q1)
        peer(core, x, norms[:, 1, :], w_q1, d["sub_keys1"], d["up1"], d["down1"])
        with ExitStack() as local:
            y = core.sb(local, "y", [P, KC, T])
            rms_norm(core, x, norms[:, 2, :], y)
            with nc.Block() as block:
                @block.sync
                def _(sp):
                    core.stored.inc(sp.dma_start(d["y"], y), 16)
                    sp.wait_ge(core.stored.sem, core.stored.at)


def kernel(**inputs):
    import numpy as np
    import concourse.bacc as bacc
    from concourse.bass_utils import run_bass_kernel_spmd as run

    nc = bacc.Bacc("TRN2", target_bir_lowering=False, num_devices=1)
    arrays = lay_out(inputs)
    d = {k: nc.dram_tensor("in_" + k, a.shape, F32, kind="ExternalInput").ap() for k, a in arrays.items()}
    for k, shape in {**AB_OUT, **SSM_OUT, "y": (P, KC, T)}.items():
        d[k] = nc.dram_tensor(k, shape, F32, kind="ExternalOutput").ap()
    program(nc, d)
    r = run(nc, [{"in_" + k: a for k, a in arrays.items()}], core_ids=[0]).results[0]
    (p_shift, p_rwkv, p_hgrn), (s_shift, s_rwkv, s_hgrn) = ab_back(r)
    (p_ssm, p_conv), (s_ssm, s_conv) = ssm_back(r)
    y = np.ascontiguousarray(tokens_back(r["y"]))
    return (y[None, 0:SEQ], y[SEQ:T, None], p_shift, p_rwkv, p_hgrn, p_ssm, p_conv,
            s_shift, s_rwkv, s_hgrn, s_ssm, s_conv)
```

```python
from contextlib import ExitStack

import concourse.bass as bass
from concourse import mybir

F32 = mybir.dt.float32
F32R = mybir.dt.float32r
U32 = mybir.dt.uint32
ACT = mybir.ActivationFunctionType
ALU = mybir.AluOpType
AX_X = mybir.AxisListType.X

P = 128
D_MODEL = 1024
SEQ = 256
DEC = 8
T = SEQ + DEC
KC = D_MODEL // P
RMS_EPS = 1e-6
STATE_SLOTS = 4


class Count:

    def __init__(self, nc, name):
        self.sem = nc.alloc_semaphore(name)
        self.at = 0

    def inc(self, ins, by=1):
        ins.then_inc(self.sem, by)
        self.at += by
        return self.at


class Link:

    def __init__(self, eng, count):
        self.eng, self.count = eng, count

    def __call__(self, ins):
        self.eng.wait_ge(self.count.sem, self.count.inc(ins))


class Core:

    def __init__(self, nc, ctx):
        self.nc, self.ctx = nc, ctx
        self.names = 0
        self.dve_done = Count(nc, "dve_done")
        self.act_done = Count(nc, "act_done")
        self.pool_done = Count(nc, "pool_done")
        self.pe_done = Count(nc, "pe_done")
        self.loaded = Count(nc, "loaded")
        self.stored = Count(nc, "stored")
        self.tile_loaded = [Count(nc, f"tile_loaded{i}") for i in range(RING)]
        self.state_loaded = [Count(nc, f"state_loaded{i}") for i in range(STATE_SLOTS)]
        self.state_stored = [Count(nc, f"state_stored{i}") for i in range(STATE_SLOTS)]
        self.tile_multiplied = Count(nc, "tile_multiplied")
        self.tile_evicted = Count(nc, "tile_evicted")
        self.first_slot = 0
        self.mixed = Count(nc, "mixed")
        self.hi_made = Count(nc, "hi_made")
        self.lo_made = Count(nc, "lo_made")
        self.gate_equal = Count(nc, "gate_equal")
        self.gate_summed = Count(nc, "gate_summed")
        self.gate_copied = Count(nc, "gate_copied")
        self.gated_hi = Count(nc, "gated_hi")
        self.gated_lo = Count(nc, "gated_lo")

    def sb(self, ctx, name, shape, dt=F32):
        self.names += 1
        return ctx.enter_context(self.nc.sbuf_tensor(f"{name}_{self.names}", shape, dt))[:]

    def banks(self, ctx, name, n):
        self.names += 1
        return [ctx.enter_context(self.nc.psum_tensor(f"{name}_{self.names}_{i}", [P, 512], F32)) for i in range(n)]

    def load(self, eng, dst, src):
        self.loaded.inc(eng.dma_start(dst, src), 16)

    def wait_loads(self, eng):
        eng.wait_ge(self.loaded.sem, self.loaded.at)


def constants(core, ctx):
    nc = core.nc
    core.ident = core.sb(ctx, "ident", [P, P])
    core.ones = core.sb(ctx, "ones", [P, P])
    core.index_row = core.sb(ctx, "index_row", [P, P])
    with nc.Block() as block:
        @block.gpsimd
        def _(pool):
            link = Link(pool, core.pool_done)
            link(pool.iota(core.index_row, [[1, P]], base=0, channel_multiplier=0,
                           allow_small_or_imprecise_dtypes=True))
            link(pool.memset(core.ident, 0.0))
            link(pool.affine_select(core.ident, core.ident, [[-1, P]], ALU.not_equal, 1.0, 0, 1))
            link(pool.memset(core.ones, 1.0))


def rms_norm(core, x, weight, out, hi=None, lo=None):
    nc = core.nc
    with ExitStack() as ctx:
        squares = core.sb(ctx, "squares", [P, KC, T])
        root = core.sb(ctx, "root", [P, T])
        (total,) = core.banks(ctx, "square_sum", 1)
        act0, pe0, dve0, hi0 = core.act_done.at, core.pe_done.at, core.dve_done.at, core.hi_made.at
        half = KC // 2
        with nc.Block() as block:
            @block.scalar
            def _(act):
                for k in range(half):
                    core.act_done.inc(act.activation(squares[:, k, :], x[:, k, :], ACT.Square))
                act.wait_ge(core.dve_done.sem, dve0 + half + 1)
                core.act_done.inc(act.activation(root, root, ACT.Sqrt))
                if hi is not None:
                    for k in range(KC):
                        act.wait_ge(core.dve_done.sem, dve0 + half + 3 + k)
                        core.hi_made.inc(act.copy(hi[:, k, :], out[:, k, :]))

            @block.tensor
            def _(pe):
                for n in range(KC):
                    k = n // 2 + half * (n % 2)
                    if n % 2:
                        pe.wait_ge(core.dve_done.sem, dve0 + n // 2 + 1)
                    else:
                        pe.wait_ge(core.act_done.sem, act0 + n // 2 + 1)
                    last = pe.matmul(total[:, 0:T], core.ones, squares[:, k, :], start=n == 0, stop=n == KC - 1)
                core.pe_done.inc(last)

            @block.vector
            def _(dve):
                for k in range(half, KC):
                    core.dve_done.inc(dve.tensor_tensor(squares[:, k, :], x[:, k, :], x[:, k, :], ALU.mult))
                dve.wait_ge(core.pe_done.sem, pe0 + 1)
                core.dve_done.inc(dve.tensor_scalar(root, total[:, 0:T], 1.0 / D_MODEL, RMS_EPS, ALU.mult, ALU.add))
                dve.wait_ge(core.act_done.sem, act0 + half + 1)
                core.dve_done.inc(dve.reciprocal(root, root))
                dve.wait_ge(core.dve_done.sem, dve0 + half + 2)
                for k in range(KC):
                    core.dve_done.inc(dve.scalar_tensor_tensor(out[:, k, :], x[:, k, :], weight[:, k:k + 1], root,
                                                               ALU.mult, ALU.mult))
                if hi is not None:
                    for k in range(half, KC):
                        dve.wait_ge(core.hi_made.sem, hi0 + k + 1)
                        dve.tensor_tensor(lo[:, k, :], out[:, k, :], hi[:, k, :].bitcast(F32), ALU.subtract)

            if hi is not None:
                @block.gpsimd
                def _(pool):
                    for k in range(half):
                        pool.wait_ge(core.hi_made.sem, hi0 + k + 1)
                        pool.tensor_tensor(lo[:, k, :], out[:, k, :], hi[:, k, :].bitcast(F32), ALU.subtract)


UNROLL = 6
RING = 3


def tile_loop(eng, n, one):
    for u in range(min(n, UNROLL)):
        one(0, u)
    if n // UNROLL > 1:
        with eng.Fori(1, n // UNROLL) as i:
            for u in range(UNROLL):
                one(i, u)
    if n > UNROLL:
        for u in range(n % UNROLL):
            one(n // UNROLL, u)


def fresh(i, u, ring=RING):
    return isinstance(i, int) and i * UNROLL + u < ring


def split(core, src, hi, lo):
    with core.nc.Block() as block:
        @block.scalar
        def _(act):
            act.copy(hi, src)
    with core.nc.Block() as block:
        @block.vector
        def _(dve):
            dve.tensor_tensor(lo, src, hi.bitcast(F32), ALU.subtract)


class Stream:

    def __init__(self, dram, first=0, cols=slice(0, D_MODEL)):
        self.dram, self.first, self.cols = dram, first, cols
        self.parts = dram.shape[2] if len(dram.shape) == 4 else 1
        self.width = self.parts * (cols.stop - cols.start)
        self.loading = False
        self.ahead = False

    def load(self, core, sp, i, u, slot):
        at = bass.ds(i * UNROLL + (u + self.first), 1)
        dst = core.weights_raw[:, slot, 0:self.width]
        if self.parts > 1:
            tile = self.dram[at].rearrange("a p g f -> p (a g) f")[:, :, self.cols]
            dst = dst.rearrange("p (g f) -> p g f", g=self.parts)
        else:
            tile = self.dram[at].rearrange("a p f -> p (a f)")[:, self.cols]
        sp.dma_start(dst, tile).then_inc(core.tile_loaded[slot].sem, 16)


def first_loads(core, sp, stream):
    for s in range(RING):
        stream.load(core, sp, 0, s, s)
    stream.loading = True


class Weights:

    def __init__(self, core, ctx):
        self.core = core
        self.hi = core.sb(ctx, "weights_hi", [P, RING, D_MODEL], F32R)
        self.lo = core.sb(ctx, "weights_lo", [P, RING, D_MODEL], F32R)
        self.raw = core.weights_raw

    def begin(self, stream, then=None, ahead=False):
        core = self.core
        self.stream, self.then, self.width, self.ahead = stream, then, stream.width, ahead
        self.slot0 = core.first_slot
        self.loaded0 = [c.at for c in core.tile_loaded]
        self.hi0, self.lo0, self.used0 = core.hi_made.at, core.lo_made.at, core.tile_multiplied.at

    def slot(self, u):
        return (u + self.slot0) % RING

    def load_all(self, sp, n):
        def load(i, u):
            if not fresh(i, u):
                sp.wait_ge(self.core.lo_made.sem, i * UNROLL + (u - 2 + self.lo0))
            if not fresh(i, u) or not self.stream.loading:
                self.stream.load(self.core, sp, i, u, self.slot(u))
        tile_loop(sp, n, load)
        if self.then:
            for t in range(RING):
                sp.wait_ge(self.core.lo_made.sem, self.lo0 + n - RING + t + 1)
                self.then.load(self.core, sp, 0, t, self.slot(n + t))
            self.then.loading = True

    def make_hi(self, act, i, u):
        if fresh(i, u) and self.stream.ahead:
            return
        slot = self.slot(u)
        act.wait_ge(self.core.tile_loaded[slot].sem,
                    i * (16 * UNROLL // RING) + (16 * (u // RING + 1) + self.loaded0[slot]))
        if not fresh(i, u):
            act.wait_ge(self.core.tile_multiplied.sem, i * UNROLL + (u - 2 + self.used0))
        act.copy(self.hi[:, slot, 0:self.width], self.raw[:, slot, 0:self.width]
                 ).then_inc(self.core.hi_made.sem, 1)

    def make_lo(self, pool, i, u):
        if fresh(i, u) and self.stream.ahead:
            return
        slot = self.slot(u)
        pool.wait_ge(self.core.hi_made.sem, i * UNROLL + (u + 1 + self.hi0))
        pool.tensor_tensor(self.lo[:, slot, 0:self.width], self.raw[:, slot, 0:self.width],
                           self.hi[:, slot, 0:self.width].bitcast(F32), ALU.subtract
                           ).then_inc(self.core.lo_made.sem, 1)

    def hi_ahead(self, act, n, t):
        if self.ahead:
            slot, width = self.slot(n + t), self.then.width
            before = (n - RING + t) // RING + 1
            act.wait_ge(self.core.tile_loaded[slot].sem, self.loaded0[slot] + 16 * (before + 1))
            act.wait_ge(self.core.tile_multiplied.sem, self.used0 + n - RING + t + 1)
            act.copy(self.hi[:, slot, 0:width], self.raw[:, slot, 0:width]).then_inc(self.core.hi_made.sem, 1)

    def make_lo_all(self, pool, n):
        tile_loop(pool, n, lambda i, u: self.make_lo(pool, i, u))
        if self.ahead:
            for t in range(RING):
                slot, width = self.slot(n + t), self.then.width
                pool.wait_ge(self.core.hi_made.sem, self.hi0 + n + t + 1)
                pool.tensor_tensor(self.lo[:, slot, 0:width], self.raw[:, slot, 0:width],
                                   self.hi[:, slot, 0:width].bitcast(F32), ALU.subtract
                                   ).then_inc(self.core.lo_made.sem, 1)

    def ready(self, pe, i, u):
        pe.wait_ge(self.core.lo_made.sem, i * UNROLL + (u + 1 + self.lo0))

    def product(self, pe, out, u, cols, rhs_hi, rhs_lo, start, stop):
        hi, lo = self.hi[:, self.slot(u), cols], self.lo[:, self.slot(u), cols]
        pe.matmul(out, hi, rhs_hi, start=start, stop=False, skip_group_check=True)
        pe.matmul(out, hi, rhs_lo, start=False, stop=False, skip_group_check=True)
        return pe.matmul(out, lo, rhs_hi, start=False, stop=stop, skip_group_check=True)

    def end(self, n):
        core = self.core
        for t in range(RING):
            core.tile_loaded[self.slot(t)].at += 16 * ((n - t + RING - 1) // RING)
        core.first_slot = self.slot(n)
        core.hi_made.at += n
        core.lo_made.at += n
        core.tile_multiplied.at += n
        if self.ahead:
            self.then.ahead = True


def project(core, weights, stream, n, rhs_hi, rhs_lo, dst, parts=1, residual=False, then=None, beside=None, ahead=False):
    nc = core.nc
    total = n * parts
    weights.begin(stream, then, ahead)
    with ExitStack() as ctx:
        banks = core.banks(ctx, "projected", RING)
        used0, out0 = core.tile_multiplied.at, core.tile_evicted.at
        bank_of = lambda u: banks[(u // parts) % RING]

        def evict(eng, i, u):
            eng.wait_ge(core.tile_multiplied.sem, i * UNROLL + (u + 1 + used0))
            to = dst[:, bass.ds(i * (UNROLL // parts) + u // parts, 1), :]
            got = bank_of(u)[:, 0:T].rearrange("p (a f) -> p a f", a=1)
            ins = eng.tensor_tensor(to, got, to, ALU.add) if residual else eng.copy(to, got)
            ins.then_inc(core.tile_evicted.sem, 1)

        with nc.Block() as block:
            @block.sync
            def _(sp):
                weights.load_all(sp, total)

            @block.gpsimd
            def _(pool):
                weights.make_lo_all(pool, total)

            @block.tensor
            def _(pe):
                def multiply(i, u):
                    weights.ready(pe, i, u)
                    part = u % parts
                    if part == 0 and not fresh(i, u, RING * parts):
                        pe.wait_ge(core.tile_evicted.sem, i * (UNROLL // parts) + (u // parts - 2 + out0))
                    for k in range(KC):
                        last = weights.product(pe, bank_of(u)[:, 0:T], u, slice(k * P, (k + 1) * P),
                                               rhs_hi[:, part * KC + k, :], rhs_lo[:, part * KC + k, :],
                                               start=part == 0 and k == 0, stop=part == parts - 1 and k == KC - 1)
                    last.then_inc(core.tile_multiplied.sem, 1)
                tile_loop(pe, total, multiply)

            @block.scalar
            def _(act):
                def body(i, u):
                    weights.make_hi(act, i, u)
                    if not residual and not fresh(i, u, 2):
                        evict(act, i, u - 2)
                tile_loop(act, total, body)
                weights.hi_ahead(act, total, 0)
                for t in (1, 2):
                    if not residual:
                        evict(act, (total - RING + t) // UNROLL, (total - RING + t) % UNROLL)
                    weights.hi_ahead(act, total, t)

            if beside:
                @block.vector
                def _(dve):
                    beside(dve, out0)

            if residual:
                @block.vector
                def _(dve):
                    tile_loop(dve, total, lambda i, u: evict(dve, i, u) if u % parts == parts - 1 else None)
        core.tile_evicted.at += n
    weights.end(total)


PEER_HEADS = 8
KEYS = 128
TOPK = 16
SETS = 2 * PEER_HEADS
TOKEN_TILES = [(0, P), (P, P), (2 * P, DEC)]
LOWEST = -3.0e38


def peer_scores(core, weights, streams, h_hi, h_lo, sub_keys, scores):
    nc = core.nc
    with ExitStack() as ctx:
        queries = core.sb(ctx, "queries", [P, SETS, T])
        keys = core.sb(ctx, "keys", [P, SETS, KEYS])
        with nc.Block() as block:
            @block.sync
            def _(sp):
                core.load(sp, keys[:], sub_keys)

            @block.gpsimd
            def _(pool):
                core.pool_done.inc(pool.memset(scores[:, 2, :, :], 0.0))
        project(core, weights, streams[0], SETS, h_hi, h_lo, queries, then=streams[1], ahead=True)
        banks = core.banks(ctx, "score", 4)
        per_tile = SETS // 4
        done0, out0 = core.pe_done.at, core.act_done.at
        with nc.Block() as block:
            @block.tensor
            def _(pe):
                core.wait_loads(pe)
                for tile, (t0, rows) in enumerate(TOKEN_TILES):
                    for q in range(per_tile):
                        n = tile * per_tile + q
                        if n >= 4:
                            pe.wait_ge(core.act_done.sem, out0 + n - 3)
                        for s in range(4):
                            last = pe.matmul(banks[n % 4][0:rows, s * KEYS:(s + 1) * KEYS],
                                             queries[:, 4 * q + s, t0:t0 + rows], keys[:, 4 * q + s, :],
                                             start=True, stop=True)
                        core.pe_done.inc(last)

            @block.scalar
            def _(act):
                for tile, (t0, rows) in enumerate(TOKEN_TILES):
                    for q in range(per_tile):
                        n = tile * per_tile + q
                        act.wait_ge(core.pe_done.sem, done0 + n + 1)
                        core.act_done.inc(act.copy(scores[0:rows, tile, 4 * q:4 * q + 4, :],
                                                   banks[n % 4][0:rows, :].rearrange("p (s k) -> p s k", s=4)))


def top16(dve, link, values, sets, top, index):
    for s in range(sets):
        last = dve.max(top[:, s, 0:8], values(s))
    link(last)
    for s in range(sets):
        dve.max_index(index[:, s, 0:8], top[:, s, 0:8], values(s))
    for s in range(sets):
        last = dve.match_replace(values(s), top[:, s, 0:8], values(s), LOWEST)
    link(last)
    for s in range(sets):
        last = dve.max(top[:, s, 8:16], values(s))
    link(last)
    for s in range(sets):
        last = dve.max_index(index[:, s, 8:16], top[:, s, 8:16], values(s))
    link(last)


QUADS = T // 4
HALF = KEYS // 2
GROUP = 8


class Gates:

    def __init__(self, core, ctx, first_t, second_t, gate_hi, gate_lo):
        self.core, self.first_t, self.second_t = core, first_t, second_t
        self.gate_parts = (gate_hi.bitcast(F32), gate_lo.bitcast(F32))
        self.one_hot = core.sb(ctx, "one_hot", [P, 2, 4, KEYS], F32R)
        self.weighted = core.sb(ctx, "weighted", [P, 2, 4, 2, HALF], F32R)
        self.equal = core.sb(ctx, "equal", [P, 4, HALF], mybir.dt.uint8)
        self.low = core.sb(ctx, "low", [P, 4, HALF])

    def begin(self, half, banks, activations):
        self.half, self.banks, self.activations = half, banks, activations
        self.built0, self.made0, self.applied0 = self.core.dve_done.at, self.core.pe_done.at, self.core.pool_done.at
        self.equal0, self.summed0, self.copied0 = (self.core.gate_equal.at, self.core.gate_summed.at,
                                                   self.core.gate_copied.at)

    def build(self, dve, i, u):
        if not fresh(i, u, 2):
            dve.wait_ge(self.core.pe_done.sem, i * UNROLL + (u - 1 + self.made0))
        tokens = bass.ds(i * (4 * UNROLL) + u * 4, 4)
        each = lambda a, n: a[:, tokens].unsqueeze(2).broadcast_to((P, 4, n))
        keys = lambda first, n: self.core.index_row[:, first:first + n].unsqueeze(1).broadcast_to((P, 4, n))
        if not fresh(i, u, 1):
            dve.wait_ge(self.core.dve_done.sem, i * UNROLL + (u + self.built0))
        dve.tensor_tensor(self.equal, keys(self.half * HALF, HALF), each(self.second_t, HALF), ALU.is_equal
                          ).then_inc(self.core.gate_equal.sem, 1)
        dve.tensor_tensor(self.one_hot[:, u % 2], keys(0, KEYS), each(self.first_t, KEYS), ALU.is_equal)
        dve.wait_ge(self.core.gate_equal.sem, i * UNROLL + (u + 1 + self.equal0))
        for part, gate in enumerate(self.gate_parts):
            last = dve.tensor_tensor(self.weighted[:, u % 2, :, part], self.equal, each(gate, HALF), ALU.mult)
        last.then_inc(self.core.dve_done.sem, 1)

    def multiply(self, pe, i, u):
        pe.wait_ge(self.core.dve_done.sem, i * UNROLL + (u + 1 + self.built0))
        slots = len(self.banks)
        if not fresh(i, u, slots):
            pe.wait_ge(self.core.pool_done.sem, i * UNROLL + (u + 1 - slots + self.applied0))
        for t in range(4):
            last = pe.matmul(self.banks[u % slots][:, t * KEYS:(t + 1) * KEYS], self.one_hot[:, u % 2, t, :],
                             self.weighted[:, u % 2, t].rearrange("p a k -> p (a k)"), start=True, stop=True)
        last.then_inc(self.core.pe_done.sem, 1)

    def products(self, u):
        return self.banks[u % len(self.banks)][:, :].rearrange("p (t a k) -> p t a k", t=4, a=2)

    def copy_low(self, act, i, u):
        act.wait_ge(self.core.pe_done.sem, i * UNROLL + (u + 1 + self.made0))
        if not fresh(i, u, 1):
            act.wait_ge(self.core.gate_summed.sem, i * UNROLL + (u + self.summed0))
        act.copy(self.low, self.products(u)[:, :, 1]).then_inc(self.core.gate_copied.sem, 1)

    def apply(self, dve, i, u):
        dve.wait_ge(self.core.gate_copied.sem, i * UNROLL + (u + 1 + self.copied0))
        high = self.products(u)[:, :, 0]
        dve.tensor_tensor(high, high, self.low, ALU.add).then_inc(self.core.gate_summed.sem, 1)
        dve.wait_ge(self.core.gate_summed.sem, i * UNROLL + (u + 1 + self.summed0))
        to = self.activations[:, :, bass.ds(i * (4 * UNROLL) + u * 4, 4)].rearrange("p k t -> p t k")
        dve.tensor_tensor(to, high, to, ALU.mult).then_inc(self.core.pool_done.sem, 1)

    def step(self, dve, i, u):
        if not fresh(i, u, 2):
            self.apply(dve, i, u - 2)
        self.build(dve, i, u)

    def rest_multiplied(self, pe):
        for n in range(HALF, QUADS):
            self.multiply(pe, n // UNROLL, n % UNROLL)

    def rest_copied(self, act):
        for n in range(HALF, QUADS):
            self.copy_low(act, n // UNROLL, n % UNROLL)

    def rest_applied(self, dve):
        for n in range(HALF, QUADS):
            self.step(dve, n // UNROLL, n % UNROLL)
        for n in range(QUADS - 2, QUADS):
            self.apply(dve, n // UNROLL, n % UNROLL)

    def ended(self):
        for c in (self.core.dve_done, self.core.pe_done, self.core.pool_done, self.core.gate_equal,
                  self.core.gate_summed, self.core.gate_copied):
            c.at += QUADS


def peer_select(core, select, scores):
    top, index, index_f, pairs, best, place, rank, rank_f, hit, chosen = select

    def program(dve):
        link = Link(dve, core.dve_done)
        for tile in range(3):
            top16(dve, link, lambda s: scores[:, tile, s, :], SETS, top, index)
            dve.tensor_copy(index_f, index)
            by_head = top.rearrange("p (h c) k -> p h c k", c=2)
            link(dve.tensor_tensor(
                pairs, by_head[:, :, 0, :].unsqueeze(3).broadcast_to((P, PEER_HEADS, TOPK, TOPK)),
                by_head[:, :, 1, :].unsqueeze(2).broadcast_to((P, PEER_HEADS, TOPK, TOPK)), ALU.add))
            top16(dve, link, lambda s: pairs[:, s, :, :].rearrange("p i j -> p (i j)"), PEER_HEADS, best, place)
            dve.tensor_single_scalar(rank[:, 0], place, 4, ALU.logical_shift_right)
            dve.tensor_single_scalar(rank[:, 1], place, 15, ALU.bitwise_and)
            link(dve.tensor_tensor(chosen[:, tile, 2], best,
                                   best[:, :, 0:1].broadcast_to((P, PEER_HEADS, TOPK)), ALU.subtract))
            link(dve.tensor_copy(rank_f, rank))
            for c in range(2):
                steps = core.index_row[:, 0:TOPK].unsqueeze(1).unsqueeze(1).broadcast_to((P, PEER_HEADS, TOPK, TOPK))
                link(dve.tensor_tensor(hit, rank_f[:, c].unsqueeze(3).broadcast_to(
                    (P, PEER_HEADS, TOPK, TOPK)), steps, ALU.is_equal))
                ids = index_f.rearrange("p (h c) k -> p h c k", c=2)[:, :, c, :]
                link(dve.tensor_tensor(hit, hit, ids.unsqueeze(2).broadcast_to(
                    (P, PEER_HEADS, TOPK, TOPK)), ALU.mult))
                link(dve.tensor_reduce(chosen[:, tile, c], hit, AX_X, ALU.add))
    return program


def select_buffers(core, ctx):
    return (core.sb(ctx, "top", [P, SETS, TOPK]), core.sb(ctx, "index", [P, SETS, TOPK], U32),
            core.sb(ctx, "index_f", [P, SETS, TOPK]), core.sb(ctx, "pairs", [P, PEER_HEADS, TOPK, TOPK]),
            core.sb(ctx, "best", [P, PEER_HEADS, TOPK]), core.sb(ctx, "place", [P, PEER_HEADS, TOPK], U32),
            core.sb(ctx, "rank", [P, 2, PEER_HEADS, TOPK], U32), core.sb(ctx, "rank_f", [P, 2, PEER_HEADS, TOPK]),
            core.sb(ctx, "hit", [P, PEER_HEADS, TOPK, TOPK]), core.sb(ctx, "chosen", [P, 3, 3, PEER_HEADS, TOPK]))


def peer_turn(core, chosen, first_t, second_t, gate_hi, gate_lo):
    nc = core.nc
    with ExitStack() as ctx:
        total = core.sb(ctx, "total", [P, 3, PEER_HEADS])
        banks = core.banks(ctx, "turned", 3)
        turned = core.pe_done.at
        with nc.Block() as block:
            @block.scalar
            def _(act):
                act.activation(chosen[:, :, 2], chosen[:, :, 2], ACT.Exp)
        with nc.Block() as block:
            @block.vector
            def _(dve):
                link = Link(dve, core.dve_done)
                for tile in range(3):
                    last = dve.tensor_reduce(total[:, tile], chosen[:, tile, 2], AX_X, ALU.add)
                link(last)
                link(dve.reciprocal(total, total))
                for tile in range(3):
                    dve.tensor_tensor(chosen[:, tile, 2], chosen[:, tile, 2],
                                      total[:, tile].unsqueeze(2).broadcast_to((P, PEER_HEADS, TOPK)), ALU.mult)
        with nc.Block() as block:
            @block.tensor
            def _(pe):
                for kind in range(3):
                    for tile, (t0, rows) in enumerate(TOKEN_TILES):
                        last = pe.transpose(banks[kind][:, t0:t0 + rows],
                                            chosen[0:rows, tile, kind].rearrange("p h k -> p (h k)"),
                                            core.ident[0:rows, 0:rows])
                    core.pe_done.inc(last)

            @block.vector
            def _(dve):
                for kind, dst in enumerate((first_t, second_t)):
                    dve.wait_ge(core.pe_done.sem, turned + kind + 1)
                    dve.tensor_copy(dst, banks[kind][:, 0:T])

            @block.scalar
            def _(act):
                act.wait_ge(core.pe_done.sem, turned + 3)
                act.copy(gate_hi, banks[2][:, 0:T])
        with nc.Block() as block:
            @block.vector
            def _(dve):
                dve.tensor_tensor(gate_lo, banks[2][:, 0:T], gate_hi.bitcast(F32), ALU.subtract)


def peer_up(core, weights, stream, then, h_hi, h_lo, banks, dst, beside):
    nc = core.nc
    up0, gelu0 = core.tile_multiplied.at, core.act_done.at
    gates = beside if isinstance(beside, Gates) else None
    weights.begin(stream, then, ahead=True)
    with nc.Block() as block:
        @block.sync
        def _(sp):
            weights.load_all(sp, HALF)

        @block.gpsimd
        def _(pool):
            weights.make_lo_all(pool, HALF)

        @block.tensor
        def _(pe):
            def body(i, u):
                weights.ready(pe, i, u)
                if not fresh(i, u):
                    pe.wait_ge(core.act_done.sem, i * UNROLL + (u - 2 + gelu0))
                for k in range(KC):
                    last = weights.product(pe, banks[u % RING][:, 0:T], u, slice(k * P, (k + 1) * P),
                                           h_hi[:, k, :], h_lo[:, k, :], start=k == 0, stop=k == KC - 1)
                last.then_inc(core.tile_multiplied.sem, 1)
                if gates:
                    gates.multiply(pe, i, u)
            tile_loop(pe, HALF, body)
            if gates:
                gates.rest_multiplied(pe)

        @block.scalar
        def _(act):
            def gelu(i, u):
                act.wait_ge(core.tile_multiplied.sem, i * UNROLL + (u + 1 + up0))
                act.activation(dst[:, bass.ds(i * UNROLL + u, 1), :],
                               banks[u % RING][:, 0:T].rearrange("p (a t) -> p a t", a=1), ACT.Gelu
                               ).then_inc(core.act_done.sem, 1)

            def body(i, u):
                weights.make_hi(act, i, u)
                if not fresh(i, u):
                    if gates:
                        gates.copy_low(act, i, u - 3)
                    gelu(i, u - 3)
            tile_loop(act, HALF, body)
            for t in range(RING):
                weights.hi_ahead(act, HALF, t)
                gelu((HALF - RING + t) // UNROLL, (HALF - RING + t) % UNROLL)
                if gates:
                    gates.copy_low(act, (HALF - RING + t) // UNROLL, (HALF - RING + t) % UNROLL)
            if gates:
                gates.rest_copied(act)

        @block.vector
        def _(dve):
            if gates:
                tile_loop(dve, HALF, lambda i, u: gates.step(dve, i, u))
                gates.rest_applied(dve)
            else:
                beside(dve)
    weights.end(HALF)
    core.act_done.at += HALF
    if gates:
        gates.ended()


def peer_down(core, weights, stream, then, activations, a_hi, a_lo, sums, tiles, opens, gates=None):
    nc = core.nc
    hi0, lo0 = core.gated_hi.at, core.gated_lo.at
    weights.begin(stream, then, ahead=True)
    with nc.Block() as block:
        @block.sync
        def _(sp):
            weights.load_all(sp, HALF)

        @block.gpsimd
        def _(pool):
            weights.make_lo_all(pool, HALF)

        @block.scalar
        def _(act):
            def body(i, u):
                weights.make_hi(act, i, u)
                if gates and not fresh(i, u):
                    gates.copy_low(act, i, u - 3)
                act.copy(a_hi[:, u % RING:u % RING + 1, :], activations[:, bass.ds(i * UNROLL + u, 1), :]
                         ).then_inc(core.gated_hi.sem, 1)
            tile_loop(act, HALF, body)
            for t in range(RING):
                weights.hi_ahead(act, HALF, t)
                if gates:
                    gates.copy_low(act, (HALF - RING + t) // UNROLL, (HALF - RING + t) % UNROLL)
            if gates:
                gates.rest_copied(act)

        @block.vector
        def _(dve):
            def body(i, u):
                slot = slice(u % RING, u % RING + 1)
                dve.wait_ge(core.gated_hi.sem, i * UNROLL + (u + 1 + hi0))
                dve.tensor_tensor(a_lo[:, slot, :], activations[:, bass.ds(i * UNROLL + u, 1), :],
                                  a_hi[:, slot, :].bitcast(F32), ALU.subtract).then_inc(core.gated_lo.sem, 1)
                if gates:
                    gates.step(dve, i, u)
            tile_loop(dve, HALF, body)
            if gates:
                gates.rest_applied(dve)

        @block.tensor
        def _(pe):
            def body(i, u):
                weights.ready(pe, i, u)
                pe.wait_ge(core.gated_lo.sem, i * UNROLL + (u + 1 + lo0))
                for n, d in enumerate(tiles):
                    last = weights.product(pe, sums[d][:, 0:T], u, slice(n * P, (n + 1) * P), a_hi[:, u % RING, :],
                                           a_lo[:, u % RING, :], start=fresh(i, u, 1) and d in opens, stop=False)
                last.then_inc(core.tile_multiplied.sem, 1)
                if gates:
                    gates.multiply(pe, i, u)
            tile_loop(pe, HALF, body)
            if gates:
                gates.rest_multiplied(pe)
    weights.end(HALF)
    core.gated_hi.at += HALF
    core.gated_lo.at += HALF
    if gates:
        gates.ended()


def peer_down_last(core, weights, stream, then, activations, a_hi, a_lo, total):
    nc = core.nc
    groups = HALF // GROUP
    hi0, lo0 = core.gated_hi.at, core.gated_lo.at
    weights.begin(stream, then)
    group = lambda u: activations[:, u * GROUP:(u + 1) * GROUP, :]
    with nc.Block() as block:
        @block.sync
        def _(sp):
            weights.load_all(sp, groups)

        @block.gpsimd
        def _(pool):
            for g in range(groups):
                weights.make_lo(pool, 0, g)

        @block.scalar
        def _(act):
            for g in range(groups):
                weights.make_hi(act, 0, g)
                act.copy(a_hi[:, g % RING], group(g)).then_inc(core.gated_hi.sem, 1)

        @block.vector
        def _(dve):
            for g in range(groups):
                dve.wait_ge(core.gated_hi.sem, hi0 + g + 1)
                dve.tensor_tensor(a_lo[:, g % RING], group(g), a_hi[:, g % RING].bitcast(F32), ALU.subtract
                                  ).then_inc(core.gated_lo.sem, 1)

        @block.tensor
        def _(pe):
            for g in range(groups):
                weights.ready(pe, 0, g)
                pe.wait_ge(core.gated_lo.sem, lo0 + g + 1)
                for j in range(GROUP):
                    last = weights.product(pe, total[:, 0:T], g, slice(j * P, (j + 1) * P), a_hi[:, g % RING, j, :],
                                           a_lo[:, g % RING, j, :], start=False, stop=False)
                last.then_inc(core.tile_multiplied.sem, 1)
    weights.end(groups)
    core.gated_hi.at += groups
    core.gated_lo.at += groups


def peer(core, x, norm_w, w_q, sub_keys, up_w, down_w, then=None):
    nc = core.nc
    lower_up, upper_up = Stream(up_w, 0), Stream(up_w, HALF)
    lower_down, upper_down = Stream(down_w, 0, slice(0, D_MODEL - P)), Stream(down_w, HALF)
    last_down = Stream(down_w.rearrange("(a g) p f -> a p g f", g=GROUP), 0, slice(D_MODEL - P, D_MODEL))
    with ExitStack() as ctx:
        h_hi = core.sb(ctx, "ffn_in_hi", [P, KC, T], F32R)
        h_lo = core.sb(ctx, "ffn_in_lo", [P, KC, T], F32R)
        first_t = core.sb(ctx, "first_t", [P, T])
        second_t = core.sb(ctx, "second_t", [P, T])
        gate_hi = core.sb(ctx, "gate_hi", [P, T], F32R)
        gate_lo = core.sb(ctx, "gate_lo", [P, T], F32R)
        lower_half = core.sb(ctx, "lower_half", [P, HALF, T])
        weights = Weights(core, ctx)
        with ExitStack() as select, ExitStack() as ps:
            with ExitStack() as local:
                h = core.sb(local, "ffn_in", [P, KC, T])
                rms_norm(core, x, norm_w, h, h_hi, h_lo)
            scores = core.sb(select, "scores", [P, 3, SETS, KEYS])
            peer_scores(core, weights, (w_q, lower_up), h_hi, h_lo, sub_keys, scores)
            buffers = select_buffers(core, select)
            banks = core.banks(ps, "up", RING)
            peer_up(core, weights, lower_up, upper_up, h_hi, h_lo, banks, lower_half,
                    peer_select(core, buffers, scores))
            peer_turn(core, buffers[-1], first_t, second_t, gate_hi, gate_lo)
        gates = Gates(core, ctx, first_t, second_t, gate_hi, gate_lo)
        with ExitStack() as local:
            upper_half = core.sb(local, "upper_half", [P, HALF, T])
            with ExitStack() as ps:
                banks = core.banks(ps, "up", RING)
                gates.begin(0, core.banks(ps, "gates", 2), lower_half)
                peer_up(core, weights, upper_up, lower_down, h_hi, h_lo, banks, upper_half, gates)
            sums = core.banks(ctx, "down", KC)
            gates.begin(1, sums[KC - 1:], upper_half)
            a_hi, a_lo = h_hi[:, 0:RING, :], h_lo[:, 0:RING, :]
            peer_down(core, weights, lower_down, upper_down, lower_half, a_hi, a_lo, sums, range(KC - 1),
                      range(KC - 1), gates)
            peer_down(core, weights, upper_down, last_down, upper_half, a_hi, a_lo, sums, range(KC), (KC - 1,))
        with ExitStack() as local:
            groups_hi = core.sb(local, "groups_hi", [P, RING, GROUP, T], F32R)
            groups_lo = core.sb(local, "groups_lo", [P, RING, GROUP, T], F32R)
            peer_down_last(core, weights, last_down, then, lower_half, groups_hi, groups_lo, sums[KC - 1])
        with nc.Block() as block:
            @block.vector
            def _(dve):
                for d in range(KC):
                    dve.tensor_tensor(x[:, d, :], sums[d][:, 0:T], x[:, d, :], ALU.add)


HALVES = SEQ // P
CHUNK = 64
CHUNKS = SEQ // CHUNK
RWKV_TILES = 4
SHIFT_TILES = 14
AB_TILES = 30
GN_EPS = 64e-5
L2_EPS = 1e-12
DECAY_SCALE = -0.6065306597126334

AB_PARAM = {}
_at = 0
for _name, _n in (("norm", 8), ("mu", 14), ("w0", 4), ("a0", 4), ("k_k", 4), ("k_a", 4), ("r_k", 4), ("gn_w", 4),
                  ("gn_b", 4), ("bound", 4), ("hgrn_norm", 1)):
    AB_PARAM[_name] = slice(_at, _at + _n)
    _at += _n
AB_PARAMS = _at

MASK_QUAD = 0
MASK_LOWER = 4
MASK_LEVEL = 5
MASK_FIRST = 12
MASK_CAUSAL = 13
MASK_EYE64 = 14
MASK_SCAN64 = 15
MASK_SCAN128 = 17
MASK_BLOCKS = 19
MASKS = 20


def masks():
    import numpy as np
    s, t = np.arange(P)[:, None], np.arange(P)[None, :]
    m = np.zeros((P, MASKS, P), np.float32)
    same = s // CHUNK == t // CHUNK
    m[:, 0], m[:, 1], m[:, 2], m[:, 3] = same & (s < t), same & (s <= t), same & (s < t), same & (s <= t)
    m[:, MASK_LOWER] = same & (t < s)
    for level in range(7):
        w = 1 << level
        m[:, MASK_LEVEL + level] = (s // (2 * w) == t // (2 * w)) & (s % (2 * w) < w) & (t % (2 * w) >= w)
    m[:, MASK_FIRST] = m[:, MASK_LEVEL].T
    m[:, MASK_CAUSAL] = s <= t
    m[:, MASK_EYE64] = (s % 64 == t) & (t < 64)
    m[:, MASK_SCAN64:MASK_SCAN64 + 2] = (np.arange(SEQ) % 64 != 0).reshape(2, P)
    m[:, MASK_SCAN128:MASK_SCAN128 + 2] = (np.arange(SEQ) % 128 != 0).reshape(2, P)
    m[:, MASK_BLOCKS] = same
    return m


def sum_features(core, weights, src, banks, n, start=0, width=T):
    with core.nc.Block() as block:
        @block.tensor
        def _(pe):
            for i in range(n):
                pe.matmul(banks[start + i][:, 0:width], weights, src[:, i, :], start=True, stop=True)


def head_norm(core, ones, o, scale, eps, finish, centre=False):
    nc = core.nc
    n = o.shape[1]
    with ExitStack() as ctx:
        squares = core.sb(ctx, "squares", [P, n, T])
        root = core.sb(ctx, "root", [P, n, T])
        means = core.banks(ctx, "means", n) if centre else []
        banks = core.banks(ctx, "norm", n)
        summed0, squared0, centred0, var0 = (core.pe_done.at, core.act_done.at, core.gated_hi.at, core.gated_lo.at)
        with nc.Block() as block:
            @block.tensor
            def _(pe):
                for i in range(len(means)):
                    core.pe_done.inc(pe.matmul(means[i][:, 0:T], ones, o[:, i, :], start=True, stop=True))
                for i in range(n):
                    pe.wait_ge(core.act_done.sem, squared0 + i + 1)
                    core.pe_done.inc(pe.matmul(banks[i][:, 0:T], ones, squares[:, i, :], start=True, stop=True))

            @block.scalar
            def _(act):
                for i in range(n):
                    if centre:
                        act.wait_ge(core.gated_hi.sem, centred0 + i + 1)
                    core.act_done.inc(act.activation(squares[:, i, :], o[:, i, :], ACT.Square))
                for i in range(n):
                    act.wait_ge(core.gated_lo.sem, var0 + i + 1)
                    core.act_done.inc(act.activation(root[:, i, :], root[:, i, :], ACT.Sqrt))

            @block.vector
            def _(dve):
                link = Link(dve, core.dve_done)
                for i in range(len(means)):
                    dve.wait_ge(core.pe_done.sem, summed0 + i + 1)
                    core.gated_hi.inc(dve.scalar_tensor_tensor(o[:, i, :], means[i][:, 0:T], -scale, o[:, i, :],
                                                               ALU.mult, ALU.add))
                for i in range(n):
                    dve.wait_ge(core.pe_done.sem, summed0 + len(means) + i + 1)
                    core.gated_lo.inc(dve.tensor_scalar(root[:, i, :], banks[i][:, 0:T], scale, eps,
                                                        ALU.mult, ALU.add))
                for i in range(n):
                    dve.wait_ge(core.act_done.sem, squared0 + n + i + 1)
                    last = dve.reciprocal(root[:, i, :], root[:, i, :])
                link(last)
                finish(dve, link, root)


def shift_beside(core, params, p, shift, last_rows, diff):
    def program(dve, out0):
        done0 = core.mixed.at
        core.wait_loads(dve)

        def one(i, u):
            tile = bass.ds(i * UNROLL + u, 1)
            old = p[:, tile, :]
            dve.wait_ge(core.tile_evicted.sem, i * UNROLL + (u + 1 + out0))
            if not fresh(i, u, 1):
                dve.wait_ge(core.mixed.sem, i * (2 * UNROLL) + (2 * u + done0))
            dve.tensor_copy(last_rows[:, tile, :], old[:, :, SEQ - 1:T])
            dve.tensor_tensor(diff[:, :, 1:SEQ], old[:, :, 0:SEQ - 1], old[:, :, 1:SEQ], ALU.subtract)
            dve.tensor_scalar(diff[:, :, 0:1], old[:, :, 0:1], -1.0, None, ALU.mult)
            dve.tensor_tensor(diff[:, :, SEQ:T], shift[:, tile, :], old[:, :, SEQ:T], ALU.subtract
                              ).then_inc(core.mixed.sem, 1)
            dve.wait_ge(core.mixed.sem, i * (2 * UNROLL) + (2 * u + 1 + done0))
            mu = params[:, bass.ds(i * UNROLL + (AB_PARAM["mu"].start + u), 1)]
            dve.scalar_tensor_tensor(old, diff, mu, old, ALU.mult, ALU.add).then_inc(core.mixed.sem, 1)
        tile_loop(dve, SHIFT_TILES, one)
        core.mixed.at += 2 * SHIFT_TILES
    return program


def rwkv_inputs(core, ctx, p, par, mask, lora, gup, w):
    nc = core.nc
    tile4 = [P, RWKV_TILES, T]
    for name in ("logw", "gate", "kk", "b", "bonus"):
        w[name] = core.sb(ctx, name, tile4)
    w["m"] = m = p[:, 0:SHIFT_TILES, :]
    w["key"] = m[:, 4:8, :]
    with ExitStack() as local:
        hidden = core.sb(local, "hidden", [P, 2, T])
        work = core.sb(local, "work", tile4)
        rate = core.sb(local, "rate", tile4)
        key_scale = core.sb(local, "key_scale", tile4)
        with nc.Block() as block:
            @block.scalar
            def _(act):
                act.activation(hidden[0:64, 0, :], m[0:64, 12, :], ACT.Tanh)
                act.copy(hidden[64:128, 0, :], m[64:128, 12, :])
                act.activation(hidden[:, 1, :], m[:, 13, :], ACT.Sigmoid)
        with ExitStack() as ps:
            banks = core.banks(ps, "lora", 8)
            with nc.Block() as block:
                @block.tensor
                def _(pe):
                    for i in range(RWKV_TILES):
                        pe.matmul(banks[i][:, 0:T], lora[0:64, i * P:(i + 1) * P], hidden[0:64, 0, :],
                                  start=True, stop=True)
                        pe.matmul(banks[4 + i][:, 0:T], lora[64:128, i * P:(i + 1) * P], hidden[64:128, 0, :],
                                  start=True, stop=True)
            with nc.Block() as block:
                @block.scalar
                def _(act):
                    for i in range(RWKV_TILES):
                        act.activation(w["logw"][:, i, :], banks[i][:, 0:T], ACT.Sigmoid, bias=par("w0", i))
                        act.activation(rate[:, i, :], banks[4 + i][:, 0:T], ACT.Sigmoid, bias=par("a0", i))

                @block.vector
                def _(dve):
                    link = Link(dve, core.dve_done)
                    for i in range(RWKV_TILES):
                        last = dve.tensor_scalar(w["kk"][:, i, :], m[:, 4 + i, :], par("k_k", i), None, ALU.mult)
                    link(last)
                    dve.tensor_tensor(work, w["kk"], w["kk"], ALU.mult)
            with nc.Block() as block:
                @block.tensor
                def _(pe):
                    for i in range(RWKV_TILES):
                        pe.matmul(banks[i][:, 0:T], gup[:, i * P:(i + 1) * P], hidden[:, 1, :], start=True, stop=True)
                        pe.matmul(banks[4 + i][:, 0:T], core.block_ones, work[:, i, :], start=True, stop=True)

                @block.vector
                def _(dve):
                    link = Link(dve, core.dve_done)
                    dve.tensor_scalar(w["logw"], w["logw"], DECAY_SCALE, None, ALU.mult)
                    for i in range(RWKV_TILES):
                        last = dve.tensor_scalar(key_scale[:, i, :], rate[:, i, :], -1.0, par("k_a", i),
                                                 ALU.add, ALU.mult)
                    link(last)
                    dve.scalar_tensor_tensor(w["key"], key_scale, 1.0, m[:, 4:8, :], ALU.add, ALU.mult)
            with nc.Block() as block:
                @block.scalar
                def _(act):
                    for i in range(RWKV_TILES):
                        act.activation(work[:, i, :], banks[4 + i][:, 0:T], ACT.Sqrt)
                    for i in range(RWKV_TILES):
                        act.copy(w["gate"][:, i, :], banks[i][:, 0:T])
            with nc.Block() as block:
                @block.vector
                def _(dve):
                    link = Link(dve, core.dve_done)
                    link(dve.tensor_scalar(work, work, L2_EPS, None, ALU.max))
                    link(dve.reciprocal(work, work))
                    link(dve.tensor_tensor(w["kk"], w["kk"], work, ALU.mult))
                    dve.tensor_tensor(w["b"], w["kk"], rate, ALU.mult)
                    for i in range(RWKV_TILES):
                        dve.scalar_tensor_tensor(work[:, i, :], m[:, i, :], par("r_k", i), w["key"][:, i, :],
                                                 ALU.mult, ALU.mult)
            sum_features(core, core.block_ones, work, banks, RWKV_TILES)
            with nc.Block() as block:
                @block.vector
                def _(dve):
                    for i in range(RWKV_TILES):
                        dve.tensor_tensor(w["bonus"][:, i, :], banks[i][:, 0:T], m[:, 8 + i, :], ALU.mult)


def rwkv_prompt(core, mask, w, out, state_out, aside):
    nc = core.nc
    combos = [(hp, tile, half) for hp in range(2) for tile in range(RWKV_TILES) for half in range(HALVES)]
    combo_of = {c: n for n, c in enumerate(combos)}
    with ExitStack() as ctx:
        ar = core.sb(ctx, "ar", [P, RWKV_TILES, HALVES, 2, P])
        bh = core.sb(ctx, "bh", [P, RWKV_TILES, SEQ])
        kh = core.sb(ctx, "kh", [P, RWKV_TILES, SEQ])
        end_decay = core.sb(ctx, "end_decay", [P, CHUNKS, RWKV_TILES, P])
        prompt = lambda name: w[name][:, :, 0:SEQ]
        with ExitStack() as local:
            decay = core.sb(local, "decay", [P, RWKV_TILES, SEQ])
            grow = core.sb(local, "grow", [P, RWKV_TILES, SEQ])
            before = core.sb(local, "before", [P, RWKV_TILES, SEQ])
            logs = core.sb(local, "logs", [P, RWKV_TILES, SEQ])
            with nc.Block() as block:
                @block.vector
                def _(dve):
                    link = Link(dve, core.dve_done)
                    for i in range(RWKV_TILES):
                        last = dve.tensor_tensor_scan(logs[:, i, :], mask[:, MASK_SCAN64:MASK_SCAN64 + 2, :].rearrange(
                            "p a b -> p (a b)"), w["logw"][:, i, 0:SEQ], 0.0, ALU.mult, ALU.add)
                    link(last)
                    dve.tensor_tensor(before, logs, prompt("logw"), ALU.subtract)
            with nc.Block() as block:
                @block.scalar
                def _(act):
                    act.activation(decay, logs, ACT.Exp)
                    act.activation(grow, logs, ACT.Exp, scale=-1.0)
                    act.activation(before, before, ACT.Exp)
            with nc.Block() as block:
                @block.vector
                def _(dve):
                    for i in range(RWKV_TILES):
                        split = lambda a: a.rearrange("p (h j) -> p h j", h=HALVES)
                        dve.scalar_tensor_tensor(ar[:, i, :, 0, :], split(before[:, i, :]), -1.0,
                                                 split(w["kk"][:, i, 0:SEQ]), ALU.mult, ALU.mult)
                        dve.tensor_tensor(ar[:, i, :, 1, :], split(decay[:, i, :]), split(w["m"][:, i, 0:SEQ]), ALU.mult)
                    dve.tensor_tensor(bh, grow, prompt("b"), ALU.mult)
                    dve.tensor_tensor(kh, grow, prompt("key"), ALU.mult)

                @block.gpsimd
                def _(pool):
                    for c in range(CHUNKS):
                        at = c * CHUNK + CHUNK - 1
                        pool.tensor_tensor(end_decay[:, c], decay[:, :, at:at + 1].broadcast_to((P, RWKV_TILES, P)),
                                           core.block_ones.unsqueeze(1).broadcast_to((P, RWKV_TILES, P)), ALU.mult)
        quad = core.sb(ctx, "quad", [P, 16, 4, P])
        lower = core.sb(ctx, "lower", [P, 16, P])
        tu = core.sb(ctx, "tu", [P, 16, 2, P])
        toks = core.sb(ctx, "toks", [P, 3, HALVES, 512])
        with ExitStack() as ps:
            banks = core.banks(ps, "inside", 4)
            lows = core.banks(ps, "lower", 4)
            done0, out0 = core.pe_done.at, core.dve_done.at
            with nc.Block() as block:
                @block.tensor
                def _(pe):
                    for n, (hp, tile, half) in enumerate(combos):
                        rows, cols = slice(64 * hp, 64 * hp + 64), slice(half * P, half * P + P)
                        if n >= 4:
                            pe.wait_ge(core.dve_done.sem, out0 + n - 3)
                        rhs = ar[rows, tile, half].rearrange("p a j -> p (a j)")
                        pe.matmul(banks[n % 4][:, 0:256], bh[rows, tile, cols], rhs, start=True, stop=True)
                        core.pe_done.inc(pe.matmul(banks[n % 4][:, 256:512], kh[rows, tile, cols], rhs,
                                                   start=True, stop=True))
                    for n, (hp, tile, half) in enumerate(combos):
                        rows, cols = slice(64 * hp, 64 * hp + 64), slice(half * P, half * P + P)
                        last = pe.matmul(lows[n // 4][:, (n % 4) * P:(n % 4 + 1) * P], ar[rows, tile, half, 0, :],
                                         bh[rows, tile, cols], start=True, stop=True)
                    core.pe_done.inc(last)

                @block.scalar
                def _(act):
                    aside(act)

                @block.vector
                def _(dve):
                    for n in range(16):
                        dve.wait_ge(core.pe_done.sem, done0 + n + 1)
                        core.dve_done.inc(dve.tensor_tensor(
                            quad[:, n].rearrange("p a j -> p (a j)"), banks[n % 4][:, :],
                            mask[:, MASK_QUAD:MASK_QUAD + 4, :].rearrange("p a j -> p (a j)"), ALU.mult))
                    dve.wait_ge(core.pe_done.sem, done0 + 17)
                    for g in range(4):
                        dve.tensor_tensor(lower[:, 4 * g:4 * g + 4, :],
                                          lows[g][:, :].rearrange("p (a j) -> p a j", a=4),
                                          mask[:, MASK_LOWER:MASK_LOWER + 1, :].broadcast_to((P, 4, P)), ALU.mult)
        with ExitStack() as ps:
            banks = core.banks(ps, "turned", 6)
            done0 = core.pe_done.at
            with nc.Block() as block:
                @block.tensor
                def _(pe):
                    for kind, src in enumerate((w["m"][:, 8:12, :], bh, kh)):
                        for half in range(HALVES):
                            for tile in range(RWKV_TILES):
                                last = pe.transpose(banks[kind * 2 + half][:, tile * P:(tile + 1) * P],
                                                    src[:, tile, half * P:(half + 1) * P], core.ident)
                            core.pe_done.inc(last)

                @block.scalar
                def _(act):
                    for n in range(6):
                        act.wait_ge(core.pe_done.sem, done0 + n + 1)
                        act.copy(toks[:, n // 2, n % 2, :], banks[n][:, :])

                @block.vector
                def _(dve):
                    link = Link(dve, core.dve_done)
                    wide = lambda k: mask[:, k:k + 1, :].broadcast_to((P, 16, P))
                    dve.tensor_tensor(tu[:, :, 0, :], lower, wide(MASK_FIRST), ALU.mult)
                    link(dve.tensor_tensor(tu[:, :, 1, :], quad[:, :, 0, :], wide(MASK_LEVEL), ALU.mult))
                    eye = core.ident.unsqueeze(1).broadcast_to((P, 16, P))
                    dve.tensor_tensor(tu[:, :, 0, :], tu[:, :, 0, :], eye, ALU.add)
                    dve.tensor_tensor(tu[:, :, 1, :], tu[:, :, 1, :], eye, ALU.add)
        with ExitStack() as ps:
            part = core.sb(ps, "part", [P, 2, 16, P])
            product = lower.rearrange("p (g a) j -> p g (a j)", g=4)
            first = core.banks(ps, "first", 4)
            second = core.banks(ps, "second", 4)
            levels = 5
            part0, first0, copied0, second0, added0 = (core.pool_done.at, core.pe_done.at, core.act_done.at,
                                                       core.tile_multiplied.at, core.dve_done.at)
            with nc.Block() as block:
                @block.gpsimd
                def _(pool):
                    for level in range(levels):
                        if level >= 2:
                            pool.wait_ge(core.pe_done.sem, first0 + 4 * (level - 1))
                        core.pool_done.inc(pool.tensor_tensor(
                            part[:, level % 2], quad[:, :, 0, :],
                            mask[:, MASK_LEVEL + 1 + level:MASK_LEVEL + 2 + level, :].broadcast_to((P, 16, P)),
                            ALU.mult))

                @block.tensor
                def _(pe):
                    for level in range(levels):
                        pe.wait_ge(core.pool_done.sem, part0 + level + 1)
                        for g in range(4):
                            if level:
                                pe.wait_ge(core.dve_done.sem, added0 + (level - 1) * 8 + 2 * g + 2)
                            for c in range(4 * g, 4 * g + 4):
                                last = pe.matmul(first[g][:, (c % 4) * P:(c % 4 + 1) * P], part[:, level % 2, c, :],
                                                 tu[:, c, 0, :], start=True, stop=True)
                            core.pe_done.inc(last)
                        for g in range(4):
                            pe.wait_ge(core.act_done.sem, copied0 + level * 4 + g + 1)
                            for c in range(4 * g, 4 * g + 4):
                                n = (level * 16 + c) // 2
                                if c % 2 == 0 and n >= 4:
                                    pe.wait_ge(core.dve_done.sem, added0 + n - 3)
                                o = (c % 2) * 256
                                y = product[:, g, (c % 4) * P:(c % 4 + 1) * P]
                                if level < levels - 1:
                                    pe.matmul(second[n % 4][:, o:o + P], tu[:, c, 1, :], y, start=True, stop=True)
                                last = pe.matmul(second[n % 4][:, o + P:o + 2 * P], y, tu[:, c, 1, :],
                                                 start=True, stop=True)
                                if c % 2:
                                    core.tile_multiplied.inc(last)

                @block.scalar
                def _(act):
                    for level in range(levels):
                        for g in range(4):
                            act.wait_ge(core.pe_done.sem, first0 + level * 4 + g + 1)
                            if level:
                                act.wait_ge(core.tile_multiplied.sem, second0 + (level - 1) * 8 + 2 * g + 2)
                            core.act_done.inc(act.copy(product[:, g, :], first[g][:, :]))

                @block.vector
                def _(dve):
                    for n in range(levels * 8):
                        c = (2 * n) % 16
                        dve.wait_ge(core.tile_multiplied.sem, second0 + n + 1)
                        parts = slice(0, 2) if n < (levels - 1) * 8 else slice(1, 2)
                        to = tu[:, c:c + 2, parts, :]
                        got = second[n % 4][:, :].rearrange("p (c a j) -> p c a j", c=2, a=2)[:, :, parts, :]
                        core.dve_done.inc(dve.tensor_tensor(to, got, to, ALU.add))
        with ExitStack() as ps:
            state = core.sb(ps, "state", [P, RWKV_TILES, P])
            grown = core.sb(ps, "grown", [P, RWKV_TILES, P])
            rhs = core.sb(ps, "rhs", [P, 512])
            sa = core.sb(ps, "sa", [P, 512])
            b_rhs, b_sa, b_out, b_state = core.banks(ps, "chunk", 4)
            with nc.Block() as block:
                @block.gpsimd
                def _(pool):
                    pool.memset(state, 0.0)
                    pool.memset(rhs, 0.0)
                    pool.memset(sa, 0.0)
            pe0, act0, dve0 = core.pe_done.at, core.act_done.at, core.dve_done.at
            v_tok, b_tok, k_tok = 0, 1, 2
            with nc.Block() as block:
                @block.tensor
                def _(pe):
                    for c in range(CHUNKS):
                        half, base = c // 2, CHUNK * (c % 2)
                        at = slice(base, base + CHUNK)
                        if c:
                            pe.wait_ge(core.dve_done.sem, dve0 + 2 * c)
                        for tile in range(RWKV_TILES):
                            pe.matmul(b_rhs[at, tile * P:(tile + 1) * P], ar[:, tile, half, 0, at], state[:, tile, :],
                                      start=True, stop=False, skip_group_check=True)
                            for hp in range(2):
                                cols = slice(tile * P + 64 * hp, tile * P + 64 * hp + 64)
                                last = pe.matmul(b_rhs[at, cols], quad[:, combo_of[hp, tile, half], 2, at],
                                                 toks[:, v_tok, half, cols], start=False, stop=hp == 1,
                                                 skip_group_check=True)
                        core.pe_done.inc(last)
                        pe.wait_ge(core.act_done.sem, act0 + 3 * c + 1)
                        for tile in range(RWKV_TILES):
                            for hp in range(2):
                                cols = slice(tile * P + 64 * hp, tile * P + 64 * hp + 64)
                                last = pe.matmul(b_sa[at, cols], tu[:, combo_of[hp, tile, half], 1, at], rhs[:, cols],
                                                 start=True, stop=True)
                        core.pe_done.inc(last)
                        pe.wait_ge(core.act_done.sem, act0 + 3 * c + 2)
                        for tile in range(RWKV_TILES):
                            cols = slice(tile * P, (tile + 1) * P)
                            pe.matmul(b_state[:, cols], toks[at, b_tok, half, cols], sa[at, cols],
                                      start=True, stop=False)
                            last = pe.matmul(b_state[:, cols], toks[at, k_tok, half, cols],
                                             toks[at, v_tok, half, cols], start=False, stop=True)
                        core.pe_done.inc(last)
                        for tile in range(RWKV_TILES):
                            to = slice(tile * CHUNK, (tile + 1) * CHUNK)
                            pe.matmul(b_out[:, to], state[:, tile, :], ar[:, tile, half, 1, at],
                                      start=True, stop=False, skip_group_check=True)
                            for hp in range(2):
                                cols = slice(tile * P + 64 * hp, tile * P + 64 * hp + 64)
                                head = slice(64 * hp, 64 * hp + 64)
                                n = combo_of[hp, tile, half]
                                pe.matmul(b_out[head, to], sa[:, cols], quad[:, n, 1, at],
                                          start=False, stop=False, skip_group_check=True)
                                last = pe.matmul(b_out[head, to], toks[:, v_tok, half, cols], quad[:, n, 3, at],
                                                 start=False, stop=True, skip_group_check=True)
                        core.pe_done.inc(last)

                @block.scalar
                def _(act):
                    for c in range(CHUNKS):
                        at = slice(CHUNK * (c % 2), CHUNK * (c % 2) + CHUNK)
                        act.wait_ge(core.pe_done.sem, pe0 + 4 * c + 1)
                        core.act_done.inc(act.copy(rhs[at, :], b_rhs[at, :]))
                        act.wait_ge(core.pe_done.sem, pe0 + 4 * c + 2)
                        core.act_done.inc(act.copy(sa[at, :], b_sa[at, :]))
                        act.wait_ge(core.pe_done.sem, pe0 + 4 * c + 4)
                        core.act_done.inc(act.copy(out[:, 0:4, c * CHUNK:(c + 1) * CHUNK],
                                                   b_out[:, 0:256].rearrange("p (a j) -> p a j", a=4)))

                @block.vector
                def _(dve):
                    for c in range(CHUNKS):
                        dve.wait_ge(core.pe_done.sem, pe0 + 4 * c + 3)
                        link = Link(dve, core.dve_done)
                        link(dve.tensor_tensor(grown, b_state[:, :].rearrange("p (a j) -> p a j", a=4), state, ALU.add))
                        dve.wait_ge(core.pe_done.sem, pe0 + 4 * c + 4)
                        core.dve_done.inc(dve.tensor_tensor(state, grown, end_decay[:, c], ALU.mult))
            with nc.Block() as block:
                @block.sync
                def _(sp):
                    core.stored.inc(sp.dma_start(state_out, state), 16)
                    sp.wait_ge(core.stored.sem, core.stored.at)


def rwkv_sample(core, mask, w, out, state_in, state_out):
    nc = core.nc
    wide = [P, RWKV_TILES, DEC, 64]
    with ExitStack() as ctx:
        state = core.sb(ctx, "state", wide)
        new = core.sb(ctx, "new", wide)
        work = core.sb(ctx, "work", wide)
        values = core.sb(ctx, "values", wide)
        decay = core.sb(ctx, "decay", [P, RWKV_TILES, DEC])
        reads = core.banks(ctx, "reads", 4)
        spread = core.banks(ctx, "spread", 4)
        each = lambda a: a.unsqueeze(3).broadcast_to(tuple(wide))
        sample = lambda name: each(w[name][:, :, SEQ:T])
        mixed = lambda i: each(w["m"][:, i:i + 4, SEQ:T])
        eye = mask[:, MASK_EYE64, 0:64].unsqueeze(1).unsqueeze(1).broadcast_to(tuple(wide))
        got = lambda bank: bank[:, :].rearrange("p (b v) -> p b v", b=DEC)
        flat = lambda a, tile: a[:, tile].rearrange("p b v -> p (b v)")
        with nc.Block() as block:
            @block.sync
            def _(sp):
                core.load(sp, state, state_in)

            @block.scalar
            def _(act):
                act.activation(decay, w["logw"][:, :, SEQ:T], ACT.Exp)

            @block.vector
            def _(dve):
                dve.tensor_tensor(values, eye, mixed(8), ALU.mult)
                core.wait_loads(dve)
                dve.tensor_tensor(work, state, sample("kk"), ALU.mult)
        with nc.Block() as block:
            @block.tensor
            def _(pe):
                for tile in range(RWKV_TILES):
                    pe.matmul(reads[tile][:, :], core.block_ones, flat(work, tile), start=True, stop=True)
                    pe.matmul(spread[tile][:, :], core.block_ones, flat(values, tile), start=True, stop=True)

            @block.vector
            def _(dve):
                dve.tensor_tensor(new, state, each(decay), ALU.mult)
        with nc.Block() as block:
            @block.vector
            def _(dve):
                link = Link(dve, core.dve_done)
                for tile in range(RWKV_TILES):
                    dve.tensor_tensor(work[:, tile], got(reads[tile]), sample("b")[:, tile], ALU.mult)
                    last = dve.tensor_tensor(values[:, tile], got(spread[tile]), sample("key")[:, tile], ALU.mult)
                link(last)
                link(dve.tensor_tensor(new, new, work, ALU.subtract))
                link(dve.tensor_tensor(new, new, values, ALU.add))
                dve.tensor_tensor(work, new, mixed(0), ALU.mult)
        with nc.Block() as block:
            @block.tensor
            def _(pe):
                for tile in range(RWKV_TILES):
                    pe.matmul(reads[tile][:, :], core.block_ones, flat(work, tile), start=True, stop=True)

            @block.sync
            def _(sp):
                core.stored.inc(sp.dma_start(state_out, new), 16)
        with nc.Block() as block:
            @block.sync
            def _(sp):
                sp.wait_ge(core.stored.sem, core.stored.at)

            @block.vector
            def _(dve):
                link = Link(dve, core.dve_done)
                for tile in range(RWKV_TILES):
                    last = dve.tensor_tensor(values[:, tile], got(reads[tile]), eye[:, tile], ALU.mult)
                link(last)
                dve.tensor_reduce(out[:, 0:4, SEQ:T], values, AX_X, ALU.add)


def rwkv_output(core, par, w, out):
    o = out[:, 0:4, :]

    def finish(dve, link, root):
        link(dve.tensor_tensor(o, o, root, ALU.mult))
        for i in range(RWKV_TILES):
            last = dve.tensor_scalar(out[:, i, :], out[:, i, :], par("gn_w", i), par("gn_b", i), ALU.mult, ALU.add)
        link(last)
        link(dve.tensor_tensor(o, o, w["bonus"], ALU.add))
        dve.tensor_tensor(o, o, w["gate"], ALU.mult)
    head_norm(core, core.block_ones, o, 1.0 / 64, GN_EPS, finish, centre=True)


HGRN_TILES = 4
LEVELS = 7
SMALLEST_LOG = 1.0842021724855044e-19


def hgrn_prompt(core, mask, values, q, key, logs, out, state_out, sample_reads):
    nc = core.nc
    flat = lambda a: a.rearrange("p t n -> p (t n)")
    with ExitStack() as ctx:
        att = core.sb(ctx, "att", [P, HALVES, HGRN_TILES, P])
        with ExitStack() as local:
            gap = core.sb(local, "gap", [P, 2, HGRN_TILES * SEQ])
            left = core.sb(local, "left", [P, 2, HGRN_TILES, SEQ])
            right = core.sb(local, "right", [P, 2, HGRN_TILES, SEQ])
            masked = core.sb(local, "masked", [P, 2, HALVES, HGRN_TILES, P])
            banks = core.banks(local, "level", 4)
            (sample_bank,) = core.banks(local, "reads", 1)
            with nc.Block() as block:
                @block.gpsimd
                def _(pool):
                    pool.memset(left, 0.0)
                    pool.memset(right, 0.0)
            gap0, exp0, scaled0, mult0 = core.dve_done.at, core.act_done.at, core.tile_evicted.at, core.pe_done.at
            masked0, added0 = core.tile_multiplied.at, core.pool_done.at
            with nc.Block() as block:
                @block.vector
                def _(dve):
                    def gaps(level):
                        w = 1 << level
                        if level >= 2:
                            dve.wait_ge(core.tile_evicted.sem, scaled0 + level - 1)
                        g = flat(logs).rearrange("p (n j) -> p n j", j=2 * w)
                        to = gap[:, level % 2, :].rearrange("p (n j) -> p n j", j=2 * w)
                        middle = g[:, :, w - 1:w].broadcast_to((P, HGRN_TILES * SEQ // (2 * w), w))
                        dve.tensor_tensor(to[:, :, 0:w], middle, g[:, :, 0:w], ALU.subtract)
                        core.dve_done.inc(dve.tensor_tensor(to[:, :, w:2 * w], g[:, :, w:2 * w], middle, ALU.subtract))

                    def scale(level):
                        w, slot = 1 << level, level % 2
                        dve.wait_ge(core.act_done.sem, exp0 + level + 1)
                        if level >= 2:
                            dve.wait_ge(core.pe_done.sem, mult0 + 1 + level - 1)
                        cut = lambda a: a.rearrange("p (n j) -> p n j", j=2 * w)
                        e = cut(gap[:, slot, :])
                        dve.tensor_tensor(cut(flat(left[:, slot]))[:, :, 0:w], cut(flat(key))[:, :, 0:w],
                                          e[:, :, 0:w], ALU.mult)
                        core.tile_evicted.inc(dve.tensor_tensor(
                            cut(flat(right[:, slot]))[:, :, w:2 * w], cut(flat(q))[:, :, w:2 * w],
                            e[:, :, w:2 * w], ALU.mult))

                    def cover(level, to, which):
                        slot = (level + 1) % 2
                        dve.wait_ge(core.pe_done.sem, mult0 + level + 2)
                        if level >= 2:
                            dve.wait_ge(core.pool_done.sem, added0 + level - 1)
                        for half in range(HALVES):
                            last = dve.tensor_tensor(to[:, half], banks[2 * slot + half][:, :].rearrange(
                                "p (a j) -> p a j", a=4), which.broadcast_to((P, 4, P)), ALU.mult)
                        core.tile_multiplied.inc(last)

                    gaps(0)
                    cover(-1, att, core.ident.unsqueeze(1))
                    gaps(1)
                    for level in range(LEVELS):
                        scale(level)
                        if level + 2 < LEVELS:
                            gaps(level + 2)
                        if level:
                            cover(level - 1, masked[:, (level - 1) % 2],
                                  mask[:, MASK_LEVEL + level - 1:MASK_LEVEL + level, :])
                    cover(LEVELS - 1, masked[:, (LEVELS - 1) % 2], mask[:, MASK_LEVEL + LEVELS - 1:MASK_LEVEL + LEVELS, :])

                @block.scalar
                def _(act):
                    for level in range(LEVELS):
                        act.wait_ge(core.dve_done.sem, gap0 + level + 1)
                        core.act_done.inc(act.activation(gap[:, level % 2, :], gap[:, level % 2, :], ACT.Exp))

                @block.tensor
                def _(pe):
                    for n in range(LEVELS + 1):
                        if n:
                            pe.wait_ge(core.tile_evicted.sem, scaled0 + n)
                        if n >= 2:
                            pe.wait_ge(core.tile_multiplied.sem, masked0 + n - 1)
                        for half in range(HALVES):
                            for tile in range(HGRN_TILES):
                                cols = slice(half * P, (half + 1) * P)
                                a, b = (key, q) if n == 0 else (left[:, (n - 1) % 2], right[:, (n - 1) % 2])
                                last = pe.matmul(banks[2 * (n % 2) + half][:, tile * P:(tile + 1) * P],
                                                 a[:, tile, cols], b[:, tile, cols], start=True, stop=True)
                        core.pe_done.inc(last)
                        sample_reads(pe, sample_bank, n)

                @block.gpsimd
                def _(pool):
                    for level in range(LEVELS):
                        pool.wait_ge(core.tile_multiplied.sem, masked0 + level + 2)
                        if level:
                            pool.wait_ge(core.pool_done.sem, added0 + level)
                        core.pool_done.inc(pool.tensor_tensor(att, att, masked[:, level % 2], ALU.add))
            with nc.Block() as block:
                @block.vector
                def _(dve):
                    dve.tensor_copy(out[:, 4:8, SEQ:T],
                                    sample_bank[:, 0:HGRN_TILES * DEC].rearrange("p (a b) -> p a b", b=DEC))
        decay = core.sb(ctx, "decay", [P, HGRN_TILES, SEQ])
        late = core.sb(ctx, "late", [P, HGRN_TILES, SEQ])
        toks = core.sb(ctx, "toks", [P, 2, HALVES, 512])
        state = core.sb(ctx, "state", [P, HGRN_TILES, P])
        halves = lambda a: a.rearrange("p t (h j) -> p (t h) j", h=HALVES)
        with nc.Block() as block:
            @block.vector
            def _(dve):
                g = halves(logs)
                dve.tensor_tensor(halves(late), g[:, :, P - 1:P].broadcast_to((P, 8, P)), g, ALU.subtract)
        with nc.Block() as block:
            @block.scalar
            def _(act):
                act.activation(decay, logs, ACT.Exp)
                act.activation(late, late, ACT.Exp)
        with nc.Block() as block:
            @block.vector
            def _(dve):
                dve.tensor_tensor(late, late, key, ALU.mult)
                dve.tensor_tensor(q, q, decay, ALU.mult)
        turned = core.banks(ctx, "turned", 4)
        done0 = core.pe_done.at
        with nc.Block() as block:
            @block.tensor
            def _(pe):
                for kind, src in enumerate((values, late)):
                    for half in range(HALVES):
                        for tile in range(HGRN_TILES):
                            last = pe.transpose(turned[kind * 2 + half][:, tile * P:(tile + 1) * P],
                                                src[:, tile, half * P:(half + 1) * P], core.ident)
                        core.pe_done.inc(last)

            @block.scalar
            def _(act):
                for n in range(4):
                    act.wait_ge(core.pe_done.sem, done0 + n + 1)
                    act.copy(toks[:, n // 2, n % 2, :], turned[n][:, :])
        b_out = core.banks(ctx, "outputs", 2)
        b_state = core.banks(ctx, "states", 2)
        done0, first_state = core.pe_done.at, core.dve_done.at
        with nc.Block() as block:
            @block.tensor
            def _(pe):
                for half in range(HALVES):
                    for tile in range(HGRN_TILES):
                        cols = slice(tile * P, (tile + 1) * P)
                        last = pe.matmul(b_state[half][:, cols], toks[:, 1, half, cols], toks[:, 0, half, cols],
                                         start=True, stop=True)
                    core.pe_done.inc(last)
                for half in range(HALVES):
                    if half:
                        pe.wait_ge(core.dve_done.sem, first_state + 1)
                    for tile in range(HGRN_TILES):
                        cols = slice(tile * P, (tile + 1) * P)
                        last = pe.matmul(b_out[half][:, cols], toks[:, 0, half, cols], att[:, half, tile, :],
                                         start=True, stop=half == 0)
                        if half:
                            last = pe.matmul(b_out[half][:, cols], state[:, tile, :], q[:, tile, half * P:(half + 1) * P],
                                             start=False, stop=True)
                    core.pe_done.inc(last)

            @block.vector
            def _(dve):
                dve.wait_ge(core.pe_done.sem, done0 + 1)
                core.dve_done.inc(dve.tensor_copy(state, b_state[0][:, :].rearrange("p (a j) -> p a j", a=4)))
                dve.wait_ge(core.pe_done.sem, done0 + 4)
                for tile in range(HGRN_TILES):
                    dve.scalar_tensor_tensor(state[:, tile, :], state[:, tile, :], decay[:, tile, SEQ - 1:SEQ],
                                             b_state[1][:, tile * P:(tile + 1) * P], ALU.mult, ALU.add)

            @block.scalar
            def _(act):
                for half in range(HALVES):
                    act.wait_ge(core.pe_done.sem, done0 + 3 + half)
                    act.copy(out[:, 4:8, half * P:(half + 1) * P],
                             b_out[half][:, :].rearrange("p (a j) -> p a j", a=4))
        with nc.Block() as block:
            @block.sync
            def _(sp):
                core.stored.inc(sp.dma_start(state_out, state), 16)
                sp.wait_ge(core.stored.sem, core.stored.at)


def hgrn_sample(core, values, q, key, forget, state, state_out):
    nc = core.nc
    wide = [P, HGRN_TILES, DEC, P]
    with ExitStack() as ctx:
        work = core.sb(ctx, "work", wide)
        each = lambda a: a.unsqueeze(3).broadcast_to(tuple(wide))
        with ExitStack() as ps:
            banks = core.banks(ps, "spread", 8)
            done0 = core.pe_done.at
            with nc.Block() as block:
                @block.tensor
                def _(pe):
                    for n in range(8):
                        for s in range(4 * n, 4 * n + 4):
                            last = pe.matmul(banks[n][:, (s % 4) * P:(s % 4 + 1) * P],
                                             values[:, s // DEC, s % DEC:s % DEC + 1].broadcast_to((P, P)),
                                             core.ident, start=True, stop=True)
                        core.pe_done.inc(last)

                @block.vector
                def _(dve):
                    core.wait_loads(dve)
                    link = Link(dve, core.dve_done)
                    link(dve.tensor_tensor(state, state, each(forget), ALU.mult))
                    for n in range(8):
                        dve.wait_ge(core.pe_done.sem, done0 + n + 1)
                        tile, b = n // 2, 4 * (n % 2)
                        last = dve.tensor_tensor(work[:, tile, b:b + 4, :], banks[n][:, :].rearrange(
                            "p (b v) -> p b v", b=4), each(key)[:, tile, b:b + 4, :], ALU.mult)
                    link(last)
                    dve.tensor_tensor(state, state, work, ALU.add)
    with nc.Block() as block:
        @block.sync
        def _(sp):
            core.stored.inc(sp.dma_start(state_out, state), 16)

    def reads(pe, bank, n):
        for s in range(4 * n, 4 * n + 4):
            pe.matmul(bank[:, s:s + 1], state[:, s // DEC, s % DEC, :], q[:, s // DEC, s % DEC:s % DEC + 1],
                      start=True, stop=True)
    return reads


def hgrn_activations(act, p):
    act.activation(p[:, 14:18, :], p[:, 14:18, :], ACT.Silu)
    act.activation(p[:, 26:30, :], p[:, 26:30, :], ACT.Silu)
    act.activation(p[:, 18:22, :], p[:, 18:22, :], ACT.Sigmoid)


def hgrn(core, par, mask, p, out, state_in, prompt_state, sample_state):
    nc = core.nc
    whole = [P, HGRN_TILES, T]
    prompt = [P, HGRN_TILES, SEQ]
    with ExitStack() as ctx:
        gate, forget = p[:, 26:30, :], p[:, 18:22, :]
        q = core.sb(ctx, "q", prompt)
        key = core.sb(ctx, "key", prompt)
        logs = core.sb(ctx, "logs", prompt)
        small = core.sb(ctx, "small", [P, 3, HGRN_TILES, DEC])
        sample_states = core.sb(ctx, "sample_states", [P, HGRN_TILES, DEC, P])
        with ExitStack() as local:
            logf = core.sb(local, "logf", prompt)
            bound = core.sb(local, "bound", [P, 4, HGRN_TILES])
            with nc.Block() as block:
                @block.sync
                def _(sp):
                    core.load(sp, sample_states, state_in)

                @block.scalar
                def _(act):
                    act.copy(q, p[:, 14:18, 0:SEQ])
                    act.copy(small[:, 0], p[:, 14:18, SEQ:T])

                @block.vector
                def _(dve):
                    dve.tensor_tensor(bound[:, 0], par("bound"), par("bound"), ALU.subtract)
            with nc.Block() as block:
                @block.scalar
                def _(act):
                    act.activation(bound[:, 1], bound[:, 0], ACT.Exp)
            with nc.Block() as block:
                @block.vector
                def _(dve):
                    link = Link(dve, core.dve_done)
                    link(dve.reciprocal(bound[:, 0], bound[:, 1]))
                    link(dve.tensor_tensor(bound[:, 0], bound[:, 0], bound[:, 1], ALU.mult))
                    link(dve.tensor_tensor(bound[:, 2], bound[:, 0], bound[:, 0], ALU.subtract))
                    link(dve.tensor_scalar(bound[:, 3], bound[:, 2], -1.0, 1.0, ALU.mult, ALU.add))
                    for i in range(HGRN_TILES):
                        last = dve.tensor_scalar(forget[:, i, :], forget[:, i, :], bound[:, 3, i:i + 1],
                                                 bound[:, 2, i:i + 1], ALU.mult, ALU.add)
                    link(last)
                    dve.tensor_scalar(key, forget[:, :, 0:SEQ], -1.0, 1.0, ALU.mult, ALU.add)
                    dve.tensor_scalar(small[:, 1], forget[:, :, SEQ:T], -1.0, 1.0, ALU.mult, ALU.add)
                    dve.tensor_copy(small[:, 2], forget[:, :, SEQ:T])
                    dve.tensor_scalar(logf, forget[:, :, 0:SEQ], SMALLEST_LOG, None, ALU.max)
            with nc.Block() as block:
                @block.scalar
                def _(act):
                    act.activation(logf, logf, ACT.Ln)
            with nc.Block() as block:
                @block.vector
                def _(dve):
                    for i in range(HGRN_TILES):
                        dve.tensor_tensor_scan(logs[:, i, :], mask[:, MASK_SCAN128:MASK_SCAN128 + 2, :].rearrange(
                            "p a b -> p (a b)"), logf[:, i, :], 0.0, ALU.mult, ALU.add)
        reads = hgrn_sample(core, p[:, 22:26, SEQ:T], small[:, 0], small[:, 1], small[:, 2], sample_states, sample_state)
        hgrn_prompt(core, mask, p[:, 22:26, 0:SEQ], q, key, logs, out, prompt_state, reads)
        o = out[:, 4:8, :]

        def finish(dve, link, root):
            for i in range(HGRN_TILES):
                last = dve.scalar_tensor_tensor(o[:, i, :], o[:, i, :], par("hgrn_norm", 0), root[:, i, :],
                                                ALU.mult, ALU.mult)
            link(last)
            dve.tensor_tensor(o, o, gate, ALU.mult)
        head_norm(core, core.ones, o, 1.0 / P, RMS_EPS, finish)


def mixer_ab(core, x, d, norm, w_in, then=None):
    nc = core.nc
    w_out = Stream(d["ab_w_out"])
    with ExitStack() as ctx:
        mask = core.sb(ctx, "mask", [P, MASKS, P])
        params = core.sb(ctx, "params", [P, AB_PARAMS])

        def par(name, i=None):
            at = AB_PARAM[name]
            return params[:, at] if i is None else params[:, at.start + i:at.start + i + 1]

        p = core.sb(ctx, "p", [P, AB_TILES, T])
        out = core.sb(ctx, "mixer_out", [P, KC, T])
        lora = core.sb(ctx, "lora", [P, 512])
        gup = core.sb(ctx, "gup", [P, 512])
        last_rows = core.sb(ctx, "last_rows", [P, SHIFT_TILES, DEC + 1])
        core.block_ones = mask[:, MASK_BLOCKS, :]
        with ExitStack() as local:
            shift = core.sb(local, "shift", [P, SHIFT_TILES, DEC])
            diff = core.sb(local, "diff", [P, 1, T])
            with nc.Block() as block:
                @block.sync
                def _(sp):
                    core.load(sp, params, d["ab_params"])
                    core.load(sp, shift, d["shift_in"])
                    core.load(sp, lora, d["lora_up"])
                    core.load(sp, gup, d["gate_up"])
                    core.load(sp, mask, d["masks"])
            h = core.sb(local, "mix_in", [P, KC, T])
            h_hi = core.sb(local, "mix_in_hi", [P, KC, T], F32R)
            h_lo = core.sb(local, "mix_in_lo", [P, KC, T], F32R)
            rms_norm(core, x, norm, h, h_hi, h_lo)
            project(core, Weights(core, local), w_in, AB_TILES, h_hi, h_lo, p, then=w_out,
                    beside=shift_beside(core, params, p, shift, last_rows, diff))
        with nc.Block() as block:
            @block.sync
            def _(sp):
                core.wait_loads(sp)
                core.stored.inc(sp.dma_start(d["last_shift"], last_rows), 16)
                sp.wait_ge(core.stored.sem, core.stored.at)
        with ExitStack() as local:
            w = {}
            rwkv_inputs(core, local, p, par, mask, lora, gup, w)
            rwkv_sample(core, mask, w, out, d["rwkv_in"], d["rwkv_sample"])
            rwkv_prompt(core, mask, w, out, d["rwkv_prompt"], lambda act: hgrn_activations(act, p))
            rwkv_output(core, par, w, out)
        hgrn(core, par, mask, p, out, d["hgrn_in"], d["hgrn_prompt"], d["hgrn_sample"])
        with ExitStack() as local:
            out_hi = core.sb(local, "out_hi", [P, KC, T], F32R)
            out_lo = core.sb(local, "out_lo", [P, KC, T], F32R)
            split(core, out, out_hi, out_lo)
            project(core, Weights(core, local), w_out, KC, out_hi, out_lo, x, residual=True, then=then)


HEADS = 32
GROUPS = 4
INNER_TILES = 16
CONV_TILES = 24
SSM_TILES = INNER_TILES + CONV_TILES
INNER = INNER_TILES * P
TAPS = 4
SSM_PARAM = {}
_at = 0
for _name, _n in (("norm", 8), ("conv_w", TAPS * CONV_TILES), ("conv_b", CONV_TILES), ("out_norm", INNER_TILES),
                  ("skip", INNER_TILES)):
    SSM_PARAM[_name] = slice(_at, _at + _n)
    _at += _n
SSM_PARAMS = _at
SSM_OUT = {"conv_prompt": (P, CONV_TILES, TAPS - 1), "conv_sample": (P, CONV_TILES, TAPS - 1, DEC),
           "ssm_prompt": (P, INNER), "ssm_sample": (P, DEC, INNER)}


def ssm_steps(core, h, weights, heads, mask, dt, log_a, log_sum):
    nc = core.nc
    row = [HEADS, T]
    with ExitStack() as ctx:
        rate = core.sb(ctx, "rate", [HEADS, 1])
        z = core.sb(ctx, "z", row)
        u = core.sb(ctx, "u", row)
        r = core.sb(ctx, "r", row)
        square = core.sb(ctx, "square", row)
        series = core.sb(ctx, "series", row)
        (bank,) = core.banks(ctx, "dt", 1)
        with nc.Block() as block:
            @block.tensor
            def _(pe):
                core.wait_loads(pe)
                for k in range(KC):
                    pe.matmul(bank[0:HEADS, 0:T], weights[:, k, :], h[:, k, :], start=k == 0, stop=k == KC - 1)
        with nc.Block() as block:
            @block.vector
            def _(dve):
                link = Link(dve, core.dve_done)
                link(dve.tensor_scalar(z, bank[0:HEADS, 0:T], heads[:, 0:1], None, ALU.add))
                link(dve.tensor_scalar(r, z, -1.0, None, ALU.mult))
                dve.tensor_tensor(u, z, r, ALU.max)

            @block.scalar
            def _(act):
                act.activation(rate, heads[:, 1:2], ACT.Exp)
        with nc.Block() as block:
            @block.scalar
            def _(act):
                act.activation(u, u, ACT.Exp, scale=-1.0)
        with nc.Block() as block:
            @block.vector
            def _(dve):
                link = Link(dve, core.dve_done)
                link(dve.tensor_scalar(r, u, 2.0, None, ALU.add))
                link(dve.reciprocal(r, r))
                link(dve.tensor_tensor(r, r, u, ALU.mult))
                link(dve.tensor_tensor(square, r, r, ALU.mult))
                link(dve.tensor_scalar(series, square, 1.0 / 17, None, ALU.mult))
                for n in range(15, 1, -2):
                    link(dve.scalar_tensor_tensor(series, series, 1.0 / n, square, ALU.add, ALU.mult))
                link(dve.scalar_tensor_tensor(series, series, 1.0, r, ALU.add, ALU.mult))
                link(dve.tensor_scalar(z, z, 0.0, None, ALU.max))
                link(dve.scalar_tensor_tensor(dt, series, 2.0, z, ALU.mult, ALU.add))
                link(dve.tensor_scalar(log_a, dt, rate, -1.0, ALU.mult, ALU.mult))
                dve.tensor_tensor_scan(log_sum, mask[0:HEADS, MASK_SCAN128:MASK_SCAN128 + 2, :].rearrange(
                    "p a b -> p (a b)"), log_a[:, 0:SEQ], 0.0, ALU.mult, ALU.add)


def conv_beside(core, params, p, c):
    def program(dve, out0):
        done0 = core.mixed.at
        core.wait_loads(dve)

        def one(i, u):
            at = lambda name, first=0: params[:, bass.ds(i * UNROLL + (SSM_PARAM[name].start + first + u), 1)]
            tap = lambda j: at("conv_w", j * CONV_TILES)
            x = p[:, bass.ds(i * UNROLL + (INNER_TILES + u), 1), :]
            to = c[:, bass.ds(i * UNROLL + u, 1), :]
            dve.wait_ge(core.tile_evicted.sem, i * UNROLL + (u + INNER_TILES + 1 + out0))
            dve.tensor_scalar(to, x, tap(TAPS - 1), at("conv_b"), ALU.mult, ALU.add).then_inc(core.mixed.sem, 1)
            for back in range(1, TAPS):
                dve.wait_ge(core.mixed.sem, i * (TAPS * UNROLL) + (TAPS * u + back + done0))
                dve.scalar_tensor_tensor(to[:, :, back:SEQ], x[:, :, 0:SEQ - back], tap(TAPS - 1 - back),
                                         to[:, :, back:SEQ], ALU.mult, ALU.add).then_inc(core.mixed.sem, 1)
        tile_loop(dve, CONV_TILES, one)
        core.mixed.at += TAPS * CONV_TILES
    return program


def ssm_conv(core, par, p, c, rows, conv_prompt, conv_sample):
    nc = core.nc
    with ExitStack() as ctx:
        term = core.sb(ctx, "term", [P, TAPS - 1, CONV_TILES, DEC])
        x = p[:, INNER_TILES:SSM_TILES, :]
        with nc.Block() as block:
            @block.sync
            def _(sp):
                core.stored.inc(sp.dma_start(conv_prompt, x[:, :, SEQ - 3:SEQ]), 16)
                core.stored.inc(sp.dma_start(conv_sample[:, :, 2, :], x[:, :, SEQ:T]), 16)
                core.stored.inc(sp.dma_start(conv_sample[:, :, 0:2, :], rows[:, :, 1:3, :]), 16)
        with nc.Block() as block:
            @block.gpsimd
            def _(pool):
                link = Link(pool, core.pool_done)
                for j in range(TAPS - 1):
                    w = par("conv_w")[:, j * CONV_TILES:(j + 1) * CONV_TILES].unsqueeze(2)
                    link(pool.tensor_tensor(term[:, j], rows[:, :, j, :], w.broadcast_to((P, CONV_TILES, DEC)),
                                            ALU.mult))
                for j in range(TAPS - 1):
                    link(pool.tensor_tensor(c[:, :, SEQ:T], c[:, :, SEQ:T], term[:, j], ALU.add))


def ssm_sample(core, c, xdt, log_a, y, state_in, state_out):
    nc = core.nc
    slots = STATE_SLOTS
    with ExitStack() as ctx:
        ring = core.sb(ctx, "states", [P, slots, INNER])
        a = core.sb(ctx, "a", [HEADS, DEC])
        diagonal = core.sb(ctx, "diagonal", [HEADS, DEC, HEADS])
        a_all = core.sb(ctx, "a_all", [P, DEC, HEADS])
        spread = core.banks(ctx, "spread", 4)
        reads, decays = core.banks(ctx, "reads", 2)
        loaded0 = [k.at for k in core.state_loaded]
        stored0 = [k.at for k in core.state_stored]
        ahead = 2

        def load(sp, b):
            core.state_loaded[b % slots].inc(sp.dma_start(ring[:, b % slots, :], state_in[:, b, :]), 16)

        with nc.Block() as block:
            @block.sync
            def _(sp):
                for b in range(ahead):
                    load(sp, b)

            @block.scalar
            def _(act):
                act.activation(a, log_a[:, SEQ:T], ACT.Exp)
        with nc.Block() as block:
            @block.vector
            def _(dve):
                dve.tensor_tensor(diagonal, a.unsqueeze(2).broadcast_to((HEADS, DEC, HEADS)),
                                  core.ident[0:HEADS, 0:HEADS].unsqueeze(1).broadcast_to((HEADS, DEC, HEADS)), ALU.mult)
        with nc.Block() as block:
            @block.tensor
            def _(pe):
                pe.matmul(decays[:, 0:DEC * HEADS], core.ones[0:HEADS, :], diagonal.rearrange("p b h -> p (b h)"),
                          start=True, stop=True)
        with nc.Block() as block:
            @block.scalar
            def _(act):
                act.copy(a_all, decays[:, 0:DEC * HEADS].rearrange("p (b h) -> p b h", b=DEC))
        decayed0, spread0, updated0, read0 = (core.pool_done.at, core.pe_done.at, core.dve_done.at,
                                              core.tile_multiplied.at)
        with nc.Block() as block:
            @block.sync
            def _(sp):
                for b in range(DEC):
                    n = b + ahead
                    if n < DEC:
                        if n >= slots:
                            sp.wait_ge(core.state_stored[n % slots].sem, stored0[n % slots] + 16 * (n // slots))
                            sp.wait_ge(core.tile_multiplied.sem, read0 + n - slots + 1)
                        load(sp, n)
                    sp.wait_ge(core.dve_done.sem, updated0 + GROUPS * (b + 1))
                    core.state_stored[b % slots].inc(sp.dma_start(state_out[:, b, :], ring[:, b % slots, :]), 16)
                for k in range(slots):
                    sp.wait_ge(core.state_stored[k].sem, core.state_stored[k].at)

            @block.gpsimd
            def _(pool):
                for b in range(DEC):
                    pool.wait_ge(core.state_loaded[b % slots].sem, loaded0[b % slots] + 16 * (b // slots + 1))
                    s = ring[:, b % slots, :].rearrange("p (h v) -> p h v", h=HEADS)
                    core.pool_done.inc(pool.tensor_tensor(
                        s, s, a_all[:, b, :].unsqueeze(2).broadcast_to((P, HEADS, 64)), ALU.mult))

            @block.tensor
            def _(pe):
                def rows(b):
                    for g in range(GROUPS):
                        if b:
                            pe.wait_ge(core.dve_done.sem, updated0 + GROUPS * (b - 1) + g + 1)
                        for tile in range(4 * g, 4 * g + 4):
                            last = pe.matmul(spread[g][:, (tile % 4) * P:(tile % 4 + 1) * P],
                                             xdt[:, tile, SEQ + b:SEQ + b + 1].broadcast_to((P, P)), core.ident,
                                             start=True, stop=True)
                        core.pe_done.inc(last)

                def outputs(b):
                    pe.wait_ge(core.dve_done.sem, updated0 + GROUPS * (b + 1))
                    for tile in range(INNER_TILES):
                        last = pe.matmul(reads[:, tile * DEC + b:tile * DEC + b + 1],
                                         ring[:, b % slots, tile * P:(tile + 1) * P],
                                         c[:, 20 + tile // 4, SEQ + b:SEQ + b + 1], start=True, stop=True)
                    core.tile_multiplied.inc(last)

                rows(0)
                for b in range(DEC):
                    if b + 1 < DEC:
                        rows(b + 1)
                    outputs(b)

            @block.vector
            def _(dve):
                for b in range(DEC):
                    dve.wait_ge(core.pool_done.sem, decayed0 + b + 1)
                    for g in range(GROUPS):
                        dve.wait_ge(core.pe_done.sem, spread0 + GROUPS * b + g + 1)
                        s = ring[:, b % slots, g * 512:(g + 1) * 512]
                        core.dve_done.inc(dve.scalar_tensor_tensor(
                            s, spread[g][:, :], c[:, 16 + g, SEQ + b:SEQ + b + 1], s, ALU.mult, ALU.add))
        with nc.Block() as block:
            @block.vector
            def _(dve):
                dve.tensor_copy(y[:, :, SEQ:T], reads[:, 0:INNER_TILES * DEC].rearrange("p (a b) -> p a b", b=DEC))


def ssm_prompt(core, mask, expand, c, xdt, log_sum, y, state_out):
    nc = core.nc
    with ExitStack() as ctx:
        x_tok = core.sb(ctx, "x_tok", [P, HALVES, INNER])
        x_late = core.sb(ctx, "x_late", [P, HALVES, INNER])
        b_tok = core.sb(ctx, "b_tok", [P, HALVES, 512])
        sum_tok = core.sb(ctx, "sum_tok", [P, HALVES, HEADS])
        late = core.sb(ctx, "late", [P, HALVES, HEADS])
        end = core.sb(ctx, "end", [P, HALVES, HEADS])
        diagonal = core.sb(ctx, "diagonal", [HEADS, HALVES, HEADS])
        inside = core.sb(ctx, "inside", [P, HALVES, GROUPS, P])
        grown = core.sb(ctx, "grown", [P, INNER_TILES, P])
        state = core.sb(ctx, "state", [P, INNER])
        halves = [slice(0, P), slice(P, 2 * P)]
        with ExitStack() as ps:
            banks = core.banks(ps, "turned", 4)
            sums, ends = core.banks(ps, "sums", 2)
            cb = core.banks(ps, "cb", 2)
            done0, out0 = core.pe_done.at, core.act_done.at
            jobs = [(x_tok, half, q, xdt, 4 * q) for half in range(HALVES) for q in range(4)]
            jobs += [(b_tok, half, 0, c, 16) for half in range(HALVES)]
            with nc.Block() as block:
                @block.tensor
                def _(pe):
                    for n, (dst, half, q, src, first) in enumerate(jobs):
                        if n >= 4:
                            pe.wait_ge(core.act_done.sem, out0 + n - 3)
                        for i in range(4):
                            last = pe.transpose(banks[n % 4][:, i * P:(i + 1) * P], src[:, first + i, halves[half]],
                                                core.ident)
                        core.pe_done.inc(last)
                    for half in range(HALVES):
                        pe.transpose(sums[:, half * HEADS:(half + 1) * HEADS], log_sum[:, halves[half]],
                                     core.ident[0:HEADS, 0:HEADS])
                        for g in range(GROUPS):
                            pe.matmul(cb[half][:, g * P:(g + 1) * P], c[:, 16 + g, halves[half]],
                                      c[:, 20 + g, halves[half]], start=True, stop=True)

                @block.scalar
                def _(act):
                    for n, (dst, half, q, src, first) in enumerate(jobs):
                        act.wait_ge(core.pe_done.sem, done0 + n + 1)
                        core.act_done.inc(act.copy(dst[:, half, q * 512:(q + 1) * 512], banks[n % 4][:, :]))

                @block.vector
                def _(dve):
                    for half in range(HALVES):
                        at = half * P + P - 1
                        dve.tensor_scalar(diagonal[:, half, :], core.ident[0:HEADS, 0:HEADS],
                                          log_sum[:, at:at + 1], None, ALU.mult)
            with nc.Block() as block:
                @block.tensor
                def _(pe):
                    pe.matmul(ends[:, 0:HALVES * HEADS], core.ones[0:HEADS, :],
                              diagonal.rearrange("p a h -> p (a h)"), start=True, stop=True)

                @block.vector
                def _(dve):
                    dve.tensor_copy(sum_tok, sums[:, 0:HALVES * HEADS].rearrange("p (a h) -> p a h", a=HALVES))
                    for half in range(HALVES):
                        dve.tensor_tensor(inside[:, half], cb[half][:, :].rearrange("p (g j) -> p g j", g=GROUPS),
                                          mask[:, MASK_CAUSAL:MASK_CAUSAL + 1, :].broadcast_to((P, GROUPS, P)),
                                          ALU.mult)
            with nc.Block() as block:
                @block.vector
                def _(dve):
                    dve.tensor_tensor(late, ends[:, 0:HALVES * HEADS].rearrange("p (a h) -> p a h", a=HALVES),
                                      sum_tok, ALU.subtract)
            with nc.Block() as block:
                @block.scalar
                def _(act):
                    act.activation(end, ends[:, 0:HALVES * HEADS].rearrange("p (a h) -> p a h", a=HALVES), ACT.Exp)
                    act.activation(late, late, ACT.Exp)
            with nc.Block() as block:
                @block.vector
                def _(dve):
                    for half in range(HALVES):
                        dve.tensor_tensor(x_late[:, half].rearrange("p (h v) -> p h v", h=HEADS),
                                          x_tok[:, half].rearrange("p (h v) -> p h v", h=HEADS),
                                          late[:, half].unsqueeze(2).broadcast_to((P, HEADS, 64)), ALU.mult)
        with ExitStack() as ps:
            adds = core.banks(ps, "adds", 4)
            grows = core.banks(ps, "grows", 4)
            with nc.Block() as block:
                @block.tensor
                def _(pe):
                    for g in range(GROUPS):
                        pe.matmul(adds[g][:, :], b_tok[:, 0, g * P:(g + 1) * P], x_late[:, 0, g * 512:(g + 1) * 512],
                                  start=True, stop=True)
                    for tile in range(INNER_TILES):
                        pick = expand[:, tile * P:(tile + 1) * P]
                        pe.matmul(grows[tile // 4][:, (tile % 4) * P:(tile % 4 + 1) * P], pick,
                                  log_sum[:, halves[1]], start=True, stop=True)
            with nc.Block() as block:
                @block.vector
                def _(dve):
                    for g in range(GROUPS):
                        dve.tensor_copy(state[:, g * 512:(g + 1) * 512], adds[g][:, :])

                @block.scalar
                def _(act):
                    for g in range(GROUPS):
                        act.activation(grown[:, 4 * g:4 * g + 4, :],
                                       grows[g][:, :].rearrange("p (a j) -> p a j", a=4), ACT.Exp)
        with ExitStack() as ps:
            decay = core.sb(ps, "decay", [P, 2, 8, P])
            carried = core.sb(ps, "carried", [P, 512])
            sum_banks = core.banks(ps, "sum", 4)
            y_banks = core.banks(ps, "y", 2)
            (carry_bank,) = core.banks(ps, "carry", 1)
            work = [(half, g) for half in range(HALVES) for g in range(GROUPS)]
            row0, y0, gap0, exp0, weight0, out0 = (core.pe_done.at, core.tile_multiplied.at, core.dve_done.at,
                                                   core.act_done.at, core.pool_done.at, core.tile_evicted.at)
            with nc.Block() as block:
                @block.tensor
                def _(pe):
                    def rows(n):
                        half, g = work[n]
                        if n >= 2:
                            pe.wait_ge(core.dve_done.sem, gap0 + n - 1)
                        for h in range(8):
                            last = pe.matmul(sum_banks[2 * (n % 2) + h // 4][:, (h % 4) * P:(h % 4 + 1) * P],
                                             core.ident[0:HEADS, 8 * g + h:8 * g + h + 1].broadcast_to((HEADS, P)),
                                             log_sum[:, halves[half]], start=True, stop=True)
                        core.pe_done.inc(last)

                    rows(0)
                    for n, (half, g) in enumerate(work):
                        if n + 1 < len(work):
                            rows(n + 1)
                        if n >= 2:
                            pe.wait_ge(core.tile_evicted.sem, out0 + n - 1)
                        if half:
                            if g:
                                pe.wait_ge(core.tile_evicted.sem, out0 + n)
                            for tile in range(4 * g, 4 * g + 4):
                                pe.matmul(carry_bank[:, (tile % 4) * P:(tile % 4 + 1) * P],
                                          state[:, tile * P:(tile + 1) * P], c[:, 20 + g, halves[1]],
                                          start=True, stop=True)
                        pe.wait_ge(core.pool_done.sem, weight0 + n + 1)
                        for h in range(8):
                            last = pe.matmul(
                                y_banks[n % 2][64 * (h % 2):64 * (h % 2) + 64, (h // 2) * P:(h // 2 + 1) * P],
                                x_tok[:, half, (8 * g + h) * 64:(8 * g + h + 1) * 64], decay[:, n % 2, h, :],
                                start=True, stop=True)
                        core.tile_multiplied.inc(last)

                @block.vector
                def _(dve):
                    def gaps(n):
                        half, g = work[n]
                        dve.wait_ge(core.pe_done.sem, row0 + n + 1)
                        if n >= 2:
                            dve.wait_ge(core.tile_multiplied.sem, y0 + n - 1)
                        for h in range(8):
                            last = dve.tensor_scalar(
                                decay[:, n % 2, h, :],
                                sum_banks[2 * (n % 2) + h // 4][:, (h % 4) * P:(h % 4 + 1) * P],
                                sum_tok[:, half, 8 * g + h:8 * g + h + 1], 0.0, ALU.subtract, ALU.min)
                        core.dve_done.inc(last)

                    def finish(n):
                        half, g = work[n]
                        dve.wait_ge(core.tile_multiplied.sem, y0 + n + 1)
                        to = y[:, 4 * g:4 * g + 4, halves[half]]
                        four = lambda a: a.rearrange("p (a j) -> p a j", a=4)
                        if half:
                            link = Link(dve, core.carry_done)
                            link(dve.tensor_tensor(four(carried), four(carry_bank[:, :]), grown[:, 4 * g:4 * g + 4, :],
                                                   ALU.mult))
                            core.tile_evicted.inc(dve.tensor_tensor(to, four(y_banks[n % 2][:, :]), four(carried),
                                                                    ALU.add))
                        else:
                            core.tile_evicted.inc(dve.tensor_copy(to, four(y_banks[n % 2][:, :])))

                    gaps(0)
                    for n in range(len(work)):
                        if n + 1 < len(work):
                            gaps(n + 1)
                        finish(n)

                @block.scalar
                def _(act):
                    for n in range(len(work)):
                        act.wait_ge(core.dve_done.sem, gap0 + n + 1)
                        core.act_done.inc(act.activation(decay[:, n % 2], decay[:, n % 2], ACT.Exp))

                @block.gpsimd
                def _(pool):
                    for n, (half, g) in enumerate(work):
                        pool.wait_ge(core.act_done.sem, exp0 + n + 1)
                        core.pool_done.inc(pool.tensor_tensor(
                            decay[:, n % 2], decay[:, n % 2],
                            inside[:, half, g:g + 1, :].broadcast_to((P, 8, P)), ALU.mult))
        with ExitStack() as ps:
            adds = core.banks(ps, "adds", 4)
            with nc.Block() as block:
                @block.tensor
                def _(pe):
                    for g in range(GROUPS):
                        pe.matmul(adds[g][:, :], b_tok[:, 1, g * P:(g + 1) * P], x_late[:, 1, g * 512:(g + 1) * 512],
                                  start=True, stop=True)

                @block.vector
                def _(dve):
                    s = state.rearrange("p (h v) -> p h v", h=HEADS)
                    dve.tensor_tensor(s, s, end[:, 1].unsqueeze(2).broadcast_to((P, HEADS, 64)), ALU.mult)
            with nc.Block() as block:
                @block.vector
                def _(dve):
                    for g in range(GROUPS):
                        at = slice(g * 512, (g + 1) * 512)
                        dve.tensor_tensor(state[:, at], adds[g][:, :], state[:, at], ALU.add)
            with nc.Block() as block:
                @block.sync
                def _(sp):
                    core.stored.inc(sp.dma_start(state_out, state), 16)
                    sp.wait_ge(core.stored.sem, core.stored.at)


def ssm_output(core, par, z, c, y, hi, lo):
    nc = core.nc
    per = INNER_TILES // GROUPS
    with ExitStack() as ctx:
        squares = core.sb(ctx, "squares", [P, INNER_TILES, T])
        root = core.sb(ctx, "root", [P, GROUPS, T])
        banks = core.banks(ctx, "norm", GROUPS)
        tiles = lambda g: slice(g * per, (g + 1) * per)
        act0, pe0, mean0, scaled0, hi0 = (core.act_done.at, core.pe_done.at, core.gated_lo.at,
                                         core.gated_hi.at, core.hi_made.at)
        with nc.Block() as block:
            @block.scalar
            def _(act):
                for g in range(GROUPS):
                    core.act_done.inc(act.activation(z[:, tiles(g), :], z[:, tiles(g), :], ACT.Silu))
                for g in range(GROUPS):
                    act.wait_ge(core.gated_hi.sem, scaled0 + g + 1)
                    core.act_done.inc(act.activation(squares[:, tiles(g), :], y[:, tiles(g), :], ACT.Square))
                for g in range(GROUPS):
                    act.wait_ge(core.gated_lo.sem, mean0 + g + 1)
                    core.act_done.inc(act.activation(root[:, g, :], root[:, g, :], ACT.Sqrt))
                for g in range(GROUPS):
                    act.wait_ge(core.gated_hi.sem, scaled0 + GROUPS + g + 1)
                    core.hi_made.inc(act.copy(hi[:, tiles(g), :], y[:, tiles(g), :]))

            @block.tensor
            def _(pe):
                for g in range(GROUPS):
                    pe.wait_ge(core.act_done.sem, act0 + GROUPS + g + 1)
                    for i in range(per):
                        last = pe.matmul(banks[g][:, 0:T], core.ones, squares[:, g * per + i, :], start=i == 0,
                                         stop=i == per - 1)
                    core.pe_done.inc(last)

            @block.vector
            def _(dve):
                link = Link(dve, core.dve_done)
                for g in range(GROUPS):
                    for i in range(g * per, (g + 1) * per):
                        last = dve.scalar_tensor_tensor(y[:, i, :], c[:, i, :], par("skip", i), y[:, i, :],
                                                        ALU.mult, ALU.add)
                    link(last)
                    dve.wait_ge(core.act_done.sem, act0 + g + 1)
                    core.gated_hi.inc(dve.tensor_tensor(y[:, tiles(g), :], y[:, tiles(g), :], z[:, tiles(g), :],
                                                        ALU.mult))
                for g in range(GROUPS):
                    dve.wait_ge(core.pe_done.sem, pe0 + g + 1)
                    core.gated_lo.inc(dve.tensor_scalar(root[:, g, :], banks[g][:, 0:T], 1.0 / 512, RMS_EPS,
                                                        ALU.mult, ALU.add))
                for g in range(GROUPS):
                    dve.wait_ge(core.act_done.sem, act0 + 2 * GROUPS + g + 1)
                    link(dve.reciprocal(root[:, g, :], root[:, g, :]))
                    for i in range(g * per, (g + 1) * per):
                        last = dve.scalar_tensor_tensor(y[:, i, :], y[:, i, :], par("out_norm", i), root[:, g, :],
                                                        ALU.mult, ALU.mult)
                    core.gated_hi.inc(last)

            @block.gpsimd
            def _(pool):
                for g in range(GROUPS):
                    pool.wait_ge(core.hi_made.sem, hi0 + g + 1)
                    pool.tensor_tensor(lo[:, tiles(g), :], y[:, tiles(g), :], hi[:, tiles(g), :].bitcast(F32),
                                       ALU.subtract)


def mixer_ssm(core, x, d, norm, w_in, then=None):
    nc = core.nc
    w_out = Stream(d["ssm_w_out"])
    core.carry_done = Count(nc, "carry_done")
    with ExitStack() as ctx:
        mask = core.sb(ctx, "mask", [P, MASKS, P])
        params = core.sb(ctx, "params", [P, SSM_PARAMS])

        def par(name, i=None):
            at = SSM_PARAM[name]
            return params[:, at] if i is None else params[:, at.start + i:at.start + i + 1]

        p = core.sb(ctx, "p", [P, SSM_TILES, T])
        y = p[:, INNER_TILES:2 * INNER_TILES, :]
        with ExitStack() as local:
            c = core.sb(local, "c", [P, CONV_TILES, T])
            rows = core.sb(local, "conv_rows", [P, CONV_TILES, TAPS - 1, DEC])
            w_dt = core.sb(local, "w_dt", [P, KC, HEADS])
            heads = core.sb(local, "heads", [HEADS, 2])
            dt = core.sb(local, "dt", [HEADS, T])
            log_a = core.sb(local, "log_a", [HEADS, T])
            log_sum = core.sb(local, "log_sum", [HEADS, SEQ])
            expand = core.sb(local, "expand", [HEADS, INNER])
            with nc.Block() as block:
                @block.vector
                def _(dve):
                    dve.tensor_copy(expand.rearrange("p (h v) -> p h v", h=HEADS),
                                    core.ident[0:HEADS, 0:HEADS].unsqueeze(2).broadcast_to((HEADS, HEADS, 64)))
            with nc.Block() as block:
                @block.sync
                def _(sp):
                    core.load(sp, params, d["ssm_params"])
                    core.load(sp, rows, d["conv_in"])
                    core.load(sp, w_dt, d["ssm_w_dt"])
                    core.load(sp, heads, d["ssm_heads"])
                    core.load(sp, mask, d["masks"])
            with ExitStack() as inner:
                h = core.sb(inner, "mix_in", [P, KC, T])
                h_hi = core.sb(inner, "mix_in_hi", [P, KC, T], F32R)
                h_lo = core.sb(inner, "mix_in_lo", [P, KC, T], F32R)
                rms_norm(core, x, norm, h, h_hi, h_lo)
                with ExitStack() as stream:
                    project(core, Weights(core, stream), w_in, SSM_TILES, h_hi, h_lo, p, then=w_out,
                            beside=conv_beside(core, params, p, c))
                ssm_steps(core, h, w_dt, heads, mask, dt, log_a, log_sum)
            xdt = core.sb(local, "xdt", [P, INNER_TILES, T])
            ssm_conv(core, par, p, c, rows, d["conv_prompt"], d["conv_sample"])
            with ExitStack() as ps:
                banks = core.banks(ps, "dt", 8)
                done0, used0, silu0 = core.pe_done.at, core.dve_done.at, core.act_done.at
                with nc.Block() as block:
                    @block.sync
                    def _(sp):
                        sp.wait_ge(core.stored.sem, core.stored.at)

                    @block.tensor
                    def _(pe):
                        for tile in range(INNER_TILES):
                            if tile >= 8:
                                pe.wait_ge(core.dve_done.sem, used0 + tile - 7)
                            pick = expand[:, tile * P:(tile + 1) * P]
                            core.pe_done.inc(pe.matmul(banks[tile % 8][:, 0:T], pick, dt, start=True, stop=True))

                    @block.scalar
                    def _(act):
                        for four in range(0, CONV_TILES, 4):
                            core.act_done.inc(act.activation(c[:, four:four + 4, :], c[:, four:four + 4, :], ACT.Silu))

                    @block.vector
                    def _(dve):
                        for tile in range(INNER_TILES):
                            dve.wait_ge(core.act_done.sem, silu0 + tile // 4 + 1)
                            dve.wait_ge(core.pe_done.sem, done0 + tile + 1)
                            core.dve_done.inc(dve.tensor_tensor(xdt[:, tile, :], banks[tile % 8][:, 0:T],
                                                                c[:, tile, :], ALU.mult))
            ssm_sample(core, c, xdt, log_a, y, d["ssm_in"], d["ssm_sample"])
            ssm_prompt(core, mask, expand, c, xdt, log_sum, y, d["ssm_prompt"])
            with ExitStack() as tail:
                y_hi = core.sb(tail, "y_hi", [P, INNER_TILES, T], F32R)
                y_lo = core.sb(tail, "y_lo", [P, INNER_TILES, T], F32R)
                ssm_output(core, par, p[:, 0:INNER_TILES, :], c, y, y_hi, y_lo)
                project(core, Weights(core, tail), w_out, KC, y_hi, y_lo, x, parts=2, residual=True, then=then)


def lay_out(inputs):
    import numpy as np
    c = np.ascontiguousarray

    def tiles(w, kc):
        return c(np.transpose(np.reshape(w, (kc, P, -1, P)), (2, 1, 0, 3)).reshape(-1, P, kc * P))

    def columns(*vectors):
        return c(np.concatenate([np.reshape(v, (-1, P)).T for v in vectors], axis=1))

    i = inputs
    tokens = np.concatenate([i["x_prompt"][0], i["x_sample"][:, 0]], axis=0)
    d = {"x": c(np.transpose(np.reshape(tokens, (T, KC, P)), (2, 1, 0))), "masks": masks()}
    if "ab_w_in" in i:
        d["ab_params"] = columns(i["norm_mix"][0], i["rwkv_mu"][0], i["rwkv_w0"][0], i["rwkv_a0"][0], i["rwkv_k_k"][0],
                                 i["rwkv_k_a"][0], i["rwkv_r_k"][0], i["rwkv_gn_w"][0], i["rwkv_gn_b"][0],
                                 i["hgrn_lower_bounds"][0], i["hgrn_norm_w"][0])
        d["ab_w_in"] = tiles(i["ab_w_in"][0], KC)
        d["ab_w_out"] = tiles(i["ab_w_out"][0], KC)
        d["lora_up"] = c(np.concatenate([i["rwkv_w_up"][0], i["rwkv_a_up"][0]], axis=0))
        d["gate_up"] = c(i["rwkv_g_up"][0])
        d["shift_in"] = c(np.transpose(np.reshape(i["state_rwkv_shift"][0], (DEC, SHIFT_TILES, P)), (2, 1, 0)))
        d["rwkv_in"] = c(np.transpose(np.reshape(i["state_rwkv"][0], (DEC, 4, 2, 64, 64)), (2, 4, 1, 0, 3)
                                      ).reshape(P, 4, DEC, 64))
        d["hgrn_in"] = c(np.transpose(i["state_hgrn"][0], (2, 1, 0, 3)))
    if "ssm_w_in" in i:
        w = i["ssm_w_in"][0]
        d["ssm_params"] = columns(i["norm_mix"][1], i["ssm_conv_w"][0], i["ssm_conv_b"][0], i["ssm_norm_w"][0],
                                  np.repeat(i["ssm_d"][0], 64))
        d["ssm_heads"] = c(np.stack([i["ssm_dt_bias"][0], i["ssm_a_log"][0]], axis=1))
        d["ssm_w_in"] = tiles(w[:, 0:SSM_TILES * P], KC)
        d["ssm_w_dt"] = c(np.transpose(np.reshape(w[:, SSM_TILES * P:], (KC, P, 32)), (1, 0, 2)))
        d["ssm_w_out"] = c(np.transpose(np.reshape(i["ssm_w_out"][0], (2, KC, P, KC, P)), (3, 0, 2, 1, 4)
                                        ).reshape(2 * KC, P, D_MODEL))
        d["conv_in"] = c(np.transpose(np.reshape(i["state_conv"][0], (DEC, 3, CONV_TILES, P)), (3, 2, 1, 0)))
        d["ssm_in"] = c(np.transpose(i["state_ssm"][0], (3, 0, 1, 2)).reshape(P, DEC, 2048))
    if "peer_w_q" in i:
        for n in range(2):
            d[f"norm_ffn{n}"] = columns(i["norm_ffn"][n])
            d[f"w_q{n}"] = tiles(i["peer_w_q"][n], KC)
            d[f"sub_keys{n}"] = c(np.transpose(i["peer_sub_keys"][n], (3, 1, 0, 2)).reshape(P, SETS, KEYS))
            d[f"up{n}"] = c(np.transpose(np.reshape(i["peer_u"][n], (KEYS, KEYS, KC, P)), (1, 3, 2, 0)
                                         ).reshape(KEYS, P, D_MODEL))
            d[f"down{n}"] = c(np.transpose(np.reshape(i["peer_v"][n], (KEYS, KEYS, D_MODEL)), (1, 0, 2)))
        d["norm_final"] = columns(i["norm_final"])
    return d


def tokens_back(y):
    import numpy as np
    return np.transpose(y, (2, 1, 0)).reshape(T, -1)


def ab_back(r):
    import numpy as np
    c = np.ascontiguousarray
    shift = np.transpose(r["last_shift"], (2, 1, 0)).reshape(DEC + 1, SHIFT_TILES * P)
    s = np.reshape(r["rwkv_prompt"], (2, 64, 4, 2, 64))
    rwkv = np.stack([s[0, :, :, 0, :], s[1, :, :, 1, :]], axis=0)
    rwkv = np.transpose(rwkv, (2, 0, 3, 1)).reshape(1, 1, 8, 64, 64)
    hgrn = np.transpose(r["hgrn_prompt"], (1, 0, 2)).reshape(1, 1, 4, P, P)
    s_rwkv = np.transpose(np.reshape(r["rwkv_sample"], (2, 64, 4, DEC, 64)), (3, 2, 0, 4, 1)).reshape(1, DEC, 8, 64, 64)
    s_hgrn = np.transpose(r["hgrn_sample"], (2, 1, 0, 3)).reshape(1, DEC, 4, P, P)
    return (c(shift[None, 0:1]), c(rwkv), c(hgrn)), (c(shift[None, 1:]), c(s_rwkv), c(s_hgrn))


AB_OUT = {"last_shift": (P, SHIFT_TILES, DEC + 1), "rwkv_prompt": (P, 4, P), "rwkv_sample": (P, 4, DEC, 64),
          "hgrn_prompt": (P, 4, P), "hgrn_sample": (P, 4, DEC, P)}


def ssm_back(r):
    import numpy as np
    c = np.ascontiguousarray
    conv = np.transpose(r["conv_prompt"], (2, 1, 0)).reshape(1, 1, TAPS - 1, CONV_TILES * P)
    s_conv = np.transpose(r["conv_sample"], (3, 2, 1, 0)).reshape(1, DEC, TAPS - 1, CONV_TILES * P)
    ssm = np.transpose(np.reshape(r["ssm_prompt"], (P, HEADS, 64)), (1, 2, 0))[None, None]
    s_ssm = np.transpose(np.reshape(r["ssm_sample"], (P, DEC, HEADS, 64)), (1, 2, 3, 0))[None]
    return (c(ssm), c(conv)), (c(s_ssm), c(s_conv))


def program(nc, d):
    with ExitStack() as ctx:
        core = Core(nc, ctx)
        constants(core, ctx)
        x = core.sb(ctx, "x", [P, KC, T])
        norms = core.sb(ctx, "norms", [P, 5, KC])

        core.weights_raw = core.sb(ctx, "weights_raw", [P, RING, D_MODEL])
        ab_in, ssm_in, w_q0, w_q1 = (Stream(d[name]) for name in ("ab_w_in", "ssm_w_in", "w_q0", "w_q1"))

        with nc.Block() as block:
            @block.sync
            def _(sp):
                core.load(sp, x, d["x"])
                for n, src in enumerate((d["norm_ffn0"], d["norm_ffn1"], d["norm_final"],
                                         d["ab_params"][:, AB_PARAM["norm"]], d["ssm_params"][:, SSM_PARAM["norm"]])):
                    core.load(sp, norms[:, n, :], src)
                first_loads(core, sp, ab_in)
                core.wait_loads(sp)
        mixer_ab(core, x, d, norms[:, 3, :], ab_in, then=w_q0)
        peer(core, x, norms[:, 0, :], w_q0, d["sub_keys0"], d["up0"], d["down0"], then=ssm_in)
        mixer_ssm(core, x, d, norms[:, 4, :], ssm_in, then=w_q1)
        peer(core, x, norms[:, 1, :], w_q1, d["sub_keys1"], d["up1"], d["down1"])
        with ExitStack() as local:
            y = core.sb(local, "y", [P, KC, T])
            rms_norm(core, x, norms[:, 2, :], y)
            with nc.Block() as block:
                @block.sync
                def _(sp):
                    core.stored.inc(sp.dma_start(d["y"], y), 16)
                    sp.wait_ge(core.stored.sem, core.stored.at)


def kernel(**inputs):
    import numpy as np
    import concourse.bacc as bacc
    from concourse.bass_utils import run_bass_kernel_spmd as run

    nc = bacc.Bacc("TRN2", target_bir_lowering=False, num_devices=1)
    arrays = lay_out(inputs)
    d = {k: nc.dram_tensor("in_" + k, a.shape, F32, kind="ExternalInput").ap() for k, a in arrays.items()}
    for k, shape in {**AB_OUT, **SSM_OUT, "y": (P, KC, T)}.items():
        d[k] = nc.dram_tensor(k, shape, F32, kind="ExternalOutput").ap()
    program(nc, d)
    r = run(nc, [{"in_" + k: a for k, a in arrays.items()}], core_ids=[0]).results[0]
    (p_shift, p_rwkv, p_hgrn), (s_shift, s_rwkv, s_hgrn) = ab_back(r)
    (p_ssm, p_conv), (s_ssm, s_conv) = ssm_back(r)
    y = np.ascontiguousarray(tokens_back(r["y"]))
    return (y[None, 0:SEQ], y[SEQ:T, None], p_shift, p_rwkv, p_hgrn, p_ssm, p_conv,
            s_shift, s_rwkv, s_hgrn, s_ssm, s_conv)
```
